# Optimizing a Trainium2 kernel written in Bass

```python
import jax, jax.numpy as jnp
from jax import lax
import numpy as np
import jax
import jax.numpy as jnp

D_MODEL = 1024
BATCH = 1
SEQ = 256
DEPTH = 1

N_MEM = 256
HEAD_DIM = 64
FOX_HEADS = D_MODEL // HEAD_DIM
FOX_W = FOX_HEADS * HEAD_DIM
SB_HEADS = D_MODEL // HEAD_DIM
SB_W = SB_HEADS * HEAD_DIM
LRU_W = D_MODEL
LRU_BLOCKS = D_MODEL // HEAD_DIM
LRU_BW = LRU_W // LRU_BLOCKS
LRU_CONV = 4
LRU_C = 8.0
MEM_HEADS = 4
MEM_HD = D_MODEL // MEM_HEADS
MEM_W = MEM_HEADS * MEM_HD
N_BRANCH = 4
BRANCH_W = D_MODEL
D_FF = ((8 * D_MODEL // 3 + 255) // 256) * 256
FFN_CONV = 3
Q_BLOCK = 128
EPS = 1e-6
N_IN = 3 * FOX_W + FOX_HEADS + 2 * LRU_W + 3 * SB_W + MEM_W + N_BRANCH * D_MODEL


def _column_slices():
    widths = (("fox_q", FOX_W), ("fox_k", FOX_W), ("fox_v", FOX_W), ("fox_f", FOX_HEADS),
              ("lru_x", LRU_W), ("lru_g", LRU_W),
              ("sb_q", SB_W), ("sb_k", SB_W), ("sb_v", SB_W),
              ("mem_q", MEM_W), ("gates", N_BRANCH * D_MODEL))
    out, start = {}, 0
    for name, w in widths:
        out[name] = (start, start + w)
        start += w
    return out

def _rms(x, g):
    x32 = x.astype(jnp.float32)
    y = x32 * lax.rsqrt(jnp.mean(x32 * x32, axis=-1, keepdims=True) + EPS)
    return (y * g.astype(jnp.float32)).astype(x.dtype)

def _causal_dwconv(x, w, b):
    k, s = w.shape[0], x.shape[1]
    xp = jnp.pad(x, ((0, 0), (k - 1, 0), (0, 0)))
    out = b
    for i in range(k):
        out = out + xp[:, i:i + s] * w[i]
    return out

def _heads(t, n):
    b, s, _ = t.shape
    return t.reshape(b, s, n, -1).transpose(0, 2, 1, 3)

def _merge_heads(t):
    b, h, s, d = t.shape
    return t.transpose(0, 2, 1, 3).reshape(b, s, h * d)

def _fox_attention(q, k, v, log_f):
    b, h, s, d = q.shape
    nb = s // Q_BLOCK
    scale = d ** -0.5
    cum_f = jnp.cumsum(log_f, axis=-1)
    q_blk = q.reshape(b, h, nb, Q_BLOCK, d).transpose(2, 0, 1, 3, 4)
    f_blk = cum_f.reshape(b, h, nb, Q_BLOCK).transpose(2, 0, 1, 3)
    k_pos = jnp.arange(s)

    def block(args):
        qi, fi, bi = args
        q_pos = bi * Q_BLOCK + jnp.arange(Q_BLOCK)
        logits = jnp.einsum('bhqd,bhkd->bhqk', qi, k) * scale + (fi[..., :, None] - cum_f[..., None, :])
        logits = jnp.where(k_pos[None, :] <= q_pos[:, None], logits, -jnp.inf)
        p = jax.nn.softmax(logits, axis=-1)
        return jnp.einsum('bhqk,bhkd->bhqd', p, v)

    out = lax.map(block, (q_blk, f_blk, jnp.arange(nb)))
    return out.transpose(1, 2, 0, 3, 4).reshape(b, h, s, d)

def _stick_breaking_attention(q, k, v):
    b, h, s, d = q.shape
    nb = s // Q_BLOCK
    scale = d ** -0.5
    q_blk = q.reshape(b, h, nb, Q_BLOCK, d).transpose(2, 0, 1, 3, 4)
    k_pos = jnp.arange(s)

    def block(args):
        qi, bi = args
        q_pos = bi * Q_BLOCK + jnp.arange(Q_BLOCK)
        causal = k_pos[None, :] < q_pos[:, None]
        z = jnp.einsum('bhqd,bhkd->bhqk', qi, k) * scale
        log_1m_beta = jnp.where(causal, jax.nn.log_sigmoid(-z), 0.0)
        excl = lax.cumsum(log_1m_beta, axis=3, reverse=True) - log_1m_beta
        weights = jnp.where(causal, jnp.exp(jax.nn.log_sigmoid(z) + excl), 0.0)
        return jnp.einsum('bhqk,bhkd->bhqd', weights, v)

    out = lax.map(block, (q_blk, jnp.arange(nb)))
    return out.transpose(1, 2, 0, 3, 4).reshape(b, h, s, d)

def _mem_attention(q, k, v):
    scale = q.shape[-1] ** -0.5
    p = jax.nn.softmax(jnp.einsum('bhsd,bhmd->bhsm', q, k) * scale, axis=-1)
    return jnp.einsum('bhsm,bhmd->bhsd', p, v)

def _rg_lru_branch(x, gate, conv_w, conv_b, w_a, b_a, w_x, b_x, lam):
    b, s, w = x.shape
    xc = _causal_dwconv(x, conv_w, conv_b).astype(jnp.float32)
    xg = xc.reshape(b, s, LRU_BLOCKS, LRU_BW)
    r = jax.nn.sigmoid(jnp.einsum('bsnd,nde->bsne', xg, w_a).reshape(b, s, w) + b_a)
    i = jax.nn.sigmoid(jnp.einsum('bsnd,nde->bsne', xg, w_x).reshape(b, s, w) + b_x)
    log_a = -LRU_C * r * jax.nn.softplus(-lam)
    a = jnp.exp(log_a)
    u = jnp.sqrt(-jnp.expm1(2.0 * log_a)) * (i * xc)

    def combine(c1, c2):
        a1, h1 = c1
        a2, h2 = c2
        return a1 * a2, a2 * h1 + h2

    _, hs = lax.associative_scan(combine, (a, u), axis=1)
    return hs * jax.nn.gelu(gate.astype(jnp.float32))

def first_inputs(seed: int = 0) -> dict:
    key = jax.random.key(seed)
    ks = jax.random.split(key, 32)
    f32 = jnp.float32

    def nrm(k, shape, scale):
        return jax.random.normal(k, shape, f32) * scale

    def gain(k, shape):
        return 1.0 + 0.02 * jax.random.normal(k, shape, f32)

    res_scale = (2 * DEPTH) ** -0.5
    u = jax.random.uniform(ks[12], (DEPTH, LRU_W), f32, 0.9, 0.999)
    sig = u ** (1.0 / LRU_C)
    lru_lambda = jnp.log(sig) - jnp.log1p(-sig)
    return {
        "x": nrm(ks[0], (BATCH, SEQ, D_MODEL), 1.0),
        "mem": nrm(ks[1], (BATCH, N_MEM, D_MODEL), 1.0),
        "attn_norm_g": gain(ks[2], (DEPTH, D_MODEL)),
        "mem_norm_g": gain(ks[3], (DEPTH, D_MODEL)),
        "w_in": nrm(ks[4], (DEPTH, D_MODEL, N_IN), D_MODEL ** -0.5),
        "b_forget": jax.random.uniform(ks[5], (DEPTH, FOX_HEADS), f32, 2.0, 6.0),
        "fox_q_norm_g": gain(ks[6], (DEPTH, HEAD_DIM)),
        "fox_k_norm_g": gain(ks[7], (DEPTH, HEAD_DIM)),
        "lru_conv_w": nrm(ks[8], (DEPTH, LRU_CONV, LRU_W), LRU_CONV ** -0.5),
        "lru_conv_b": nrm(ks[9], (DEPTH, LRU_W), 0.01),
        "lru_w_a": nrm(ks[10], (DEPTH, LRU_BLOCKS, LRU_BW, LRU_BW), LRU_BW ** -0.5),
        "lru_b_a": nrm(ks[11], (DEPTH, LRU_W), 0.01),
        "lru_w_x": nrm(ks[13], (DEPTH, LRU_BLOCKS, LRU_BW, LRU_BW), LRU_BW ** -0.5),
        "lru_b_x": nrm(ks[14], (DEPTH, LRU_W), 0.01),
        "lru_lambda": lru_lambda,
        "w_mem_kv": nrm(ks[15], (DEPTH, D_MODEL, 2 * MEM_W), D_MODEL ** -0.5),
        "mem_q_norm_g": gain(ks[16], (DEPTH, MEM_HD)),
        "mem_k_norm_g": gain(ks[17], (DEPTH, MEM_HD)),
        "b_gate": nrm(ks[18], (DEPTH, N_BRANCH, D_MODEL), 0.01),
        "w_branch": nrm(ks[19], (DEPTH, N_BRANCH, BRANCH_W, D_MODEL), BRANCH_W ** -0.5),
        "w_out": nrm(ks[20], (DEPTH, D_MODEL, D_MODEL), D_MODEL ** -0.5 * res_scale),
        "ffn_norm_g": gain(ks[21], (DEPTH, D_MODEL)),
        "w_up": nrm(ks[22], (DEPTH, D_MODEL, 2 * D_FF), D_MODEL ** -0.5),
        "ffn_conv_w": nrm(ks[23], (DEPTH, FFN_CONV, D_FF), FFN_CONV ** -0.5),
        "ffn_conv_b": nrm(ks[24], (DEPTH, D_FF), 0.01),
        "w_down": nrm(ks[25], (DEPTH, D_FF, D_MODEL), D_FF ** -0.5 * res_scale),
    }

def first_block(x, mem, attn_norm_g, mem_norm_g, w_in, b_forget, fox_q_norm_g, fox_k_norm_g,
              lru_conv_w, lru_conv_b, lru_w_a, lru_b_a, lru_w_x, lru_b_x, lru_lambda,
              w_mem_kv, mem_q_norm_g, mem_k_norm_g, b_gate, w_branch, w_out,
              ffn_norm_g, w_up, ffn_conv_w, ffn_conv_b, w_down):
    f32 = jnp.float32
    cols = _column_slices()
    b, s, _ = x.shape
    for l in range(DEPTH):
        h = _rms(x, attn_norm_g[l])
        w_l = w_in[l]

        def proj(name):
            lo, hi = cols[name]
            return h @ w_l[:, lo:hi]

        fq = _rms(_heads(proj("fox_q"), FOX_HEADS), fox_q_norm_g[l]).astype(f32)
        fk = _rms(_heads(proj("fox_k"), FOX_HEADS), fox_k_norm_g[l]).astype(f32)
        fv = _heads(proj("fox_v"), FOX_HEADS).astype(f32)
        log_f = jax.nn.log_sigmoid(proj("fox_f").astype(f32) + b_forget[l]).transpose(0, 2, 1)
        y_fox = _merge_heads(_fox_attention(fq, fk, fv, log_f))

        y_lru = _rg_lru_branch(proj("lru_x"), proj("lru_g"), lru_conv_w[l], lru_conv_b[l],
                               lru_w_a[l], lru_b_a[l], lru_w_x[l], lru_b_x[l], lru_lambda[l])

        sq = _heads(proj("sb_q"), SB_HEADS).astype(f32)
        sk = _heads(proj("sb_k"), SB_HEADS).astype(f32)
        sv = _heads(proj("sb_v"), SB_HEADS).astype(f32)
        y_sb = _merge_heads(_stick_breaking_attention(sq, sk, sv))

        mem_n = _rms(mem, mem_norm_g[l])
        w_kv = w_mem_kv[l]
        mk = _rms(_heads(mem_n @ w_kv[:, :MEM_W], MEM_HEADS), mem_k_norm_g[l]).astype(f32)
        mv = _heads(mem_n @ w_kv[:, MEM_W:], MEM_HEADS).astype(f32)
        mq = _rms(_heads(proj("mem_q"), MEM_HEADS), mem_q_norm_g[l]).astype(f32)
        y_mem = _merge_heads(_mem_attention(mq, mk, mv))

        branches = jnp.stack([y_fox, y_lru, y_sb, y_mem], axis=2).astype(x.dtype)
        gates = jax.nn.sigmoid(proj("gates").reshape(b, s, N_BRANCH, D_MODEL) + b_gate[l])
        projected = jnp.einsum('bsnc,ncd->bsnd', branches, w_branch[l])
        mixed = jnp.sum(gates * projected, axis=2)
        x = x + mixed @ w_out[l]

        h2 = _rms(x, ffn_norm_g[l])
        w_u = w_up[l]
        gate_pre = _causal_dwconv(h2 @ w_u[:, :D_FF], ffn_conv_w[l], ffn_conv_b[l])
        val = h2 @ w_u[:, D_FF:]
        x = x + (jax.nn.silu(gate_pre) * val) @ w_down[l]
    return x


DEPTH_2 = 2

GRID_W = 64
CTX_LEN = 256

N_HEADS = 8
N_KV_HEADS = 2
HEAD_DIM_2 = 128
Q_PER_KV = N_HEADS // N_KV_HEADS
ROPE_THETA = 10000.0

GLA_HEADS = 4
GLA_DK = D_MODEL // 2 // GLA_HEADS
GLA_DV = D_MODEL // GLA_HEADS
GLA_RANK = 16
GLA_TAU = 16.0
GLA_CHUNK = 64

CONV_CH = D_MODEL
CONV_WIDTH = 31

D_FF_2 = -(-8 * D_MODEL // (3 * 256)) * 256

ALPHA = (2.0 * DEPTH_2) ** 0.25
BETA = (8.0 * DEPTH_2) ** -0.25
NORM_EPS = 1e-6

ATT_Q = N_HEADS * HEAD_DIM_2
ATT_KV = N_KV_HEADS * HEAD_DIM_2
GLA_K = GLA_HEADS * GLA_DK
GLA_V = GLA_HEADS * GLA_DV
N_BRANCH_2 = 3
MEM_SPLITS = (ATT_KV, ATT_KV, GLA_K, GLA_V, 2 * GLA_RANK)
REST_SPLITS = (ATT_Q, GLA_K, GLA_V, 2 * CONV_CH, N_BRANCH_2 * D_MODEL)
MEM_COLS = sum(MEM_SPLITS)
IN_COLS = MEM_COLS + sum(REST_SPLITS)


def _split(a, sizes):
    return jnp.split(a, np.cumsum(sizes)[:-1].tolist(), axis=-1)

def _layernorm(x, g=None, b=None):
    xf = x.astype(jnp.float32)
    xc = xf - jnp.mean(xf, -1, keepdims=True)
    y = xc * lax.rsqrt(jnp.mean(xc * xc, -1, keepdims=True) + NORM_EPS)
    if g is not None:
        y = y * g.astype(jnp.float32) + b.astype(jnp.float32)
    return y.astype(x.dtype)

def _rmsnorm(x, g):
    xf = x.astype(jnp.float32)
    y = xf * lax.rsqrt(jnp.mean(xf * xf, -1, keepdims=True) + NORM_EPS)
    return (y * g.astype(jnp.float32)).astype(x.dtype)

def _modulate(x, shift, scale):
    return _layernorm(x) * (1.0 + scale) + shift

def _post(x, f, gate, g, b):
    return _layernorm(ALPHA * x + gate * f, g, b)

def _heads_2(a, n):
    B, L, _ = a.shape
    return a.reshape(B, L, n, -1).transpose(0, 2, 1, 3)

def _flip(a):
    return a[:, :, ::-1]

def _axial_rope(rows):
    t = jnp.arange(rows * GRID_W)
    row = (t // GRID_W).astype(jnp.float32)
    col = (t % GRID_W).astype(jnp.float32)
    half = HEAD_DIM_2 // 2
    inv = ROPE_THETA ** (-jnp.arange(0, half, 2, dtype=jnp.float32) / half)
    ang = jnp.concatenate([row[:, None] * inv, col[:, None] * inv], axis=-1)
    return jnp.cos(ang), jnp.sin(ang)

def _apply_rope(x, cos, sin):
    xf = x.astype(jnp.float32)
    x1, x2 = xf[..., 0::2], xf[..., 1::2]
    y = jnp.stack([x1 * cos - x2 * sin, x1 * sin + x2 * cos], axis=-1)
    return y.reshape(x.shape).astype(x.dtype)

def _sdpa(q, k, v):
    s = jnp.einsum('bkgqd,bkld->bkgql', q, k, preferred_element_type=jnp.float32) * (HEAD_DIM_2 ** -0.5)
    p = jax.nn.softmax(s, axis=-1)
    return jnp.einsum('bkgql,bkld->bkgqd', p.astype(v.dtype), v)

def _attend_blocks(q, k_all, v_all):
    B, Hk, G, S, Dh = q.shape
    nb = S // Q_BLOCK
    qb = jnp.moveaxis(q.reshape(B, Hk, G, nb, Q_BLOCK, Dh), 3, 0)
    o = lax.map(lambda blk: _sdpa(blk, k_all, v_all), qb)
    return jnp.moveaxis(o, 0, 3).reshape(B, Hk, G, S, Dh)

def _gla_log_gates(glr, w_a2, b_a):
    B, L, _ = glr.shape
    z = jnp.einsum('blnr,nrk->nblk', glr.reshape(B, L, 2, GLA_RANK), w_a2) + b_a[:, None, None, :]
    lg = jax.nn.log_sigmoid(z.astype(jnp.float32)) / GLA_TAU
    lg = lg.reshape(2, B, L, GLA_HEADS, GLA_DK).transpose(0, 1, 3, 2, 4)
    return lg[0], lg[1]

def _gla_scan(q, k, v, logg, s0):
    B, H, L, dk = q.shape
    dv = v.shape[-1]
    n = L // GLA_CHUNK

    def chunks(a):
        a = a.astype(jnp.float32)
        return a.reshape(B, H, n, GLA_CHUNK, a.shape[-1]).transpose(2, 0, 1, 3, 4)

    lower = jnp.tril(jnp.ones((GLA_CHUNK, GLA_CHUNK), dtype=bool))[:, :, None]

    def step(s, inp):
        qc, kc, vc, gc = inp
        b = jnp.cumsum(gc, axis=2)
        rel = jnp.where(lower, b[:, :, :, None, :] - b[:, :, None, :, :], -jnp.inf)
        a = jnp.einsum('bhid,bhjd,bhijd->bhij', qc, kc, jnp.exp(rel))
        o = jnp.einsum('bhid,bhde->bhie', qc * jnp.exp(b), s) + jnp.einsum('bhij,bhje->bhie', a, vc)
        b_end = b[:, :, -1:, :]
        s = jnp.exp(b_end[:, :, 0, :, None]) * s + jnp.einsum('bhjd,bhje->bhde', kc * jnp.exp(b_end - b), vc)
        return s, o

    s_end, o = lax.scan(step, s0, (chunks(q), chunks(k), chunks(v), chunks(logg)))
    return o.transpose(1, 2, 0, 3, 4).reshape(B, H, L, dv).astype(v.dtype), s_end

def _gla_final_state(k, v, logg):
    b = jnp.cumsum(logg, axis=2)
    w = jnp.exp(b[:, :, -1:, :] - b)
    return jnp.einsum('bhld,bhle->bhde', k.astype(jnp.float32) * w, v.astype(jnp.float32))

def _gla_bidir(qg, kg, vg, gf, gb, s_f, s_b):
    o_f, s_f_end = _gla_scan(qg, kg, vg, gf, s_f)
    o_b, s_b_end = _gla_scan(_flip(qg), _flip(kg), _flip(vg), _flip(gb), s_b)
    return o_f + _flip(o_b), s_f_end, s_b_end

def _mem_parts(pm, p):
    k, v, kg, vg, glr = _split(pm, MEM_SPLITS)
    k = _rmsnorm(_heads_2(k, N_KV_HEADS), p['k_norm'])
    v = _heads_2(v, N_KV_HEADS)
    gf, gb = _gla_log_gates(glr, p['gla_w_a2'], p['gla_b_a'])
    return k, v, _heads_2(kg, GLA_HEADS), _heads_2(vg, GLA_HEADS), gf, gb

def _rest_parts(pr, p):
    q, qg, r, glu, gates = _split(pr, REST_SPLITS)
    B, L, _ = q.shape
    q = _rmsnorm(q.reshape(B, L, N_KV_HEADS, Q_PER_KV, HEAD_DIM_2), p['q_norm']).transpose(0, 2, 3, 1, 4)
    qg = _heads_2(qg, GLA_HEADS) * (GLA_DK ** -0.5)
    return q, qg, r, glu, gates

def _conv_module(glu, p):
    a, g = jnp.split(glu, 2, axis=-1)
    y = a * jax.nn.sigmoid(g)
    pad = CONV_WIDTH // 2
    y = lax.conv_general_dilated(y, p['conv_w_dw'].astype(y.dtype), (1,), [(pad, pad)],
                                 dimension_numbers=('NWC', 'WIO', 'NWC'),
                                 feature_group_count=CONV_CH) + p['conv_b_dw']
    y = jax.nn.silu(_layernorm(y, p['conv_ln_g'], p['conv_ln_b']))
    return y @ p['w_conv_o']

def _merge(o_att, o_gla, r, glu, gates, p):
    B, L, _ = r.shape
    y_att = o_att.transpose(0, 3, 1, 2, 4).reshape(B, L, ATT_Q) @ p['w_att_o']
    o_gla = _rmsnorm(o_gla, p['gla_norm']).transpose(0, 2, 1, 3).reshape(B, L, GLA_V)
    y_gla = (o_gla * jax.nn.silu(r)) @ p['w_gla_o']
    y_conv = _conv_module(glu, p)
    g_att, g_gla, g_conv = jnp.split(jax.nn.sigmoid(gates), N_BRANCH_2, axis=-1)
    return (g_att * y_att + g_gla * y_gla + g_conv * y_conv) @ p['w_out']

def _context_mixer(h, p):
    proj = h @ p['w_in']
    k, v, kg, vg, gf, gb = _mem_parts(proj[..., :MEM_COLS], p)
    q, qg, r, glu, gates = _rest_parts(proj[..., MEM_COLS:], p)
    o_att = _sdpa(q, k, v)
    zero = jnp.zeros(kg.shape[:2] + (GLA_DK, GLA_DV), jnp.float32)
    o_gla, s_f, s_b = _gla_bidir(qg, kg, vg, gf, gb, zero, zero)
    return _merge(o_att, o_gla, r, glu, gates, p), (k, v, s_f, s_b)

def _context_memory(h, p):
    k, v, kg, vg, gf, gb = _mem_parts(h @ p['w_in'][:, :MEM_COLS], p)
    s_f = _gla_final_state(kg, vg, gf)
    s_b = _gla_final_state(_flip(kg), _flip(vg), _flip(gb))
    return k, v, s_f, s_b

def _latent_mixer(h, mem, cos, sin, p):
    proj = h @ p['w_in']
    k, v, kg, vg, gf, gb = _mem_parts(proj[..., :MEM_COLS], p)
    q, qg, r, glu, gates = _rest_parts(proj[..., MEM_COLS:], p)
    k_ctx, v_ctx, s_f, s_b = mem
    k_all = jnp.concatenate([_apply_rope(k, cos, sin), k_ctx], axis=2)
    v_all = jnp.concatenate([v, v_ctx], axis=2)
    o_att = _attend_blocks(_apply_rope(q, cos, sin), k_all, v_all)
    o_gla, _, _ = _gla_bidir(qg, kg, vg, gf, gb, s_f, s_b)
    return _merge(o_att, o_gla, r, glu, gates, p)

def _ffn(h, p):
    return (jax.nn.silu(h @ p['w_ff_gate']) * (h @ p['w_ff_up'])) @ p['w_ff_down']

def second_inputs(seed: int = 0) -> dict:
    key = jax.random.key(seed)
    ks = jax.random.split(key, 27)

    def nrm(i, shape, scale):
        return jax.random.normal(ks[i], shape, jnp.float32) * scale

    D = D_MODEL
    L = DEPTH_2
    return {
        'x': nrm(0, (BATCH, SEQ, D), 1.0),
        'c': nrm(1, (BATCH, D), 1.0),
        'ctx': nrm(2, (BATCH, CTX_LEN, D), 1.0),
        'c_ctx': nrm(3, (D,), 1.0),
        'w_ada': nrm(4, (L, D, 6 * D), 0.3 * D ** -0.5),
        'b_ada': nrm(5, (L, 6 * D), 0.02),
        'w_in': nrm(6, (L, D, IN_COLS), D ** -0.5),
        'q_norm': 1.0 + nrm(7, (L, HEAD_DIM_2), 0.02),
        'k_norm': 1.0 + nrm(8, (L, HEAD_DIM_2), 0.02),
        'w_att_o': nrm(9, (L, ATT_Q, D), ATT_Q ** -0.5),
        'gla_w_a2': nrm(10, (L, 2, GLA_RANK, GLA_K), GLA_RANK ** -0.5),
        'gla_b_a': nrm(11, (L, 2, GLA_K), 0.5),
        'gla_norm': 1.0 + nrm(12, (L, GLA_DV), 0.02),
        'w_gla_o': nrm(13, (L, GLA_V, D), GLA_V ** -0.5),
        'conv_w_dw': nrm(14, (L, CONV_WIDTH, 1, CONV_CH), CONV_WIDTH ** -0.5),
        'conv_b_dw': nrm(15, (L, CONV_CH), 0.02),
        'conv_ln_g': 1.0 + nrm(16, (L, CONV_CH), 0.02),
        'conv_ln_b': nrm(17, (L, CONV_CH), 0.02),
        'w_conv_o': nrm(18, (L, CONV_CH, D), CONV_CH ** -0.5),
        'w_out': nrm(19, (L, D, D), BETA * D ** -0.5),
        'ln1_g': 1.0 + nrm(20, (L, D), 0.02),
        'ln1_b': nrm(21, (L, D), 0.02),
        'w_ff_gate': nrm(22, (L, D, D_FF_2), D ** -0.5),
        'w_ff_up': nrm(23, (L, D, D_FF_2), D ** -0.5),
        'w_ff_down': nrm(24, (L, D_FF_2, D), BETA * D_FF_2 ** -0.5),
        'ln2_g': 1.0 + nrm(25, (L, D), 0.02),
        'ln2_b': nrm(26, (L, D), 0.02),
    }

def second_block(x, c, ctx, c_ctx, w_ada, b_ada, w_in, q_norm, k_norm, w_att_o, gla_w_a2, gla_b_a,
              gla_norm, w_gla_o, conv_w_dw, conv_b_dw, conv_ln_g, conv_ln_b, w_conv_o, w_out,
              ln1_g, ln1_b, w_ff_gate, w_ff_up, w_ff_down, ln2_g, ln2_b):
    rows = x.shape[1] // GRID_W
    cos, sin = _axial_rope(rows)
    silu_c = jax.nn.silu(c)
    silu_cc = jax.nn.silu(c_ctx)
    xc = ctx
    for l in range(DEPTH_2):
        p = {'w_in': w_in[l], 'q_norm': q_norm[l], 'k_norm': k_norm[l], 'w_att_o': w_att_o[l],
             'gla_w_a2': gla_w_a2[l], 'gla_b_a': gla_b_a[l], 'gla_norm': gla_norm[l],
             'w_gla_o': w_gla_o[l], 'conv_w_dw': conv_w_dw[l], 'conv_b_dw': conv_b_dw[l],
             'conv_ln_g': conv_ln_g[l], 'conv_ln_b': conv_ln_b[l], 'w_conv_o': w_conv_o[l],
             'w_out': w_out[l], 'w_ff_gate': w_ff_gate[l], 'w_ff_up': w_ff_up[l],
             'w_ff_down': w_ff_down[l]}
        last = l == DEPTH_2 - 1
        mod = (silu_c @ w_ada[l] + b_ada[l])[:, None, :]
        sh1, sc1, g1, sh2, sc2, g2 = jnp.split(mod, 6, axis=-1)
        n_cm = 2 if last else 6
        mod_c = jnp.split(silu_cc @ w_ada[l][:, :n_cm * D_MODEL] + b_ada[l][:n_cm * D_MODEL], n_cm)
        hc = _modulate(xc, mod_c[0], mod_c[1])
        if last:
            mem = _context_memory(hc, p)
        else:
            yc, mem = _context_mixer(hc, p)
            xc = _post(xc, yc, mod_c[2], ln1_g[l], ln1_b[l])
            xc = _post(xc, _ffn(_modulate(xc, mod_c[3], mod_c[4]), p), mod_c[5], ln2_g[l], ln2_b[l])
        x = _post(x, _latent_mixer(_modulate(x, sh1, sc1), mem, cos, sin, p), g1, ln1_g[l], ln1_b[l])
        x = _post(x, _ffn(_modulate(x, sh2, sc2), p), g2, ln2_g[l], ln2_b[l])
    return x


def setup_inputs(seed=0):
    out = dict(first_inputs(seed))
    for name, value in second_inputs(seed + 1).items():
        if name != "x":
            out[name + "_2"] = value
    return out


def reference(
    x, mem, attn_norm_g, mem_norm_g, w_in, b_forget, fox_q_norm_g, fox_k_norm_g, lru_conv_w,
    lru_conv_b, lru_w_a, lru_b_a, lru_w_x, lru_b_x, lru_lambda, w_mem_kv, mem_q_norm_g,
    mem_k_norm_g, b_gate, w_branch, w_out, ffn_norm_g, w_up, ffn_conv_w, ffn_conv_b, w_down,
    c_2, ctx_2, c_ctx_2, w_ada_2, b_ada_2, w_in_2, q_norm_2, k_norm_2, w_att_o_2, gla_w_a2_2,
    gla_b_a_2, gla_norm_2, w_gla_o_2, conv_w_dw_2, conv_b_dw_2, conv_ln_g_2, conv_ln_b_2,
    w_conv_o_2, w_out_2, ln1_g_2, ln1_b_2, w_ff_gate_2, w_ff_up_2, w_ff_down_2, ln2_g_2,
    ln2_b_2,
):
    x = first_block(
        x, mem, attn_norm_g, mem_norm_g, w_in, b_forget, fox_q_norm_g, fox_k_norm_g, lru_conv_w,
        lru_conv_b, lru_w_a, lru_b_a, lru_w_x, lru_b_x, lru_lambda, w_mem_kv, mem_q_norm_g,
        mem_k_norm_g, b_gate, w_branch, w_out, ffn_norm_g, w_up, ffn_conv_w, ffn_conv_b, w_down,
    )
    return second_block(
        x, c_2, ctx_2, c_ctx_2, w_ada_2, b_ada_2, w_in_2, q_norm_2, k_norm_2, w_att_o_2,
        gla_w_a2_2, gla_b_a_2, gla_norm_2, w_gla_o_2, conv_w_dw_2, conv_b_dw_2, conv_ln_g_2,
        conv_ln_b_2, w_conv_o_2, w_out_2, ln1_g_2, ln1_b_2, w_ff_gate_2, w_ff_up_2, w_ff_down_2,
        ln2_g_2, ln2_b_2,
    )


_drawn_inputs = setup_inputs


def setup_inputs(seed=0):
    import zlib

    import numpy as np

    out = dict(_drawn_inputs(seed))
    spreads = {}
    factors = {'attn_norm_g': 6.676,
     'mem_norm_g': 8.0,
     'fox_q_norm_g': 8.0,
     'fox_k_norm_g': 8.0,
     'lru_conv_b': 5.65,
     'lru_b_a': 8.0,
     'lru_b_x': 8.0,
     'mem_q_norm_g': 8.0,
     'mem_k_norm_g': 8.0,
     'b_gate': 8.0,
     'ffn_norm_g': 4.93,
     'ffn_conv_b': 8.0,
     'ctx_2': 8.0,
     'c_ctx_2': 8.0,
     'b_ada_2': 6.706,
     'q_norm_2': 8.0,
     'k_norm_2': 8.0,
     'w_att_o_2': 7.4,
     'gla_w_a2_2': 8.0,
     'gla_b_a_2': 8.0,
     'gla_norm_2': 8.0,
     'conv_b_dw_2': 8.0,
     'conv_ln_g_2': 8.0,
     'conv_ln_b_2': 8.0}
    for name, (base, spread) in spreads.items():
        noise = np.random.default_rng([zlib.crc32(name.encode()), seed]).standard_normal(out[name].shape)
        drawn = base * np.exp(spread * noise) if base else spread * noise
        out[name] = jnp.asarray(drawn.astype(out[name].dtype))
    for name, factor in factors.items():
        out[name] = (out[name] * factor).astype(out[name].dtype)
    return out
```

```python
from contextlib import ExitStack

import numpy as np
import concourse.bass as bass
from concourse import mybir

F32 = mybir.dt.float32
U32 = mybir.dt.uint32
ALU = mybir.AluOpType
ACT = mybir.ActivationFunctionType
AX = mybir.AxisListType.X

P = 128
D = 1024
KC = D // P
S = 256
T2 = 2 * S
CTX = slice(0, S)
XS = slice(S, T2)
D_FF = 2816
FT = D_FF // P
LAYERS = 2
EPS = 1e-6
ALPHA = (2.0 * LAYERS) ** 0.25
NEG = -1e30
SLOTS = 8
LEVELS = [64, 32, 16, 8, 4, 2, 1]
GLA_TAU = 16.0
CONV = 31
PAD = CONV // 2
ACT_SET_SIGMOID = 2
ACT_SET_LN_EXP = 6
WORKERS = 4


def first_column(layer):
    return 0 if layer < LAYERS - 1 else S


def norm_column(kind, layer):
    return 0 if kind == "ln_mixer" else first_column(layer)


def phases():
    full = KC * P
    out = [("prepare", 0, 1, []), ("forget", 0, 1, []), ("fox", 0, 8, [full] * 3),
           ("lru_in", 0, 8, [full, full, 2 * P]), ("lru_mix", 0, 1, []),
           ("stick", 0, 8, [full] * 3), ("memory", 0, 4, [full] * 6),
           ("merge1", 0, 8, [full] * 8), ("out1", 0, 2, [full] * 4),
           ("norm_ffn1", 0, 1, []), ("up1", 0, 11, [full] * 4),
           ("down1", 0, 4, [full, full, 6 * P] * 2), ("cond", 0, 1, [])]
    for l in range(LAYERS):
        out += [("ada", l, 6, [full] * 8), ("modulation", l, 1, []), ("ln_mixer", l, 1, []),
                ("attend", l, 2, [full] * 6), ("gla", l, 4, [full] * 4 + [2 * P] + [full] * 2),
                ("conv", l, 4, [full] * 4), ("conv_norm", l, 1, []),
                ("merge2", l, 8, [full] * 6), ("out2", l, 2, [full] * 4), ("post_mixer", l, 1, []),
                ("ln_ffn", l, 1, []), ("up2", l, 11, [full] * 4),
                ("down2", l, 4, [full, full, 6 * P] * 2), ("post_ffn", l, 1, [])]
    return out


def column_layout(names_widths):
    at, out = 0, {}
    for name, width in names_widths:
        out[name] = at
        at += width
    return out, at


PARAMS = [("attn_g", KC), ("mem_g", KC), ("wf", KC * 48), ("bf", 1), ("fox_qg", 1), ("fox_kg", 2),
          ("lru_w", 4 * KC), ("lru_b", KC), ("lru_ba", KC), ("lru_bx", KC), ("lru_lam", KC),
          ("mem_qg", 2), ("mem_kg", 2), ("b_gate", 4 * KC), ("ffn_g", KC), ("ffn_w", 3 * FT), ("ffn_b", FT),
          ("cond", 2 * KC)]
for _l in range(LAYERS):
    PARAMS += [(f"b_ada{_l}", 48), (f"qg{_l}", 1), (f"kg{_l}", 1), (f"wglr{_l}", KC * 32), (f"gla_ba{_l}", 8),
               (f"gla_g{_l}", 2), (f"conv_w{_l}", CONV * KC), (f"conv_b{_l}", KC), (f"conv_g{_l}", KC),
               (f"conv_be{_l}", KC), (f"ln1_g{_l}", KC), (f"ln1_b{_l}", KC), (f"ln2_g{_l}", KC), (f"ln2_b{_l}", KC)]
PCOL, N_PARAMS = column_layout(PARAMS)

CONSTS = [("ident", P), ("mean1024", P), ("mean64", P), ("mean128", P), ("mean256", P), ("ones", P),
          ("suffix", P), ("swap", P), ("causal_neg", P), ("strict", 3 * P), ("strict_big", 3 * P),
          ("levels", len(LEVELS) * P), ("twice_ident", P), ("cos", S), ("sin", S), ("run_f", T2), ("run_b", T2),
          ("head_l", 16), ("head_r", 16), ("add_l", 1), ("add_r", 1), ("head_rows", 2)]
CCOL, N_CONSTS = column_layout(CONSTS)


class Tally:

    def __init__(self, nc, ctx, counted):
        self.nc, self.ctx, self.counted = nc, ctx, counted
        self.primed = set(counted.get("primed", {}))
        self.sems, self.seen = {}, {}

    def sem(self, name):
        if name not in self.sems:
            self.sems[name] = self.ctx.enter_context(self.nc.semaphore(name))
        return self.sems[name]


class Step:

    def __init__(self, tally, plan, number, turn):
        self.tally, self.plan, self.number, self.turn = tally, plan, number, turn
        self.made = {}
        self.layer = plan[number][1]

    def start(self, name):
        counts = self.tally.counted.get(name, {})
        base = int(name in self.tally.primed) + sum(self.plan[p][2] * n for p, n in counts.items() if p < self.number)
        return self.turn * counts.get(self.number, 0) + base

    def unit(self, name):
        return 16 if name.startswith("loaded") else 1

    def done(self, name, k=0):
        return self.tally.sem(name), (self.start(name) + (k + 1)) * self.unit(name)

    def before(self, name, k=0):
        if self.number == min(self.tally.counted.get(name, {self.number: 0})):
            self.tally.seen.setdefault("primed", {})[name] = 1
        return self.tally.sem(name), (self.start(name) + k) * self.unit(name)

    def so_far(self, name):
        return self.tally.sem(name), self.start(name) + self.made.get(name, 0)

    def tick(self, name):
        self.made[name] = self.made.get(name, 0) + 1
        row = self.tally.seen.setdefault(name, {})
        row[self.number] = row.get(self.number, 0) + 1
        return self.tally.sem(name), self.unit(name)


def program(nc, params, consts, stream, x_in, mem_in, ctx_in, out, counted, dump=None, nc_dump=None):
    plan = phases()
    with ExitStack() as ctx:
        tally = Tally(nc, ctx, counted)

        def sb(name, *shape):
            return ctx.enter_context(nc.sbuf_tensor(name, [P, *shape], F32))

        X = sb("X", KC, T2)
        H = sb("H", KC, T2)
        YG = sb("YG", 3 * KC * T2)
        MX = sb("MX", KC, T2)
        SQ = sb("SQ", KC, T2)
        WORK = sb("WORK", 6144)
        PR = sb("PR", N_PARAMS)
        CN = sb("CN", N_CONSTS)
        W = [sb(f"W{u}", KC, P) for u in range(SLOTS)]
        small = sb("small", 64)
        MOD = sb("MOD", 48, 2)
        COND = sb("COND", KC, 2)
        lru_c = sb("lru_c", KC)
        bank = [ctx.enter_context(nc.psum_tensor(f"bank{b}", [P, 512], F32)) for b in range(8)]

        Y1 = [YG[:, n * KC * S:(n + 1) * KC * S].rearrange("p (c t) -> p c t", c=KC) for n in range(4)]
        Y2 = [YG[:, n * KC * T2:(n + 1) * KC * T2].rearrange("p (c t) -> p c t", c=KC) for n in range(3)]
        G = YG[:, 0:FT * T2].rearrange("p (c t) -> p c t", c=FT)
        SQF = SQ[:, :, :].rearrange("p c t -> p (c t)")
        MXF = MX[:, :, :].rearrange("p c t -> p (c t)")

        def const(name, width=P, rows=P, at=0):
            return CN[0:rows, CCOL[name] + at:CCOL[name] + at + width]

        def par(name, c=0, rows=P):
            return PR[0:rows, bass.ds(PCOL[name] + c, 1)]

        def work(at, *shape):
            n = int(np.prod(shape))
            v = WORK[:, at:at + n]
            if len(shape) == 2:
                v = v.rearrange("p (a b) -> p a b", a=shape[0])
            return v

        def wide(ap, n):
            return ap.broadcast_to([ap.shape[0], ap.shape[1], n])

        ident = const("ident")

        probs = work(0, 2, 512)
        probs_t = work(1024, 2, 512)
        qn = work(2048, 512)
        kn = work(2560, 512)
        sq2 = work(3072, 2, 512)
        rstd = work(4096, 2, 512)
        vt = work(5120, 4, P)
        kn2 = work(2560, 2, S)
        forget_f = sb("forget_f", S)
        forget_l = sb("forget_l", 2, S)
        forget_r = sb("forget_r", 2, S)
        rowmax = sb("rowmax", 2, 2)
        rowsum = sb("rowsum", 2, 2)
        rowinv = sb("rowinv", 2, 2)

        block = ctx.enter_context(nc.Block())

        def run(engine, bodies, prologue=None):
            for number, (kind, layer, turns, _) in enumerate(plan):
                if dump is not None and number > dump:
                    break
                if number:
                    engine.wait_ge(tally.sem("phase_done"), WORKERS * number)
                if prologue is not None:
                    prologue(kind)
                body = bodies.get(kind)
                if body is not None:
                    if turns == 1:
                        body(Step(tally, plan, number, 0))
                    else:
                        with engine.Fori(0, turns) as turn:
                            body(Step(tally, plan, number, turn))
                engine.drain().then_inc(tally.sem("phase_done"), 1)


        def soft_max(dve, s, k, logits, segments):
            dve.wait_ge(*s.done("logits", k))
            for j, (o, w) in enumerate(segments):
                mm = dve.tensor_reduce(rowmax[:, k % 2, j:j + 1], logits[:, o:o + w], AX, ALU.max, negate=True)
            mm.then_inc(*s.tick("rowmax"))

        def soft_exp(act, s, k, logits, segments):
            act.wait_ge(*s.done("rowmax", k))
            act.wait_ge(*s.before(f"transposed{k % 2}", k // 2))
            for j, (o, w) in enumerate(segments):
                e = act.activation(probs[:, k % 2, o:o + w], logits[:, o:o + w], ACT.Exp,
                                   bias=rowmax[:, k % 2, j:j + 1], accum_out=rowsum[:, k % 2, j:j + 1])
            e.then_inc(*s.tick("probs"))

        def soft_norm(dve, s, k, segments):
            n = len(segments)
            dve.wait_ge(*s.done("probs", k))
            dve.reciprocal(rowinv[:, k % 2, 0:n], rowsum[:, k % 2, 0:n]).then_inc(*s.tick("dve"))
            dve.wait_ge(*s.so_far("dve"))
            for j, (o, w) in enumerate(segments):
                m = dve.tensor_scalar(probs[:, k % 2, o:o + w], probs[:, k % 2, o:o + w],
                                      rowinv[:, k % 2, j:j + 1], None, ALU.mult)
            m.then_inc(*s.tick("normed"))

        def soft_transpose(pe, s, k, out_bank, moves):
            pe.wait_ge(*s.done("normed", k))
            pe.wait_ge(*s.before("probs_t", k))
            for o, to in moves:
                m = pe.transpose(out_bank[:, to:to + P], probs[:, k % 2, o:o + P], ident)
            m.then_inc(*s.tick(f"transposed{k % 2}"))

        def soft_take(act, s, k, out_bank, width):
            act.wait_ge(*s.done(f"transposed{k % 2}", k // 2))
            act.wait_ge(*s.before(f"pv{k % 2}", k // 2))
            act.activation(probs_t[:, k % 2, 0:width], out_bank[:, 0:width], ACT.Copy)\
               .then_inc(*s.tick("probs_t"))

        FOX_SEGS = [(0, P), (P, 2 * P)]
        FOX_MOVES = [(0, 0), (P, P), (2 * P, 2 * P)]
        MEM_SEGS = [(0, S), (S, S)]
        MEM_MOVES = [(0, 0), (S, P), (P, 2 * P), (S + P, 3 * P)]
        LAT_SEGS = [(0, T2)]
        LAT_MOVES = [(j * P, j * P) for j in range(4)]

        def attend_units(layer):
            out = []
            for g in range(4):
                if first_column(layer) == 0:
                    out.append((g, "ctx", 0))
                out += [(g, "x", 0), (g, "x", 1)]
            return out

        gq, gk = work(0, T2), work(512, T2)
        gv = work(1024, 4, S)
        cum = work(2048, 2, T2)
        dist = work(3072, 2, T2)
        eq, ek = work(4096, T2), work(4608, T2)
        gr = work(5120, 2, T2)
        mq, mk = SQF[:, 0:T2], SQF[:, 512:1024]
        scores = SQF[:, 1024:1536].rearrange("p (c t) -> p c t", c=4)
        qdecay = SQF[:, 1536:2560].rearrange("p (d t) -> p d t", d=2)
        kw = SQF[:, 2560:3584].rearrange("p (d t) -> p d t", d=2)
        glr = SQF[:, 3584:4096]
        kwt = MXF[:, 0:1024].rearrange("p (d c t) -> p d c t", d=2, c=4)
        states = MXF[:, 1024:3072].rearrange("p (d c e) -> p d c e", d=2, c=4)
        decay = MXF[:, 3072:3080].rearrange("p (d c) -> p d c", d=2)
        gtmp = MXF[:, 3584:4096]
        gtmp2 = MXF[:, 0:512]
        glr2 = sb("glr2", T2)
        orderf, orderb = [0, 1, 2, 3], [1, 0, 3, 2]

        def halves(ap, m):
            return ap.rearrange("p (n h m) -> p n h m", h=2, m=m)

        padded = [work(j * 1024, 2, S + 2 * PAD) for j in range(2)]
        conv_sg = work(2048, 2, T2)

        mem_v = SQF[:, 0:512].rearrange("p (t e) -> p t e", t=2)
        att_n = SQF[:, 0:512]
        att_t = SQF[:, 512:768]
        att_k = SQF[:, 1024:1536]
        att_q = SQF[:, 1536:3584].rearrange("p (g t) -> p g t", g=4)
        sg = WORK[:, 0:4 * T2].rearrange("p (n t) -> p n t", n=4)
        lru_x = SQF[:, 0:KC * S]
        lru_r = SQF[:, KC * S:2 * KC * S]
        lru_i = MXF[:, 0:KC * S]
        lru_g = MXF[:, KC * S:2 * KC * S]

        up_s = work(0, 2, T2)
        up_c = work(1024, 2, T2)
        small_f = work(0, 2, S)

        @block.sync
        def _(sp):
            if dump is not None:
                sp.wait_ge(tally.sem("zeroed"), 4)
            sp.dma_start(X[:, :, XS], x_in).then_inc(tally.sem("inputs"), 16)
            sp.dma_start(X[:, :, CTX], ctx_in).then_inc(tally.sem("inputs"), 16)
            sp.dma_start(MX[:, :, CTX], mem_in).then_inc(tally.sem("inputs"), 16)
            sp.dma_start(PR[:, :], params).then_inc(tally.sem("inputs"), 16)
            sp.dma_start(CN[:, :], consts).then_inc(tally.sem("inputs"), 16)
            first, last_use = 0, [0] * SLOTS
            for number, (kind, layer, turns, widths) in enumerate(plan):
                if dump is not None and number > dump:
                    break
                n = len(widths)
                if not n:
                    continue
                s = Step(tally, plan, number, 0)
                for u, w in enumerate(widths):
                    if last_use[u]:
                        sp.wait_ge(tally.sem("unit"), last_use[u])
                    sp.dma_start(W[u][:, 0:w // P, :], stream[first + u, :, 0:w]
                                 .rearrange("p (c m) -> p c m", m=P)).then_inc(*s.tick(f"loaded{u}"))
                with sp.Fori(1, turns) as turn:
                    for u, w in enumerate(widths):
                        sp.wait_ge(tally.sem("unit"), turn * n + (first - n + u + 1))
                        sp.dma_start(W[u][:, 0:w // P, :], stream[turn * n + (first + u), :, 0:w]
                                     .rearrange("p (c m) -> p c m", m=P)).then_inc(tally.sem(f"loaded{u}"), 16)
                for u in range(n):
                    last_use[u] = first + (turns - 1) * n + u + 1
                first += turns * n
            done = len(plan) if dump is None else dump + 1
            sp.wait_ge(tally.sem("phase_done"), WORKERS * done)
            sp.dma_start(out, X[:, :, XS]).then_inc(tally.sem("stored"), 16)
            if dump is None:
                sp.wait_ge(tally.sem("stored"), 16)
            else:
                sp.dma_start(nc_dump["H"], H[:, :, :]).then_inc(tally.sem("stored"), 16)
                sp.dma_start(nc_dump["YG"], YG[:, :]).then_inc(tally.sem("stored"), 16)
                sp.dma_start(nc_dump["MX"], MX[:, :, :]).then_inc(tally.sem("stored"), 16)
                sp.dma_start(nc_dump["X"], X[:, :, :]).then_inc(tally.sem("stored"), 16)
                sp.wait_ge(tally.sem("stored"), 80)

        @block.tensor
        def _(pe):
            def project(s, u, out_ap, cols, src=H, k=KC, first=True, last=True, tick=True):
                pe.wait_ge(*s.done(f"loaded{u}"))
                for c in range(k):
                    m = pe.matmul(out_ap, W[u][:, c, :], src[:, c, cols], start=first and c == 0,
                                  stop=last and c == k - 1)
                if tick:
                    m.then_inc(*s.tick("unit"))
                return m

            def project_tokens(s, u, outs, col0, tick=True):
                pe.wait_ge(*s.done(f"loaded{u}"))
                for t, o in enumerate(outs):
                    for c in range(KC):
                        m = pe.matmul(o, H[:, c, col0 + t * P:col0 + (t + 1) * P], W[u][:, c, :],
                                      start=c == 0, stop=c == KC - 1)
                if tick:
                    m.then_inc(*s.tick("unit"))
                return m

            def mean_square(s, out_ap, cols, name):
                for c in range(KC):
                    pe.wait_ge(*s.done("squared", c))
                    m = pe.matmul(out_ap, const("mean1024"), SQ[:, c, cols], start=c == 0, stop=c == KC - 1)
                m.then_inc(*s.tick(name))

            def prepare(s):
                pe.wait_ge(tally.sem("inputs"), 80)
                mean_square(s, bank[0][:, :], slice(0, T2), "variance")

            def forget(s):
                wf = PR[:, PCOL["wf"]:PCOL["wf"] + KC * 48].rearrange("p (c m) -> p c m", c=KC)
                for c in range(KC):
                    m = pe.matmul(bank[0][0:48, 0:S], wf[:, c, :], H[:, c, XS], start=c == 0, stop=c == KC - 1)
                m.then_inc(*s.tick("forget_logits"))

            def pv_pair(s, k, values, weights):
                pe.wait_ge(*s.before(f"taken_out{k}"))
                o = bank[7][64 * k:64 * k + 64, 0:S]
                pe.matmul(o, values[:, 0, 64 * k:64 * k + 64], weights[:, 0:S], start=True, stop=False)
                pe.matmul(o[:, P:S], values[:, 1, 64 * k:64 * k + 64], weights[:, S:3 * P],
                          start=False, stop=True).then_inc(*s.tick(f"pv{k % 2}"))

            def fox(s):
                pe.wait_ge(*s.before("q_taken"))
                project(s, 0, bank[0][:, 0:S], XS)
                pe.wait_ge(*s.before("k_taken"))
                project(s, 1, bank[1][:, 0:S], XS)
                pe.wait_ge(*s.before("v_taken"))
                project_tokens(s, 2, [bank[2][:, t * P:(t + 1) * P] for t in range(2)], S)
                pe.wait_ge(*s.before("rstd"))
                for j in range(2):
                    pe.wait_ge(*s.done("qk_squared", j))
                    m = pe.matmul(bank[3][:, j * S:(j + 1) * S], const("mean64"), sq2[:, j, 0:S],
                                  start=True, stop=True)
                m.then_inc(*s.tick("variance"))

                def logits(k):
                    b = bank[4 + k]
                    pe.wait_ge(*s.before("probs"))
                    pe.wait_ge(*s.done("k_taken"))
                    for (o, w), q in zip(FOX_SEGS, range(2)):
                        qs = slice(q * P, (q + 1) * P)
                        pe.matmul(b[:, o:o + w], qn[:, qs], kn2[:, k, 0:w], start=True, stop=False)
                        pe.matmul(b[:, o:o + w], forget_l[0:48, k, qs], forget_r[0:48, k, 0:w],
                                  start=False, stop=False)
                        m = pe.matmul(b[:, o + w - P:o + w], ident, const("causal_neg"), start=False, stop=True)
                    m.then_inc(*s.tick("logits"))

                logits(0)
                for k in range(2):
                    if k == 0:
                        logits(1)
                    soft_transpose(pe, s, k, bank[6], FOX_MOVES)
                    pe.wait_ge(*s.done("probs_t", k))
                    if k == 0:
                        pe.wait_ge(*s.done("v_taken"))
                    pv_pair(s, k, vt, probs_t[:, k, :])

            def lru_in(s):
                pe.wait_ge(*s.before("conv_done"))
                project(s, 0, bank[0][:, 0:S], XS)
                pe.wait_ge(*s.before("gate_taken"))
                project(s, 1, bank[1][:, 0:S], XS)
                pe.wait_ge(*s.done("loaded2"))
                pe.wait_ge(*s.done("conv_done"))
                pe.wait_ge(*s.before("ri_taken"))
                xc = SQF[:, bass.ds(s.turn * S, S)]
                pe.matmul(bank[2][:, 0:S], W[2][:, 0, :], xc, start=True, stop=True)
                pe.matmul(bank[3][:, 0:S], W[2][:, 1, :], xc, start=True, stop=True).then_inc(*s.tick("unit"))

            def stick(s):
                pe.wait_ge(*s.before("q_taken"))
                project(s, 0, bank[0][:, 0:S], XS)
                pe.wait_ge(*s.before("k_taken"))
                project(s, 1, bank[1][:, 0:S], XS)
                pe.wait_ge(*s.before("v_taken"))
                project_tokens(s, 2, [bank[2][:, t * P:(t + 1) * P] for t in range(2)], S)
                for k in range(2):
                    if k == 0:
                        pe.wait_ge(*s.done("q_taken"))
                        pe.wait_ge(*s.done("k_taken"))
                    pe.wait_ge(*s.before("log_beta", k))
                    pe.matmul(bank[4 + k][:, 0:S], kn2[:, k, 0:P], qn[:, 0:S], start=True, stop=True)
                    pe.matmul(bank[4 + k][:, S:3 * P], kn2[:, k, P:S], qn[:, P:S], start=True, stop=True)\
                      .then_inc(*s.tick("logits"))
                for k in range(2):
                    b = bank[3 if k == 0 else 6]
                    sp_k = sq2[:, k, :]
                    pe.wait_ge(*s.before(f"minus_suffix{k}"))
                    pe.wait_ge(*s.done("softplus", k))
                    pe.matmul(b[:, 0:3 * P], const("suffix"), sp_k[:, 0:3 * P], start=True, stop=False)
                    pe.matmul(b[:, P:S], const("ones"), sp_k[:, S:3 * P], start=False, stop=False)
                    pe.matmul(b[:, 0:3 * P], ident, const("strict_big", 3 * P), start=False, stop=True)\
                      .then_inc(*s.tick("suffix"))
                for k in range(2):
                    pe.wait_ge(*s.done("weights", k))
                    if k == 0:
                        pe.wait_ge(*s.done("v_taken"))
                    pv_pair(s, k, vt, probs[:, k, :])

            def memory(s):
                pe.wait_ge(*s.before("k_taken"))
                for u in range(2):
                    project(s, u, bank[0][:, u * S:(u + 1) * S], CTX)
                pe.wait_ge(*s.before("q_taken"))
                for u in range(2):
                    project(s, 2 + u, bank[1][:, u * S:(u + 1) * S], XS)
                pe.wait_ge(*s.before("v_taken"))
                for u in range(2):
                    project_tokens(s, 4 + u, [bank[2][:, t * S + u * P:t * S + (u + 1) * P] for t in range(2)], 0)
                pe.wait_ge(*s.before("rstd"))
                for j in range(2):
                    pe.wait_ge(*s.done("qk_squared", j))
                    for u in range(2):
                        m = pe.matmul(bank[3][:, j * S:(j + 1) * S], const("mean256"), sq2[:, j, u * S:(u + 1) * S],
                                      start=u == 0, stop=u == 1)
                m.then_inc(*s.tick("variance"))
                pe.wait_ge(*s.done("q_taken"))
                pe.wait_ge(*s.before("probs"))
                for q in range(2):
                    for u in range(2):
                        m = pe.matmul(bank[4][:, q * S:(q + 1) * S], qn[:, u * S + q * P:u * S + (q + 1) * P],
                                      kn[:, u * S:(u + 1) * S], start=u == 0, stop=u == 1)
                m.then_inc(*s.tick("logits"))
                soft_transpose(pe, s, 0, bank[6], MEM_MOVES)
                pe.wait_ge(*s.done("probs_t"))
                pe.wait_ge(*s.done("v_taken"))
                pe.wait_ge(*s.before("taken_out0"))
                for e in range(2):
                    for j in range(2):
                        m = pe.matmul(bank[7][:, e * S:(e + 1) * S], mem_v[:, j, e * P:(e + 1) * P],
                                      probs_t[:, 0, j * S:(j + 1) * S], start=j == 0, stop=j == 1)
                m.then_inc(*s.tick("pv0"))

            def merge(s, branches, cols, count):
                for n in range(count):
                    pe.wait_ge(*s.before(f"gate{n}"))
                    project(s, 2 * n, bank[2 * n][:, 0:T2 - cols.start], cols)
                    pe.wait_ge(*s.before(f"mixed{n}"))
                    project(s, 2 * n + 1, bank[2 * n + 1][:, 0:T2 - cols.start], branches[n][1], src=branches[n][0])

            def merge1(s):
                merge(s, [(y, slice(0, S)) for y in Y1], XS, 4)

            def merge2(s):
                cols = slice(first_column(s.layer), T2)
                merge(s, [(y, cols) for y in Y2], cols, 3)

            def out_tiles(s):
                cols = slice(S if s.plan[s.number][0] == "out1" else first_column(s.layer), T2)
                for u in range(4):
                    pe.wait_ge(*s.before(f"added{u}"))
                    project(s, u, bank[u][:, 0:T2 - cols.start], cols, src=MX)

            def up(s):
                cols = slice(S if s.plan[s.number][0] == "up1" else first_column(s.layer), T2)
                for j in range(2):
                    pe.wait_ge(*s.before(f"hidden{j}"))
                    for u in range(2):
                        project(s, 2 * j + u, bank[2 * j + u][:, 0:T2 - cols.start], cols)

            def down(s):
                c0 = S if s.plan[s.number][0] == "down1" else first_column(s.layer)
                cols = slice(0, S) if s.plan[s.number][0] == "down1" else slice(c0, T2)
                for j in range(2):
                    pe.wait_ge(*s.before(f"added{j}"))
                    for q in range(3):
                        u = 3 * j + q
                        project(s, u, bank[j][:, 0:T2 - c0], cols, src=G[:, 8 * q:min(8 * q + 8, FT), :],
                                k=min(8, FT - 8 * q), first=q == 0, last=q == 2)

            def norm_ffn1(s):
                mean_square(s, bank[0][:, 0:S], XS, "variance")

            def ada(s):
                for j in range(2):
                    pe.wait_ge(*s.before(f"row{j}"))
                    for q in range(4):
                        u = 4 * j + q
                        pe.wait_ge(*s.done(f"loaded{u}"))
                        w = W[u][:, :, :].rearrange("p c m -> p (c m)").rearrange("p (c m) -> p c m", c=2)
                        for c in range(2):
                            m = pe.matmul(bank[j][0:2, :], COND[:, 2 * q + c, :], w[:, c, :],
                                          start=q == 0 and c == 0, stop=q == 3 and c == 1)
                        m.then_inc(*s.tick("unit"))

            def modulation(s):
                for j in range(48):
                    m = pe.transpose(bank[0][:, 2 * j:2 * j + 2], WORK[0:2, j * P:(j + 1) * P], ident[0:2, 0:2])
                m.then_inc(*s.tick("mod_columns"))

            def layernorm(s):
                c0 = norm_column(s.plan[s.number][0], s.layer)
                src = MX if s.plan[s.number][0] == "conv_norm" else X
                for c in range(KC):
                    m = pe.matmul(bank[0][:, 0:T2 - c0], const("mean1024"), src[:, c, c0:T2],
                                  start=c == 0, stop=c == KC - 1)
                m.then_inc(*s.tick("mean"))
                mean_square(s, bank[1][:, 0:T2 - c0], slice(c0, T2), "variance")

            def attend(s):
                c0 = first_column(s.layer)
                n = T2 - c0

                def normed(j, u, b, cols, width):
                    pe.wait_ge(*s.before("head_taken", j))
                    project(s, u, bank[0][:, 0:width], cols)
                    pe.wait_ge(*s.done("head_squared", j))
                    pe.wait_ge(*s.before("head_rstd", j))
                    pe.matmul(bank[2][:, 0:width], const("mean128"), sq2[:, 0, 0:width], start=True, stop=True)\
                      .then_inc(*s.tick("variance"))

                def rotated(j, width):
                    pe.wait_ge(*s.done("head_taken", j))
                    pe.wait_ge(*s.before("rotated", j))
                    pe.matmul(bank[3][:, 0:S], const("swap"), att_n[:, width - S:width], start=True, stop=True)\
                      .then_inc(*s.tick("swapped"))

                normed(0, 0, 0, slice(0, T2), T2)
                pe.wait_ge(*s.before("v_taken"))
                project_tokens(s, 1, [bank[1][:, t * P:(t + 1) * P] for t in range(4)], 0)
                rotated(0, T2)
                for g in range(4):
                    normed(1 + g, 2 + g, 0, slice(c0, T2), n)
                    rotated(1 + g, n)
                units = attend_units(s.layer)

                def logits(k):
                    g, part, q = units[k]
                    b = bank[4 + k % 2]
                    if k < 2:
                        pe.wait_ge(*s.before("probs"))
                        pe.wait_ge(*s.done("rotated", 4))
                    else:
                        pe.wait_ge(*s.done("probs", k - 2))
                    if part == "x":
                        m = pe.matmul(b[:, :], att_q[:, g, S + q * P:S + (q + 1) * P], att_k, start=True, stop=True)
                    else:
                        for j in range(2):
                            m = pe.matmul(b[:, j * S:(j + 1) * S], att_q[:, g, j * P:(j + 1) * P], att_k[:, CTX],
                                          start=True, stop=True)
                    m.then_inc(*s.tick("logits"))

                logits(0)
                for k, (g, part, q) in enumerate(units):
                    if k + 1 < len(units):
                        logits(k + 1)
                    soft_transpose(pe, s, k, bank[6], LAT_MOVES if part == "x" else MEM_MOVES)
                    pe.wait_ge(*s.done("probs_t", k))
                    if k == 0:
                        pe.wait_ge(*s.done("v_taken"))
                    pe.wait_ge(*s.before("taken_out", k))
                    if part == "x":
                        for j in range(4):
                            m = pe.matmul(bank[7][:, 0:P], vt[:, j, :], probs_t[:, k % 2, j * P:(j + 1) * P],
                                          start=j == 0, stop=j == 3)
                    else:
                        for j in range(2):
                            m = pe.matmul(bank[7][:, 0:S], vt[:, j, :], probs_t[:, k % 2, j * S:(j + 1) * S],
                                          start=j == 0, stop=j == 1)
                    m.then_inc(*s.tick(f"pv{k % 2}"))

            def gla(s):
                c0 = first_column(s.layer)
                n = T2 - c0
                active = range(c0 // P, 4)
                pe.wait_ge(*s.before("gla_end"))
                wg = PR[:, PCOL[f"wglr{s.layer}"]:PCOL[f"wglr{s.layer}"] + KC * 32]\
                    .rearrange("p (d c m) -> p d c m", d=2, c=KC)
                for d in range(2):
                    for c in range(KC):
                        m = pe.matmul(bank[6 + d][0:16, :], wg[:, d, c, :], H[:, c, :], start=c == 0, stop=c == KC - 1)
                m.then_inc(*s.tick("glr"))
                project(s, 0, bank[0][:, 0:n], slice(c0, T2))
                project(s, 1, bank[1][:, :], slice(0, T2))
                for u in range(2):
                    project_tokens(s, 2 + u, [bank[2 + t // 2][:, (t % 2) * S + u * P:(t % 2) * S + (u + 1) * P]
                                              for t in range(4)], 0)
                pe.wait_ge(*s.done("loaded4"))
                pe.wait_ge(*s.done("glr_taken", 1))
                for d in range(2):
                    m = pe.matmul(bank[4 + d][:, :], W[4][0:16, d, :], (glr, glr2)[d][0:16, 0:T2], start=True, stop=True)
                m.then_inc(*s.tick("unit"))
                for u in range(2):
                    project(s, 5 + u, bank[6 + u][:, 0:n], slice(c0, T2))
                pe.wait_ge(*s.done("q_taken"))
                pe.wait_ge(*s.done("k_taken"))
                for lv in range(len(LEVELS) + 1):
                    b = bank[lv % 2]
                    if lv >= 2:
                        pe.wait_ge(*s.done("scored", lv - 2))
                    if lv:
                        pe.wait_ge(*s.done("level", lv - 1))
                    for c in active:
                        cs = slice(c * P, (c + 1) * P)
                        m = pe.matmul(b[:, cs], (mk if lv else gk)[:, cs], (mq if lv else gq)[:, cs],
                                      start=True, stop=True)
                    m.then_inc(*s.tick("level_scores"))
                pe.wait_ge(*s.done("v_taken"))
                pe.wait_ge(*s.done("decayed"))
                for d, order in enumerate((orderf, orderb)):
                    for c in order[:3]:
                        m = pe.transpose(bank[2 + d][:, c * P:(c + 1) * P], kw[:, d, c * P:(c + 1) * P], ident)
                m.then_inc(*s.tick("kw_transposed"))
                pe.wait_ge(*s.done("kw_taken"))
                for j in range(3):
                    for d, order in enumerate((orderf, orderb)):
                        if j:
                            pe.wait_ge(*s.done(f"state{d}", j - 1))
                        pe.matmul(bank[4 + d][:, 0:S], kwt[:, d, order[j], :], gv[:, order[j], :],
                                  start=True, stop=True).then_inc(*s.tick(f"update{d}"))
                pe.wait_ge(*s.done("r_taken"))
                pe.wait_ge(*s.done("state0", 2))
                pe.wait_ge(*s.done("state1", 2))
                pe.wait_ge(*s.done("scored", len(LEVELS)))
                for e in range(2):
                    es = slice(e * P, (e + 1) * P)
                    for c in active:
                        o = bank[6 + e][:, c * P - c0:(c + 1) * P - c0]
                        cs = slice(c * P, (c + 1) * P)
                        m = pe.matmul(o, gv[:, c, es], scores[:, c, :], start=True, stop=False)
                        if c != orderf[0]:
                            m = pe.matmul(o, states[:, 0, c, es], qdecay[:, 0, cs], start=False, stop=c == orderb[0])
                        if c != orderb[0]:
                            m = pe.matmul(o, states[:, 1, c, es], qdecay[:, 1, cs], start=False, stop=True)
                m.then_inc(*s.tick("gla_out"))
                for e in range(2):
                    pe.wait_ge(*s.done("gla_squared", e))
                    m = pe.matmul(bank[0][:, 0:n], const("mean256"), dist[:, e, 0:n], start=e == 0, stop=e == 1)
                m.then_inc(*s.tick("variance"))

            def conv(s):
                c0 = first_column(s.layer)
                for j in range(2):
                    pe.wait_ge(*s.before(f"glu{j}"))
                    for u in range(2):
                        project(s, 2 * j + u, bank[2 * j + u][:, 0:T2 - c0], slice(c0, T2))

            run(pe, {"prepare": prepare, "forget": forget, "fox": fox, "lru_in": lru_in, "stick": stick,
                     "memory": memory, "merge1": merge1, "out1": out_tiles, "norm_ffn1": norm_ffn1, "up1": up,
                     "down1": down, "ada": ada, "modulation": modulation, "ln_mixer": layernorm, "attend": attend,
                     "gla": gla, "conv": conv, "conv_norm": layernorm, "merge2": merge2, "out2": out_tiles,
                     "post_mixer": layernorm, "ln_ffn": layernorm, "up2": up, "down2": down, "post_ffn": layernorm})

        @block.scalar
        def _(act):
            def tables(which):
                act.add_instruction(mybir.InstLoadActFuncSet(
                    act_func_set_id=which, name=nc.get_next_instruction_name(),
                    engine=mybir.EngineType.Activation, ins=[], outs=[]))

            def fence(s):
                act.wait_ge(*s.so_far("act"))

            def rsqrt(s, out_ap, mean_ap, tmp, factor=1.0, name="rstd", eps=EPS):
                act.activation(tmp, mean_ap, ACT.Ln, bias=eps).then_inc(*s.tick("act"))
                fence(s)
                act.activation(out_ap, tmp, ACT.Exp, scale=-0.5, bias=float(np.log(factor)))\
                   .then_inc(*s.tick(name))

            def prepare(s):
                act.wait_ge(*s.done("variance"))
                rsqrt(s, work(0, T2), bank[0][:, :], work(512, T2))

            def forget(s):
                act.wait_ge(*s.done("forget_logits"))
                y, e = small_f[0:48, 0, :], small_f[0:48, 1, :]
                act.activation(y, bank[0][0:48, 0:S], ACT.Identity, bias=par("bf", 0, 48)).then_inc(*s.tick("act"))
                fence(s)
                act.activation(e, y, ACT.Abs).then_inc(*s.tick("act"))
                fence(s)
                act.activation(e, e, ACT.Exp, scale=-1.0).then_inc(*s.tick("act"))
                fence(s)
                act.activation(e, e, ACT.Ln, bias=1.0).then_inc(*s.tick("forget_ln"))
                lam = PR[:, PCOL["lru_lam"]:PCOL["lru_lam"] + KC]
                act.activation(small[:, 0:KC], lam, ACT.Abs).then_inc(*s.tick("act"))
                fence(s)
                act.activation(small[:, 0:KC], small[:, 0:KC], ACT.Exp, scale=-1.0).then_inc(*s.tick("lam_exp"))

            def fox(s):
                for j in range(2):
                    act.wait_ge(*s.done("unit", j))
                    if j == 0:
                        act.wait_ge(*s.before("variance"))
                    act.activation(sq2[:, j, 0:S], bank[j][:, 0:S], ACT.Square).then_inc(*s.tick("qk_squared"))
                act.wait_ge(*s.done("variance"))
                act.wait_ge(*s.before("k_taken"))
                act.activation(rstd[:, 1, :], bank[3][:, :], ACT.Ln, bias=EPS).then_inc(*s.tick("act"))
                fence(s)
                act.activation(rstd[:, 0, 0:S], rstd[:, 1, 0:S], ACT.Exp, scale=-0.5, bias=float(np.log(64 ** -0.5)))
                act.activation(rstd[:, 0, S:T2], rstd[:, 1, S:T2], ACT.Exp, scale=-0.5).then_inc(*s.tick("rstd"))
                act.wait_ge(*s.done("unit", 2))
                act.wait_ge(*s.before("pv0"))
                act.wait_ge(*s.before("pv1"))
                act.activation(vt[:, 0:2, :], bank[2][:, 0:S].rearrange("p (t d) -> p t d", t=2), ACT.Copy)\
                   .then_inc(*s.tick("v_taken"))
                soft_exp(act, s, 0, bank[4], FOX_SEGS)
                soft_exp(act, s, 1, bank[5], FOX_SEGS)
                for k in range(2):
                    soft_take(act, s, k, bank[6], 3 * P)

            def lru_in(s):
                i = s.turn
                act.wait_ge(*s.done("unit", 1))
                act.activation(lru_g[:, bass.ds(i * S, S)], bank[1][:, 0:S], ACT.Copy).then_inc(*s.tick("gate_taken"))
                act.wait_ge(*s.done("unit", 2))
                act.activation(lru_r[:, bass.ds(i * S, S)], bank[2][:, 0:S], ACT.Sigmoid, bias=par("lru_ba", i))
                act.activation(lru_i[:, bass.ds(i * S, S)], bank[3][:, 0:S], ACT.Sigmoid, bias=par("lru_bx", i))\
                   .then_inc(*s.tick("ri_taken"))

            def lru_mix(s):
                t1, t2 = work(0, KC * S), work(KC * S, KC * S)
                act.wait_ge(*s.done("log_a"))
                act.activation(t1, lru_r, ACT.Tanh).then_inc(*s.tick("tanh_a"))
                act.wait_ge(*s.done("gelu_in"))
                act.activation(t2, t2, ACT.Tanh, scale=float(np.sqrt(2 / np.pi))).then_inc(*s.tick("gelu_tanh"))
                tables(ACT_SET_LN_EXP)
                act.wait_ge(*s.done("one_minus_a2"))
                act.activation(t1, t1, ACT.Ln).then_inc(*s.tick("act"))
                fence(s)
                act.activation(t1, t1, ACT.Exp, scale=0.5).then_inc(*s.tick("root"))
                act.activation(lru_r, lru_r, ACT.Exp).then_inc(*s.tick("a"))

            def stick(s):
                act.wait_ge(*s.done("unit", 0))
                act.wait_ge(*s.before("logits"))
                act.activation(qn[:, 0:S], bank[0][:, 0:S], ACT.Copy, scale=64 ** -0.5).then_inc(*s.tick("q_taken"))
                act.wait_ge(*s.done("unit", 2))
                act.wait_ge(*s.before("pv0"))
                act.wait_ge(*s.before("pv1"))
                act.activation(vt[:, 0:2, :], bank[2][:, 0:S].rearrange("p (t d) -> p t d", t=2), ACT.Copy)\
                   .then_inc(*s.tick("v_taken"))
                for k in range(2):
                    z, e = rstd[:, k, 0:3 * P], sq2[:, k, 0:3 * P]
                    act.wait_ge(*s.done("logits", k))
                    act.wait_ge(*s.before(f"minus_suffix{k}"))
                    act.activation(z, bank[4 + k][:, 0:3 * P], ACT.Copy).then_inc(*s.tick("act"))
                    act.wait_ge(*s.before("suffix", k))
                    act.activation(e, bank[4 + k][:, 0:3 * P], ACT.Abs).then_inc(*s.tick("log_beta"))
                    act.wait_ge(*s.so_far("log_beta"))
                    act.activation(e, e, ACT.Exp, scale=-1.0).then_inc(*s.tick("act"))
                    fence(s)
                    act.activation(e, e, ACT.Ln, bias=1.0).then_inc(*s.tick("log1p"))
                for k in range(2):
                    act.wait_ge(*s.done(f"minus_suffix{k}"))
                    act.activation(probs[:, k, 0:3 * P], probs[:, k, 0:3 * P], ACT.Exp).then_inc(*s.tick("weights"))

            def memory(s):
                for j in range(2):
                    act.wait_ge(*s.done("unit", 2 * j + 1))
                    if j == 0:
                        act.wait_ge(*s.before("variance"))
                    act.activation(sq2[:, j, :], bank[j][:, :], ACT.Square).then_inc(*s.tick("qk_squared"))
                act.wait_ge(*s.done("variance"))
                act.wait_ge(*s.before("q_taken"))
                act.activation(rstd[:, 1, :], bank[3][:, :], ACT.Ln, bias=EPS).then_inc(*s.tick("act"))
                fence(s)
                act.activation(rstd[:, 0, 0:S], rstd[:, 1, 0:S], ACT.Exp, scale=-0.5)
                act.activation(rstd[:, 0, S:T2], rstd[:, 1, S:T2], ACT.Exp, scale=-0.5, bias=float(np.log(256 ** -0.5)))\
                   .then_inc(*s.tick("rstd"))
                act.wait_ge(*s.done("unit", 5))
                act.wait_ge(*s.before("pv0"))
                act.activation(mem_v, bank[2][:, :].rearrange("p (t e) -> p t e", t=2), ACT.Copy)\
                   .then_inc(*s.tick("v_taken"))
                soft_exp(act, s, 0, bank[4], MEM_SEGS)
                soft_take(act, s, 0, bank[6], T2)

            def merge(s, count, width, bias):
                for n in range(count):
                    act.wait_ge(*s.done("unit", 2 * n))
                    act.wait_ge(*s.before(f"mixed{n}"))
                    act.activation(sg[:, n, 0:width], bank[2 * n][:, 0:width], ACT.Sigmoid,
                                   bias=bias(n)).then_inc(*s.tick(f"gate{n}"))

            def merge1(s):
                merge(s, 4, S, lambda n: par("b_gate", s.turn + n * KC))

            def merge2(s):
                merge(s, 3, T2 - first_column(s.layer), lambda n: 0.0)

            def norm_ffn1(s):
                for c in range(KC):
                    act.activation(SQ[:, c, XS], X[:, c, XS], ACT.Square).then_inc(*s.tick("squared"))
                act.wait_ge(*s.done("variance"))
                rsqrt(s, work(0, S), bank[0][:, 0:S], work(512, S))

            def up1(s):
                for j in range(2):
                    act.wait_ge(*s.done(f"gate_conv{j}"))
                    act.activation(up_s[:, j, 0:S], up_c[:, j, 0:S], ACT.Sigmoid).then_inc(*s.tick(f"gate_sig{j}"))

            def up2(s):
                n = T2 - first_column(s.layer)
                for j in range(2):
                    act.wait_ge(*s.done("unit", 2 * j))
                    act.wait_ge(*s.before(f"hidden{j}"))
                    act.activation(up_s[:, j, 0:n], bank[2 * j][:, 0:n], ACT.Sigmoid).then_inc(*s.tick(f"gate_sig{j}"))

            def cond(s):
                c = PR[:, PCOL["cond"]:PCOL["cond"] + 2 * KC]
                act.activation(COND[:, :, :].rearrange("p c m -> p (c m)"), c, ACT.Sigmoid).then_inc(*s.tick("cond_sig"))

            def ada(s):
                for j in range(2):
                    act.wait_ge(*s.done("unit", 4 * j + 3))
                    act.activation(WORK[0:2, bass.ds((s.turn * 2 + j) * 512, 512)], bank[j][0:2, :], ACT.Copy)\
                       .then_inc(*s.tick(f"row{j}"))

            def layernorm(s, dest, scale, shift):
                c0 = norm_column(s.plan[s.number][0], s.layer)
                n = T2 - c0
                cen = MX if s.plan[s.number][0] == "conv_norm" else H
                for c in range(KC):
                    act.wait_ge(*s.done("centred", c))
                    act.activation(SQ[:, c, c0:T2], cen[:, c, c0:T2], ACT.Square).then_inc(*s.tick("squared"))
                act.wait_ge(*s.done("variance"))
                rsqrt(s, work(0, n), bank[1][:, 0:n], work(512, n))
                for c in range(KC):
                    act.wait_ge(*s.done("scaled", c))
                    for part in ([0, 1] if c0 == 0 else [1]):
                        cs = slice(part * S, (part + 1) * S)
                        act.activation(dest[:, c, cs], cen[:, c, cs], ACT.Identity, scale=scale(c, part),
                                       bias=shift(c, part)).then_inc(*s.tick("affine"))

            def ln_mixer(s):
                layernorm(s, H, lambda c, part: MOD[:, 8 + c, 1 - part:2 - part],
                          lambda c, part: MOD[:, c, 1 - part:2 - part])

            def ln_ffn(s):
                layernorm(s, H, lambda c, part: MOD[:, 32 + c, 1 - part:2 - part],
                          lambda c, part: MOD[:, 24 + c, 1 - part:2 - part])

            def post_mixer(s):
                layernorm(s, X, lambda c, part: par(f"ln1_g{s.layer}", c), lambda c, part: par(f"ln1_b{s.layer}", c))

            def post_ffn(s):
                layernorm(s, X, lambda c, part: par(f"ln2_g{s.layer}", c), lambda c, part: par(f"ln2_b{s.layer}", c))

            def conv_norm(s):
                layernorm(s, MX, lambda c, part: par(f"conv_g{s.layer}", c), lambda c, part: par(f"conv_be{s.layer}", c))
                tables(ACT_SET_SIGMOID)
                act.wait_ge(*s.so_far("affine"))
                c0 = first_column(s.layer)
                for c in range(KC):
                    act.activation(SQ[:, c, c0:T2], MX[:, c, c0:T2], ACT.Sigmoid).then_inc(*s.tick("conv_sig"))

            def attend(s):
                c0 = first_column(s.layer)
                for j in range(5):
                    n = T2 if j == 0 else T2 - c0
                    act.wait_ge(*s.done("unit", 0 if j == 0 else 1 + j))
                    act.wait_ge(*s.before("variance", j))
                    act.activation(sq2[:, 0, 0:n], bank[0][:, 0:n], ACT.Square).then_inc(*s.tick("head_squared"))
                    act.wait_ge(*s.done("variance", j))
                    act.wait_ge(*s.before("head_taken", j))
                    rsqrt(s, rstd[:, 0, 0:n], bank[2][:, 0:n], rstd[:, 1, 0:n],
                          1.0 if j == 0 else P ** -0.5, "head_rstd")
                    if j == 0:
                        act.wait_ge(*s.done("unit", 1))
                        act.wait_ge(*s.before("pv0"))
                        act.wait_ge(*s.before("pv1"))
                        act.activation(vt, bank[1][:, :].rearrange("p (t e) -> p t e", t=4), ACT.Copy)\
                           .then_inc(*s.tick("v_taken"))
                units = attend_units(s.layer)

                def exp(k):
                    soft_exp(act, s, k, bank[4 + k % 2], LAT_SEGS if units[k][1] == "x" else MEM_SEGS)

                exp(0)
                for k in range(len(units)):
                    if k + 1 < len(units):
                        exp(k + 1)
                    soft_take(act, s, k, bank[6], T2)

            def gla(s):
                i = s.turn
                c0 = first_column(s.layer)
                n = T2 - c0
                act.wait_ge(*s.done("glr"))
                act.activation(glr[0:16, :], bank[6][0:16, :], ACT.Copy).then_inc(*s.tick("glr_taken"))
                act.activation(glr2[0:16, :], bank[7][0:16, :], ACT.Copy).then_inc(*s.tick("glr_taken"))
                act.wait_ge(*s.done("unit", 0))
                act.activation(gq[:, c0:T2], bank[0][:, 0:n], ACT.Copy, scale=P ** -0.5).then_inc(*s.tick("q_taken"))
                act.wait_ge(*s.done("unit", 3))
                for t in range(2):
                    v = act.activation(gv[:, 2 * t:2 * t + 2, :], bank[2 + t][:, :].rearrange("p (t e) -> p t e", t=2),
                                       ACT.Copy)
                v.then_inc(*s.tick("v_taken"))
                act.wait_ge(*s.done("unit", 4))
                for d in range(2):
                    y, e = dist[:, d, :], (gtmp, gtmp2)[d]
                    act.activation(y, bank[4 + d][:, :], ACT.Identity, bias=par(f"gla_ba{s.layer}", i + 4 * d))\
                       .then_inc(*s.tick("act"))
                    fence(s)
                    act.activation(e, y, ACT.Abs).then_inc(*s.tick("act"))
                    fence(s)
                    act.activation(e, e, ACT.Exp, scale=-1.0).then_inc(*s.tick("act"))
                    fence(s)
                    act.activation(e, e, ACT.Ln, bias=1.0).then_inc(*s.tick("gate_ln"))
                act.wait_ge(*s.done("unit", 6))
                for u in range(2):
                    act.activation(gr[:, u, 0:n], bank[6 + u][:, 0:n], ACT.Exp, scale=-1.0).then_inc(*s.tick("r_exp"))
                for lv, m in enumerate(LEVELS):
                    act.wait_ge(*s.done("dist", lv))
                    f, b = (halves(dist[:, d, c0:T2], m) for d in range(2))
                    oq, ok = halves(eq[:, c0:T2], m), halves(ek[:, c0:T2], m)
                    if lv:
                        act.wait_ge(*s.done("level", lv - 1))
                    act.activation(oq[:, :, 0, :], b[:, :, 0, :], ACT.Exp, scale=1 / GLA_TAU)
                    act.activation(oq[:, :, 1, :], f[:, :, 1, :], ACT.Exp, scale=1 / GLA_TAU)
                    act.activation(ok[:, :, 0, :], f[:, :, 0, :], ACT.Exp, scale=-1 / GLA_TAU)
                    act.activation(ok[:, :, 1, :], b[:, :, 1, :], ACT.Exp, scale=-1 / GLA_TAU)\
                       .then_inc(*s.tick("level_exp"))
                act.wait_ge(*s.done("cum"))
                for d in range(2):
                    act.activation(qdecay[:, d, c0:T2], cum[:, d, c0:T2], ACT.Exp, scale=1 / GLA_TAU)\
                       .then_inc(*s.tick("qdecay_exp"))
                act.wait_ge(*s.done("end_dist"))
                act.activation(kw[:, :, :], kw[:, :, :], ACT.Exp, scale=1 / GLA_TAU).then_inc(*s.tick("kw_exp"))
                for d, at in enumerate((P - 1, 0)):
                    e = act.activation(decay[:, d, :], cum[:, d, :].rearrange("p (c t) -> p c t", c=4)[:, :, at],
                                       ACT.Exp, scale=1 / GLA_TAU)
                e.then_inc(*s.tick("decay_exp"))
                act.wait_ge(*s.done("kw_transposed"))
                for d, order in enumerate((orderf, orderb)):
                    for c in order[:3]:
                        e = act.activation(kwt[:, d, c, :], bank[2 + d][:, c * P:(c + 1) * P], ACT.Copy)
                e.then_inc(*s.tick("kw_taken"))
                act.wait_ge(*s.done("gla_out"))
                for e in range(2):
                    act.activation(dist[:, e, 0:n], bank[6 + e][:, 0:n], ACT.Square).then_inc(*s.tick("gla_squared"))
                act.wait_ge(*s.done("variance"))
                rsqrt(s, eq[:, 0:n], bank[0][:, 0:n], ek[:, 0:n], 1.0, "gla_rstd")

            def conv(s):
                n = T2 - first_column(s.layer)
                for j in range(2):
                    act.wait_ge(*s.done("unit", 2 * j + 1))
                    act.wait_ge(*s.before(f"glu{j}"))
                    act.activation(conv_sg[:, j, 0:n], bank[2 * j + 1][:, 0:n], ACT.Sigmoid)\
                       .then_inc(*s.tick(f"glu_sig{j}"))

            bodies = {"prepare": prepare, "forget": forget, "fox": fox, "lru_in": lru_in, "lru_mix": lru_mix,
                      "stick": stick, "memory": memory, "merge1": merge1, "norm_ffn1": norm_ffn1, "up1": up1,
                      "cond": cond, "ada": ada, "ln_mixer": ln_mixer, "attend": attend, "gla": gla, "conv": conv,
                      "conv_norm": conv_norm, "merge2": merge2, "post_mixer": post_mixer, "ln_ffn": ln_ffn,
                      "up2": up2, "post_ffn": post_ffn}
            sets = {"prepare": ACT_SET_LN_EXP, "lru_in": ACT_SET_SIGMOID, "merge1": ACT_SET_SIGMOID,
                    "norm_ffn1": ACT_SET_LN_EXP, "up1": ACT_SET_SIGMOID, "ln_mixer": ACT_SET_LN_EXP,
                    "conv": ACT_SET_SIGMOID, "conv_norm": ACT_SET_LN_EXP, "post_mixer": ACT_SET_LN_EXP,
                    "up2": ACT_SET_SIGMOID, "post_ffn": ACT_SET_LN_EXP}
            run(act, bodies, lambda kind: tables(sets[kind]) if kind in sets else None)

        @block.vector
        def _(dve):
            def link(s, instruction):
                instruction.then_inc(*s.tick("dve"))
                dve.wait_ge(*s.so_far("dve"))

            def rms_apply(s, dest, src, gain, r):
                for c in range(KC):
                    dve.scalar_tensor_tensor(dest[:, c, :], src[:, c, :], par(gain, c), r, ALU.mult, ALU.mult)

            def prepare(s):
                dve.wait_ge(tally.sem("inputs"), 80)
                for c in range(KC):
                    dve.tensor_tensor(SQ[:, c, CTX], MX[:, c, CTX], MX[:, c, CTX], ALU.mult)
                    dve.tensor_tensor(SQ[:, c, XS], X[:, c, XS], X[:, c, XS], ALU.mult).then_inc(*s.tick("squared"))
                dve.wait_ge(*s.done("rstd"))
                rms_apply(s, H[:, :, XS], X[:, :, XS], "attn_g", work(0, T2)[:, XS])
                rms_apply(s, H[:, :, CTX], MX[:, :, CTX], "mem_g", work(0, T2)[:, CTX])

            def forget(s):
                y, e = small_f[0:48, 0, :], small_f[0:48, 1, :]
                dve.wait_ge(*s.done("forget_ln"))
                link(s, dve.scalar_tensor_tensor(e, y, 0.0, e, ALU.min, ALU.subtract))
                link(s, dve.memset(y, 1.0))
                dve.tensor_tensor_scan(forget_f[0:48, :], y, e, 0.0, ALU.mult, ALU.add)
                dve.wait_ge(*s.done("lam_exp"))
                e, t, w, q = (small[:, j * KC:(j + 1) * KC] for j in range(4))
                link(s, dve.tensor_scalar(t, e, 2.0, None, ALU.add))
                link(s, dve.reciprocal(t, t))
                link(s, dve.tensor_tensor(t, t, e, ALU.mult))
                link(s, dve.tensor_tensor(w, t, t, ALU.mult))
                link(s, dve.tensor_scalar(q, w, 2.0 / 19, 2.0 / 17, ALU.mult, ALU.add))
                for n in range(15, 0, -2):
                    link(s, dve.tensor_tensor(q, q, w, ALU.mult))
                    link(s, dve.tensor_scalar(q, q, 2.0 / n, None, ALU.add))
                link(s, dve.tensor_tensor(q, q, t, ALU.mult))
                lam = PR[:, PCOL["lru_lam"]:PCOL["lru_lam"] + KC]
                link(s, dve.tensor_scalar(t, lam, -1.0, 0.0, ALU.mult, ALU.max))
                link(s, dve.tensor_tensor(q, q, t, ALU.add))
                dve.tensor_scalar(lru_c[:, :], q, -8.0, None, ALU.mult)

            def take_pair(s, k, y):
                dve.wait_ge(*s.done(f"pv{k}"))
                r = slice(64 * k, 64 * k + 64)
                dve.tensor_copy(y[r, s.turn, :], bank[7][r, 0:S]).then_inc(*s.tick(f"taken_out{k}"))

            def fox(s):
                dve.wait_ge(*s.before("logits"))
                for k in range(2):
                    h = s.turn * 2 + k
                    dve.tensor_scalar(forget_l[0:48, k, :], forget_f[0:48, :], CN[0:48, bass.ds(h + CCOL["head_l"], 1)],
                                      const("add_l", 1, 48), ALU.mult, ALU.add)
                    dve.tensor_scalar(forget_r[0:48, k, :], forget_f[0:48, :], CN[0:48, bass.ds(h + CCOL["head_r"], 1)],
                                      const("add_r", 1, 48), ALU.mult, ALU.add)
                dve.wait_ge(*s.done("rstd"))
                dve.scalar_tensor_tensor(qn[:, 0:S], bank[0][:, 0:S], par("fox_qg"), rstd[:, 0, 0:S],
                                         ALU.mult, ALU.mult).then_inc(*s.tick("q_taken"))
                for k in range(2):
                    o = dve.scalar_tensor_tensor(kn2[:, k, :], bank[1][:, 0:S], par("fox_kg", k), rstd[:, 0, S:T2],
                                                 ALU.mult, ALU.mult)
                o.then_inc(*s.tick("k_taken"))
                soft_max(dve, s, 0, bank[4], FOX_SEGS)
                soft_max(dve, s, 1, bank[5], FOX_SEGS)
                soft_norm(dve, s, 0, FOX_SEGS)
                soft_norm(dve, s, 1, FOX_SEGS)
                take_pair(s, 0, Y1[0])
                take_pair(s, 1, Y1[0])

            def lru_in(s):
                i = s.turn
                xc = lru_x[:, bass.ds(i * S, S)]
                dve.wait_ge(*s.done("unit", 0))
                link(s, dve.tensor_scalar(xc, bank[0][:, 0:S], par("lru_w", i + 3 * KC), par("lru_b", i),
                                          ALU.mult, ALU.add))
                for tap in (2, 1, 0):
                    sh = 3 - tap
                    part = lru_x[:, bass.ds(i * S + sh, S - sh)]
                    o = dve.scalar_tensor_tensor(part, bank[0][:, 0:S - sh], par("lru_w", i + tap * KC), part,
                                                 ALU.mult, ALU.add)
                    if tap:
                        link(s, o)
                o.then_inc(*s.tick("conv_done"))

            def lru_mix(s):
                t1, t2 = work(0, KC * S), work(KC * S, KC * S)
                v = lambda ap: ap.rearrange("p (c t) -> p c t", c=KC)
                dve.tensor_tensor(v(lru_r), v(lru_r), wide(lru_c[:, :].rearrange("p (c o) -> p c o", o=1), S), ALU.mult)\
                   .then_inc(*s.tick("log_a"))
                link(s, dve.tensor_tensor(t2, lru_g, lru_g, ALU.mult))
                link(s, dve.tensor_scalar(t2, t2, 0.044715, 1.0, ALU.mult, ALU.add))
                dve.tensor_tensor(t2, t2, lru_g, ALU.mult).then_inc(*s.tick("gelu_in"))
                link(s, dve.tensor_tensor(lru_i, lru_i, lru_x, ALU.mult))
                dve.wait_ge(*s.done("tanh_a"))
                t3 = work(2 * KC * S, KC * S)
                link(s, dve.tensor_scalar(t3, t1, -1.0, 1.0, ALU.mult, ALU.add))
                link(s, dve.reciprocal(t3, t3))
                link(s, dve.scalar_tensor_tensor(t1, t1, -2.0, t3, ALU.mult, ALU.mult))
                dve.tensor_scalar(t1, t1, 1e-18, None, ALU.max).then_inc(*s.tick("one_minus_a2"))
                dve.wait_ge(*s.done("gelu_tanh"))
                link(s, dve.scalar_tensor_tensor(lru_g, t2, 1.0, lru_g, ALU.add, ALU.mult))
                dve.wait_ge(*s.done("root"))
                dve.wait_ge(*s.done("a"))
                link(s, dve.tensor_tensor(lru_i, lru_i, t1, ALU.mult))
                y = YG[:, KC * S:2 * KC * S]
                for c in range(KC):
                    cs = slice(c * S, (c + 1) * S)
                    o = dve.tensor_tensor_scan(y[:, cs], lru_r[:, cs], lru_i[:, cs], 0.0, ALU.mult, ALU.add)
                link(s, o)
                dve.scalar_tensor_tensor(y, y, 0.5, lru_g, ALU.mult, ALU.mult)

            def stick(s):
                dve.wait_ge(*s.done("unit", 1))
                dve.wait_ge(*s.before("logits"))
                for k in range(2):
                    o = dve.tensor_scalar(kn2[:, k, :], bank[1][:, 0:S], const("head_rows", 1, P, k), None, ALU.mult)
                o.then_inc(*s.tick("k_taken"))
                for k in range(2):
                    z, e = rstd[:, k, 0:3 * P], sq2[:, k, 0:3 * P]
                    dve.wait_ge(*s.done("log1p", k))
                    link(s, dve.scalar_tensor_tensor(e, z, 0.0, e, ALU.max, ALU.add))
                    dve.tensor_tensor(e, e, const("strict", 3 * P), ALU.mult).then_inc(*s.tick("softplus"))
                for k in range(2):
                    b = bank[3 if k == 0 else 6]
                    dve.wait_ge(*s.done("suffix", k))
                    dve.wait_ge(*s.before(f"pv{k}"))
                    dve.tensor_tensor(probs[:, k, 0:3 * P], rstd[:, k, 0:3 * P], b[:, 0:3 * P], ALU.subtract)\
                       .then_inc(*s.tick(f"minus_suffix{k}"))
                take_pair(s, 0, Y1[2])
                take_pair(s, 1, Y1[2])

            def memory(s):
                dve.wait_ge(*s.done("rstd"))
                dve.wait_ge(*s.before("logits"))
                for u in range(2):
                    o = dve.scalar_tensor_tensor(kn[:, u * S:(u + 1) * S], bank[0][:, u * S:(u + 1) * S],
                                                 par("mem_kg", u), rstd[:, 0, 0:S], ALU.mult, ALU.mult)
                o.then_inc(*s.tick("k_taken"))
                for u in range(2):
                    o = dve.scalar_tensor_tensor(qn[:, u * S:(u + 1) * S], bank[1][:, u * S:(u + 1) * S],
                                                 par("mem_qg", u), rstd[:, 0, S:T2], ALU.mult, ALU.mult)
                o.then_inc(*s.tick("q_taken"))
                soft_max(dve, s, 0, bank[4], MEM_SEGS)
                soft_norm(dve, s, 0, MEM_SEGS)
                dve.wait_ge(*s.done("pv0"))
                dve.tensor_copy(Y1[3][:, bass.ds(s.turn * 2, 2), :], bank[7][:, :].rearrange("p (e t) -> p e t", e=2))\
                   .then_inc(*s.tick("taken_out0"))

            def merge(s, count, cols):
                w = T2 - cols.start
                for n in range(count):
                    dve.wait_ge(*s.done("unit", 2 * n + 1))
                    dve.wait_ge(*s.done(f"gate{n}"))
                    dest = MX[:, s.turn, cols]
                    if n == 0:
                        dve.tensor_tensor(dest, sg[:, n, 0:w], bank[2 * n + 1][:, 0:w], ALU.mult)\
                           .then_inc(*s.tick(f"mixed{n}"))
                    else:
                        link(s, dve.tensor_tensor(sg[:, n, 0:w], sg[:, n, 0:w], bank[2 * n + 1][:, 0:w], ALU.mult))
                        dve.tensor_tensor(dest, dest, sg[:, n, 0:w], ALU.add).then_inc(*s.tick(f"mixed{n}"))
                    dve.wait_ge(*s.done(f"mixed{n}"))

            def merge1(s):
                merge(s, 4, XS)

            def merge2(s):
                merge(s, 3, slice(first_column(s.layer), T2))

            def out1(s):
                for u in range(4):
                    dve.wait_ge(*s.done("unit", u))
                    t = X[:, s.turn * 4 + u, XS]
                    dve.tensor_tensor(t, t, bank[u][:, 0:S], ALU.add).then_inc(*s.tick(f"added{u}"))

            def down1(s):
                for j in range(2):
                    dve.wait_ge(*s.done("unit", 3 * j + 2))
                    t = X[:, s.turn * 2 + j, XS]
                    dve.tensor_tensor(t, t, bank[j][:, 0:S], ALU.add).then_inc(*s.tick(f"added{j}"))

            def gated_add(s, u, tile, b, gate):
                c0 = first_column(s.layer)
                for part in ([0, 1] if c0 == 0 else [1]):
                    o = dve.tensor_scalar(up_s[:, 0, part * S:(part + 1) * S], b[:, part * S - c0:(part + 1) * S - c0],
                                          MOD[:, bass.ds(tile + gate, 1), 1 - part:2 - part].rearrange("p a b -> p (a b)"),
                                          None, ALU.mult)
                link(s, o)
                t = X[:, tile, c0:T2]
                dve.scalar_tensor_tensor(t, t, ALPHA, up_s[:, 0, c0:T2], ALU.mult, ALU.add)\
                   .then_inc(*s.tick(f"added{u}"))
                dve.wait_ge(*s.done(f"added{u}"))

            def out2(s):
                for u in range(4):
                    dve.wait_ge(*s.done("unit", u))
                    gated_add(s, u, s.turn * 4 + u, bank[u], 16)

            def down2(s):
                for j in range(2):
                    dve.wait_ge(*s.done("unit", 3 * j + 2))
                    gated_add(s, j, s.turn * 2 + j, bank[j], 40)

            def norm_ffn1(s):
                dve.wait_ge(*s.done("rstd"))
                rms_apply(s, H[:, :, XS], X[:, :, XS], "ffn_g", work(0, S))

            def up1(s):
                for j in range(2):
                    f = s.turn * 2 + j
                    g = bank[2 * j]
                    c = up_c[:, j, :]
                    dve.wait_ge(*s.done("unit", 2 * j))
                    link(s, dve.tensor_scalar(c[:, 0:S], g[:, 0:S], par("ffn_w", f + 2 * FT), par("ffn_b", f),
                                              ALU.mult, ALU.add))
                    link(s, dve.scalar_tensor_tensor(c[:, 1:S], g[:, 0:S - 1], par("ffn_w", f + FT), c[:, 1:S],
                                                     ALU.mult, ALU.add))
                    dve.scalar_tensor_tensor(c[:, 2:S], g[:, 0:S - 2], par("ffn_w", f), c[:, 2:S],
                                             ALU.mult, ALU.add).then_inc(*s.tick(f"gate_conv{j}"))
                    dve.wait_ge(*s.done(f"gate_sig{j}"))
                    link(s, dve.tensor_tensor(c[:, 0:S], c[:, 0:S], up_s[:, j, 0:S], ALU.mult))
                    dve.wait_ge(*s.done("unit", 2 * j + 1))
                    dve.tensor_tensor(G[:, f, 0:S], c[:, 0:S], bank[2 * j + 1][:, 0:S], ALU.mult)\
                       .then_inc(*s.tick(f"hidden{j}"))

            def up2(s):
                c0 = first_column(s.layer)
                n = T2 - c0
                for j in range(2):
                    f = s.turn * 2 + j
                    dve.wait_ge(*s.done(f"gate_sig{j}"))
                    link(s, dve.tensor_tensor(up_c[:, j, 0:n], up_s[:, j, 0:n], bank[2 * j][:, 0:n], ALU.mult))
                    dve.wait_ge(*s.done("unit", 2 * j + 1))
                    dve.tensor_tensor(G[:, f, c0:T2], up_c[:, j, 0:n], bank[2 * j + 1][:, 0:n], ALU.mult)\
                       .then_inc(*s.tick(f"hidden{j}"))

            def cond(s):
                c = PR[:, PCOL["cond"]:PCOL["cond"] + 2 * KC]
                o = COND[:, :, :].rearrange("p c m -> p (c m)")
                dve.wait_ge(*s.done("cond_sig"))
                dve.tensor_tensor(o, o, c, ALU.mult)

            def modulation(s):
                b = PR[:, PCOL[f"b_ada{s.layer}"]:PCOL[f"b_ada{s.layer}"] + 48].rearrange("p (c o) -> p c o", o=1)
                dve.wait_ge(*s.done("mod_columns"))
                link(s, dve.tensor_tensor(MOD[:, :, :], bank[0][:, 0:96].rearrange("p (c o) -> p c o", o=2),
                                          wide(b, 2), ALU.add))
                for at in (8, 32):
                    dve.tensor_scalar(MOD[:, at:at + 8, :], MOD[:, at:at + 8, :], 1.0, None, ALU.add)

            def layernorm(s):
                c0 = norm_column(s.plan[s.number][0], s.layer)
                n = T2 - c0
                kind = s.plan[s.number][0]
                src, cen = (MX, MX) if kind == "conv_norm" else (X, H)
                dve.wait_ge(*s.done("mean"))
                for c in range(KC):
                    dve.tensor_tensor(cen[:, c, c0:T2], src[:, c, c0:T2], bank[0][:, 0:n], ALU.subtract)\
                       .then_inc(*s.tick("centred"))
                dve.wait_ge(*s.done("rstd"))
                for c in range(KC):
                    dve.wait_ge(*s.done("squared", c))
                    dve.tensor_tensor(cen[:, c, c0:T2], cen[:, c, c0:T2], work(0, n), ALU.mult)\
                       .then_inc(*s.tick("scaled"))
                if kind == "conv_norm":
                    for c in range(KC):
                        dve.wait_ge(*s.done("conv_sig", c))
                        dve.tensor_tensor(Y2[2][:, c, c0:T2], MX[:, c, c0:T2], SQ[:, c, c0:T2], ALU.mult)

            def attend(s):
                c0 = first_column(s.layer)
                cos, sin = const("cos", S), const("sin", S)
                for j in range(5):
                    n = T2 if j == 0 else T2 - c0
                    dest = att_k if j == 0 else att_q[:, j - 1, c0:T2]
                    gain = par(f"kg{s.layer}" if j == 0 else f"qg{s.layer}")
                    if j == 0:
                        dve.wait_ge(*s.before("logits"))
                    dve.wait_ge(*s.done("head_rstd", j))
                    dve.scalar_tensor_tensor(att_n[:, 0:n], bank[0][:, 0:n], gain, rstd[:, 0, 0:n],
                                             ALU.mult, ALU.mult).then_inc(*s.tick("head_taken"))
                    dve.wait_ge(*s.so_far("head_taken"))
                    if n == T2:
                        dve.tensor_copy(dest[:, 0:S], att_n[:, 0:S])
                    link(s, dve.tensor_tensor(dest[:, n - S:n], att_n[:, n - S:n], cos, ALU.mult))
                    dve.wait_ge(*s.done("swapped", j))
                    link(s, dve.tensor_tensor(att_t, sin, bank[3][:, 0:S], ALU.mult))
                    dve.tensor_tensor(dest[:, n - S:n], dest[:, n - S:n], att_t, ALU.add)\
                       .then_inc(*s.tick("rotated"))
                    dve.wait_ge(*s.so_far("rotated"))
                units = attend_units(s.layer)

                def segments(k):
                    return LAT_SEGS if units[k][1] == "x" else MEM_SEGS

                def take(k):
                    g, part, q = units[k]
                    w = P if part == "x" else S
                    at = S + q * P if part == "x" else 0
                    dve.wait_ge(*s.done(f"pv{k % 2}", k // 2))
                    dve.tensor_copy(Y2[0][:, s.turn * 4 + g, at:at + w], bank[7][:, 0:w])\
                       .then_inc(*s.tick("taken_out"))

                soft_max(dve, s, 0, bank[4], segments(0))
                for k in range(len(units)):
                    if k + 1 < len(units):
                        soft_max(dve, s, k + 1, bank[4 + (k + 1) % 2], segments(k + 1))
                    soft_norm(dve, s, k, segments(k))
                    if k:
                        take(k - 1)
                take(len(units) - 1)

            def gla(s):
                c0 = first_column(s.layer)
                n = T2 - c0
                first = c0 // P
                dve.wait_ge(*s.done("unit", 1))
                dve.tensor_copy(gk, bank[1][:, :]).then_inc(*s.tick("k_taken"))
                for d in range(2):
                    y, e = dist[:, d, :], (gtmp, gtmp2)[d]
                    dve.wait_ge(*s.done("gate_ln", d))
                    link(s, dve.scalar_tensor_tensor(e, y, 0.0, e, ALU.min, ALU.subtract))
                    if d == 0:
                        dve.tensor_tensor_scan(cum[:, 0, :], const("run_f", T2), e, 0.0, ALU.mult, ALU.add)
                    else:
                        dve.tensor_tensor_scan(cum[:, 1, ::-1], const("run_b", T2)[:, ::-1], e[:, ::-1], 0.0,
                                               ALU.mult, ALU.add).then_inc(*s.tick("cum"))
                dve.wait_ge(*s.so_far("cum"))
                dve.wait_ge(*s.done("r_exp", 1))
                link(s, dve.tensor_scalar(gr[:, :, 0:n], gr[:, :, 0:n], 1.0, None, ALU.add))
                link(s, dve.reciprocal(gr[:, :, 0:n], gr[:, :, 0:n]))
                for u in range(2):
                    o = dve.tensor_tensor(gr[:, u, 0:n], gr[:, u, 0:n], bank[6 + u][:, 0:n], ALU.mult)
                o.then_inc(*s.tick("r_taken"))

                def distances(lv):
                    m = LEVELS[lv]
                    if lv:
                        dve.wait_ge(*s.done("level_exp", lv - 1))
                    for d, at in enumerate((m - 1, m)):
                        v = cum[:, d, c0:T2].rearrange("p (n w) -> p n w", w=2 * m)
                        o = dve.tensor_tensor(dist[:, d, c0:T2].rearrange("p (n w) -> p n w", w=2 * m), v,
                                              wide(v[:, :, at:at + 1], 2 * m), ALU.subtract)
                    o.then_inc(*s.tick("dist"))

                distances(0)
                active = range(first, 4)
                sc = scores[:, first:4, :]

                def scored(lv):
                    b = bank[lv % 2][:, c0:T2].rearrange("p (c t) -> p c t", t=P)
                    dve.wait_ge(*s.done("level_scores", lv))
                    if lv == 0:
                        o = dve.tensor_tensor(sc, const("twice_ident").rearrange("p (o t) -> p o t", o=1)
                                              .broadcast_to([P, 4 - first, P]), b, ALU.mult)
                    else:
                        mask = const("levels", P, P, (lv - 1) * P).rearrange("p (o t) -> p o t", o=1)\
                            .broadcast_to([P, 4 - first, P]).bitcast(U32)
                        dve.wait_ge(*s.so_far("scored"))
                        dve.memset(small[:, 63:64], 0.0)
                        o = dve.copy_predicated(sc, mask, b)
                    o.then_inc(*s.tick("scored"))

                for lv in range(len(LEVELS)):
                    dve.wait_ge(*s.done("level_exp", lv))
                    if lv:
                        dve.wait_ge(*s.done("level_scores", lv))
                    dve.tensor_tensor(mq[:, c0:T2], gq[:, c0:T2], eq[:, c0:T2], ALU.mult)
                    dve.tensor_tensor(mk[:, c0:T2], gk[:, c0:T2], ek[:, c0:T2], ALU.mult).then_inc(*s.tick("level"))
                    if lv + 1 < len(LEVELS):
                        distances(lv + 1)
                    scored(lv)
                scored(len(LEVELS))
                for d, at in enumerate((P - 1, 0)):
                    v = cum[:, d, :].rearrange("p (c t) -> p c t", c=4)
                    o = dve.tensor_tensor(kw[:, d, :].rearrange("p (c t) -> p c t", c=4),
                                          wide(v[:, :, at:at + 1], P), v, ALU.subtract)
                o.then_inc(*s.tick("end_dist"))
                for d in range(2):
                    dve.wait_ge(*s.done("qdecay_exp", d))
                    dve.tensor_tensor(qdecay[:, d, c0:T2], qdecay[:, d, c0:T2], gq[:, c0:T2], ALU.mult)
                dve.wait_ge(*s.done("kw_exp"))
                for d in range(2):
                    o = dve.tensor_tensor(kw[:, d, :], kw[:, d, :], gk, ALU.mult)
                o.then_inc(*s.tick("decayed"))
                dve.wait_ge(*s.done("decay_exp"))
                for j in range(3):
                    for d, order in enumerate((orderf, orderb)):
                        c, nxt = order[j], order[j + 1]
                        dve.wait_ge(*s.done(f"update{d}", j))
                        if j == 0:
                            dve.tensor_copy(states[:, d, nxt, :], bank[4 + d][:, 0:S]).then_inc(*s.tick(f"state{d}"))
                        else:
                            dve.wait_ge(*s.so_far(f"state{d}"))
                            dve.scalar_tensor_tensor(states[:, d, nxt, :], states[:, d, c, :], decay[:, d, c:c + 1],
                                                     bank[4 + d][:, 0:S], ALU.mult, ALU.add)\
                               .then_inc(*s.tick(f"state{d}"))
                dve.wait_ge(*s.done("gla_rstd"))
                for e in range(2):
                    o = dve.scalar_tensor_tensor(dist[:, e, 0:n], bank[6 + e][:, 0:n], par(f"gla_g{s.layer}", e),
                                                 eq[:, 0:n], ALU.mult, ALU.mult)
                link(s, o)
                o = dve.tensor_tensor(Y2[1][:, bass.ds(s.turn * 2, 2), c0:T2], dist[:, :, 0:n], gr[:, :, 0:n], ALU.mult)
                o.then_inc(*s.tick("gla_end"))

            def conv(s):
                c0 = first_column(s.layer)
                n = T2 - c0
                parts = slice(c0 // S, 2)
                for j in range(2):
                    tile = s.turn * 2 + j
                    dve.wait_ge(*s.done(f"glu_sig{j}"))
                    for at in (0, PAD + S):
                        dve.memset(padded[j][:, :, at:at + PAD], 0.0)
                    dve.wait_ge(*s.so_far("dve"))
                    o = dve.tensor_tensor(padded[j][:, parts, PAD:PAD + S],
                                          conv_sg[:, j, 0:n].rearrange("p (a t) -> p a t", t=S),
                                          bank[2 * j][:, 0:n].rearrange("p (a t) -> p a t", t=S), ALU.mult)
                    o.then_inc(*s.tick(f"glu{j}"))
                    dve.wait_ge(*s.done(f"glu{j}"))
                    acc = MX[:, tile, c0:T2].rearrange("p (a t) -> p a t", t=S)
                    link(s, dve.tensor_scalar(acc, padded[j][:, parts, 0:S], par(f"conv_w{s.layer}", tile),
                                              par(f"conv_b{s.layer}", tile), ALU.mult, ALU.add))
                    for tap in range(1, CONV):
                        link(s, dve.scalar_tensor_tensor(acc, padded[j][:, parts, tap:tap + S],
                                                         par(f"conv_w{s.layer}", tile + tap * KC), acc,
                                                         ALU.mult, ALU.add))

            run(dve, {"prepare": prepare, "forget": forget, "fox": fox, "lru_in": lru_in, "lru_mix": lru_mix,
                      "stick": stick, "memory": memory, "merge1": merge1, "out1": out1, "norm_ffn1": norm_ffn1,
                      "up1": up1, "down1": down1, "cond": cond, "modulation": modulation, "ln_mixer": layernorm,
                      "attend": attend, "gla": gla, "conv": conv, "conv_norm": layernorm, "merge2": merge2,
                      "out2": out2, "post_mixer": layernorm, "ln_ffn": layernorm, "up2": up2, "down2": down2,
                      "post_ffn": layernorm})

        @block.gpsimd
        def _(pool):
            if dump is not None:
                for t in (H, MX, YG, SQ):
                    v = t[:, :, :] if t is not YG else t[:, :]
                    pool.memset(v, 0.0).then_inc(tally.sem("zeroed"), 1)
            for name in sorted(tally.primed):
                pool.nop().then_inc(tally.sem(name), 1)
            run(pool, {})

    return tally.seen



def columns(v):
    return np.asarray(v).reshape(-1, P).T


def unit(w, col, width=P):
    rows = w.shape[0]
    out = np.zeros((P, KC, P), np.float32)
    out[:, 0:rows // P, :] = w[:, col:col + P].reshape(rows // P, P, P).transpose(1, 0, 2)
    return out.reshape(P, KC * P)


def weight_stream(a):
    w_in, kv = a["w_in"][0], a["w_mem_kv"][0]
    fq, fk, fv, ff = 0, D, 2 * D, 3 * D
    lx = ff + 16
    lg, sq_, sk, sv = lx + D, lx + 2 * D, lx + 3 * D, lx + 4 * D
    mq, gates = lx + 5 * D, lx + 6 * D
    out = []
    for i in range(8):
        out += [unit(w_in, fq + i * P), unit(w_in, fk + i * P), unit(w_in, fv + i * P)]
    for i in range(8):
        diag = np.zeros((P, KC * P), np.float32)
        for j, name in enumerate(("lru_w_a", "lru_w_x")):
            for b in range(2):
                diag[64 * b:64 * b + 64, j * P + 64 * b:j * P + 64 * b + 64] = a[name][0, 2 * i + b]
        out += [unit(w_in, lx + i * P), unit(w_in, lg + i * P), diag]
    for i in range(8):
        out += [unit(w_in, sq_ + i * P), unit(w_in, sk + i * P), unit(w_in, sv + i * P)]
    for h in range(4):
        out += [unit(w, c + h * 2 * P + u * P) for w, c in ((kv, 0), (w_in, mq), (kv, D)) for u in range(2)]
    for i in range(8):
        for n in range(4):
            out += [unit(w_in, gates + n * D + i * P), unit(a["w_branch"][0, n], i * P)]
    out += [unit(a["w_out"][0], i * P) for i in range(8)]
    for f in range(FT):
        out += [unit(a["w_up"][0], f * P), unit(a["w_up"][0], D_FF + f * P)]
    for i in range(8):
        out += [unit(a["w_down"][0][q * D:(q + 1) * D], i * P) for q in range(3)]
    for l in range(LAYERS):
        ada = a["w_ada_2"][l].reshape(4, 2, P, 12, 512).transpose(3, 0, 2, 1, 4)
        out += list(ada.reshape(48, P, 1024))
        w = a["w_in_2"][l]
        k, v, kg, vg, glr = 0, 256, 512, 1024, 2048
        q, qg, r = 2080, 2080 + 1024, 2080 + 1536
        glu, gate = r + 1024, r + 1024 + 2048
        for j in range(2):
            out += [unit(w, k + j * P), unit(w, v + j * P)] + [unit(w, q + (4 * j + g) * P) for g in range(4)]
        for h in range(4):
            a2 = np.zeros((P, KC * P), np.float32)
            for d in range(2):
                a2[0:16, d * P:(d + 1) * P] = a["gla_w_a2_2"][l, d][:, h * P:(h + 1) * P]
            out += [unit(w, qg + h * P), unit(w, kg + h * P), unit(w, vg + 2 * h * P), unit(w, vg + (2 * h + 1) * P),
                    a2, unit(w, r + 2 * h * P), unit(w, r + (2 * h + 1) * P)]
        for i in range(8):
            out += [unit(w, glu + i * P), unit(w, glu + D + i * P)]
        for i in range(8):
            for n, name in enumerate(("w_att_o_2", "w_gla_o_2", "w_conv_o_2")):
                out += [unit(w, gate + n * D + i * P), unit(a[name][l], i * P)]
        out += [unit(a["w_out_2"][l], i * P) for i in range(8)]
        for f in range(FT):
            out += [unit(a["w_ff_gate_2"][l], f * P), unit(a["w_ff_up_2"][l], f * P)]
        for i in range(8):
            out += [unit(a["w_ff_down_2"][l][q_ * D:(q_ + 1) * D], i * P) for q_ in range(3)]
    return np.stack(out)


def parameters(a):
    p = np.zeros((P, N_PARAMS), np.float32)

    def put(name, block):
        p[0:block.shape[0], PCOL[name]:PCOL[name] + block.shape[1]] = block

    put("attn_g", columns(a["attn_norm_g"]))
    put("mem_g", columns(a["mem_norm_g"]))
    wf = np.zeros((P, KC, 48), np.float32)
    wf[:, :, 0:16] = a["w_in"][0][:, 3 * D:3 * D + 16].reshape(KC, P, 16).transpose(1, 0, 2)
    wf[:, :, 32:48] = wf[:, :, 0:16]
    put("wf", wf.reshape(P, -1))
    bf = np.zeros((48, 1), np.float32)
    bf[0:16, 0] = bf[32:48, 0] = a["b_forget"][0]
    put("bf", bf)
    put("fox_qg", np.tile(a["fox_q_norm_g"][0], 2)[:, None])
    for k in range(2):
        p[64 * k:64 * k + 64, PCOL["fox_kg"] + k] = a["fox_k_norm_g"][0]
    put("lru_w", columns(a["lru_conv_w"][0]))
    for name, key in (("lru_b", "lru_conv_b"), ("lru_ba", "lru_b_a"), ("lru_bx", "lru_b_x"), ("lru_lam", "lru_lambda"),
                      ("mem_qg", "mem_q_norm_g"), ("mem_kg", "mem_k_norm_g"), ("b_gate", "b_gate"),
                      ("ffn_g", "ffn_norm_g"), ("ffn_w", "ffn_conv_w"), ("ffn_b", "ffn_conv_b")):
        put(name, columns(a[key][0]))
    put("cond", np.stack([columns(a["c_2"][0]), columns(a["c_ctx_2"])], axis=2).reshape(P, -1))
    for l in range(LAYERS):
        for name, key in (("b_ada", "b_ada_2"), ("qg", "q_norm_2"), ("kg", "k_norm_2"), ("gla_ba", "gla_b_a_2"),
                          ("gla_g", "gla_norm_2"), ("conv_w", "conv_w_dw_2"), ("conv_b", "conv_b_dw_2"),
                          ("conv_g", "conv_ln_g_2"), ("conv_be", "conv_ln_b_2"), ("ln1_g", "ln1_g_2"),
                          ("ln1_b", "ln1_b_2"), ("ln2_g", "ln2_g_2"), ("ln2_b", "ln2_b_2")):
            put(f"{name}{l}", columns(a[key][l]))
        glr = a["w_in_2"][l][:, 2048:2080].reshape(KC, P, 2, 16).transpose(1, 2, 0, 3)
        put(f"wglr{l}", glr.reshape(P, -1))
    return p


def constants():
    c = np.zeros((P, N_CONSTS), np.float32)

    def put(name, block, at=0):
        block = np.asarray(block, np.float32)
        c[0:block.shape[0], CCOL[name] + at:CCOL[name] + at + block.shape[1]] = block

    k, q = np.arange(P)[:, None], np.arange(P)[None, :]
    eye = np.eye(P)
    put("ident", eye)
    put("mean1024", np.full((P, P), 1 / 1024))
    put("mean64", (k // 64 == q // 64) / 64)
    put("mean128", np.full((P, P), 1 / 128))
    put("mean256", np.full((P, P), 1 / 256))
    put("ones", np.ones((P, P)))
    put("suffix", k >= q)
    swap = np.zeros((P, P))
    swap[np.arange(1, P, 2), np.arange(0, P, 2)] = -1
    swap[np.arange(0, P, 2), np.arange(1, P, 2)] = 1
    put("swap", swap)
    put("causal_neg", np.where(q > k, NEG, 0.0))
    strict = k < q
    put("strict", np.concatenate([strict, np.ones((P, P)), strict], 1))
    big = np.where(strict, 0.0, -NEG)
    put("strict_big", np.concatenate([big, np.zeros((P, P)), big], 1))
    for n, m in enumerate(LEVELS):
        put("levels", (k // (2 * m) == q // (2 * m)) & (k // m != q // m), n * P)
    put("twice_ident", 2 * eye)
    t = np.arange(S)
    half = P // 2
    inv = np.float32(10000.0) ** (-np.arange(0, half, 2, dtype=np.float32) / np.float32(half))
    ang = np.concatenate([(t // 64).astype(np.float32)[:, None] * inv, (t % 64).astype(np.float32)[:, None] * inv], 1)
    put("cos", np.repeat(np.cos(ang), 2, axis=1).T)
    put("sin", np.repeat(np.sin(ang), 2, axis=1).T)
    cols = np.arange(T2)
    put("run_f", np.tile((cols % P != 0), (P, 1)))
    put("run_b", np.tile((cols % P != P - 1), (P, 1)))
    h = np.arange(16)[None, :]
    rows = np.arange(48)[:, None]
    put("head_l", rows == 32 + h)
    put("head_r", np.where(rows == h, -1.0, 0.0))
    put("add_l", rows < 16)
    put("add_r", rows >= 32)
    put("head_rows", k // 64 == np.arange(2)[None, :])
    return c


def feature_major(v):
    return np.ascontiguousarray(np.asarray(v).T.reshape(KC, P, -1).transpose(1, 0, 2))


def kernel(**inputs):
    import concourse.bacc as bacc
    from concourse.bass_utils import run_bass_kernel_spmd

    a = {k: np.asarray(v) for k, v in inputs.items()}
    arrays = {"params": parameters(a), "consts": constants(), "stream": weight_stream(a),
              "x_in": feature_major(a["x"][0]), "mem_in": feature_major(a["mem"][0]),
              "ctx_in": feature_major(a["ctx_2"][0])}

    def build(counted):
        nc = bacc.Bacc("TRN2", target_bir_lowering=False, num_devices=1)
        ins = {k: nc.dram_tensor(k, v.shape, F32, kind="ExternalInput").ap() for k, v in arrays.items()}
        out = nc.dram_tensor("out", (P, KC, S), F32, kind="ExternalOutput").ap()
        return nc, program(nc, out=out, counted=counted, **ins)

    _, counted = build({})
    _, counted = build(counted)
    nc, _ = build(counted)
    result = run_bass_kernel_spmd(nc, [arrays], core_ids=[0])
    got = result.results[0]["out"]
    return np.ascontiguousarray(got.transpose(1, 0, 2).reshape(D, S).T)[None]
```

```python
from contextlib import ExitStack

import numpy as np
import concourse.bass as bass
from concourse import mybir

F32 = mybir.dt.float32
U32 = mybir.dt.uint32
ALU = mybir.AluOpType
ACT = mybir.ActivationFunctionType
AX = mybir.AxisListType.X

P = 128
D = 1024
KC = D // P
S = 256
T2 = 2 * S
CTX = slice(0, S)
XS = slice(S, T2)
D_FF = 2816
FT = D_FF // P
LAYERS = 2
EPS = 1e-6
ALPHA = (2.0 * LAYERS) ** 0.25
NEG = -1e30
SLOTS = 8
LEVELS = [64, 32, 16, 8, 4, 2, 1]
GLA_TAU = 16.0
CONV = 31
PAD = CONV // 2
ACT_SET_SIGMOID = 2
ACT_SET_LN_EXP = 6
WORKERS = 4


def first_column(layer):
    return 0 if layer < LAYERS - 1 else S


def norm_column(kind, layer):
    return 0 if kind == "ln_mixer" else first_column(layer)


def phases():
    full = KC * P
    out = [("prepare", 0, 1, []), ("forget", 0, 1, []),
           ("fox_first", 0, 1, [full] * 3), ("fox", 0, 7, [full] * 3), ("fox_last", 0, 1, []),
           ("cond", 0, 1, []),
           ("lru_in", 0, 8, [full, full, 2 * P]), ("lru_mix", 0, 1, [full] * 48), ("modulation", 0, 1, []),
           ("stick_first", 0, 1, [full] * 3), ("stick", 0, 7, [full] * 3), ("stick_last", 0, 1, []),
           ("memory_first", 0, 1, [full] * 6), ("memory", 0, 3, [full] * 6), ("memory_last", 0, 1, []),
           ("merge1", 0, 8, [full] * 8), ("out1", 0, 2, [full] * 4),
           ("norm_ffn1", 0, 1, []), ("up1", 0, 11, [full] * 4),
           ("down1", 0, 4, [full, full, 6 * P] * 2)]
    for l in range(LAYERS):
        if l:
            out += [("ada", l, 6, [full] * 8), ("modulation", l, 1, [])]
        out += [("ln_mixer", l, 1, []),
                ("attend_first", l, 1, [full] * 4), ("attend", l, 1, [full] * 6), ("attend_last", l, 1, [full] * 2),
                ("gla", l, 4, [2 * P] + [full] * 6),
                ("conv", l, 8, [full] * 6), ("conv_norm", l, 1, [full] * 8),
                ("merge2", l, 4, [full] * 2), ("out2", l, 2, [full] * 4), ("post_mixer", l, 1, []),
                ("ln_ffn", l, 1, []), ("up2", l, 11, [full] * 4),
                ("down2", l, 4, [full, full, 6 * P] * 2), ("post_ffn", l, 1, [])]
    return out


def column_layout(names_widths):
    at, out = 0, {}
    for name, width in names_widths:
        out[name] = at
        at += width
    return out, at


PARAMS = [("attn_g", KC), ("mem_g", KC), ("wf", KC * 48), ("bf", 1), ("fox_qg", 1), ("fox_kg", 2),
          ("lru_w", 4 * KC), ("lru_b", KC), ("lru_ba", KC), ("lru_bx", KC), ("lru_lam", KC),
          ("mem_qg", 2), ("mem_kg", 2), ("b_gate", 4 * KC), ("ffn_g", KC), ("ffn_w", 3 * FT), ("ffn_b", FT),
          ("cond", 2 * KC)]
for _l in range(LAYERS):
    PARAMS += [(f"b_ada{_l}", 48), (f"qg{_l}", 1), (f"kg{_l}", 1), (f"wglr{_l}", KC * 48), (f"gla_ba{_l}", 8),
               (f"gla_g{_l}", 2), (f"conv_w{_l}", CONV * KC), (f"conv_b{_l}", KC), (f"conv_g{_l}", KC),
               (f"conv_be{_l}", KC), (f"ln1_g{_l}", KC), (f"ln1_b{_l}", KC), (f"ln2_g{_l}", KC), (f"ln2_b{_l}", KC)]
PCOL, N_PARAMS = column_layout(PARAMS)

CONSTS = [("ident", P), ("mean1024", P), ("mean64", P), ("causal_neg", P), ("head_l", 16), ("head_r", 16),
          ("add_l", 1), ("add_r", 1), ("head_rows", 2),
          ("mean128", P), ("mean256", P), ("ones", P), ("suffix", P), ("swap", P), ("strict", 3 * P),
          ("strict_big", 3 * P), ("levels", len(LEVELS) * P), ("twice_ident", P), ("cos", S), ("sin", S),
          ("run_f", T2), ("run_b", T2)]
CCOL, N_CONSTS = column_layout(CONSTS)
EARLY_CONSTS = CCOL["mean128"]


class Tally:

    def __init__(self, nc, ctx, counted):
        self.nc, self.ctx, self.counted = nc, ctx, counted
        self.primed = set(counted.get("primed", {}))
        self.sems, self.seen = {}, {}

    def sem(self, name):
        if name not in self.sems:
            self.sems[name] = self.ctx.enter_context(self.nc.semaphore(name))
        return self.sems[name]


class Step:

    def __init__(self, tally, plan, number, turn):
        self.tally, self.plan, self.number, self.turn = tally, plan, number, turn
        self.made = {}
        self.layer = plan[number][1]

        kind = plan[number][0]
        self.attends = not kind.endswith("_first")
        self.projects = not kind.endswith("_last")
        self.now = plan[number - 1][2] if kind.endswith("_last") else turn
        self.next = 0 if kind.endswith("_first") else turn + 1

    def start(self, name):
        counts = self.tally.counted.get(name, {})
        base = int(name in self.tally.primed) + sum(self.plan[p][2] * n for p, n in counts.items() if p < self.number)
        return self.turn * counts.get(self.number, 0) + base

    def unit(self, name):
        return 16 if name.startswith("loaded") else 1

    def done(self, name, k=0):
        return self.tally.sem(name), (self.start(name) + (k + 1)) * self.unit(name)

    def before(self, name, k=0):
        if self.number == min(self.tally.counted.get(name, {self.number: 0})):
            self.tally.seen.setdefault("primed", {})[name] = 1
        return self.tally.sem(name), (self.start(name) + k) * self.unit(name)

    def earlier(self, name, k):
        counts = self.tally.counted.get(name, {})
        n = int(name in self.tally.primed) + sum(self.plan[p][2] * n for p, n in counts.items() if p < self.number)
        return self.tally.sem(name), max(1, n - k)

    def so_far(self, name):
        return self.tally.sem(name), self.start(name) + self.made.get(name, 0)

    def tick(self, name):
        self.made[name] = self.made.get(name, 0) + 1
        row = self.tally.seen.setdefault(name, {})
        row[self.number] = row.get(self.number, 0) + 1
        return self.tally.sem(name), self.unit(name)


def program(nc, params, consts, stream, x_in, mem_in, ctx_in, out, counted):
    plan = phases()
    with ExitStack() as ctx:
        tally = Tally(nc, ctx, counted)

        def sb(name, *shape):
            return ctx.enter_context(nc.sbuf_tensor(name, [P, *shape], F32))

        X = sb("X", KC, T2)
        H = sb("H", KC, T2)
        YG = sb("YG", 3 * KC * T2)
        MX = sb("MX", KC, T2)
        SQ = sb("SQ", KC, T2)
        WORK = sb("WORK", 6144)
        PR = sb("PR", N_PARAMS)
        CN = sb("CN", N_CONSTS)
        slots = sb("W", SLOTS, KC, P)
        W = [slots[:, u] for u in range(SLOTS)]
        small = sb("small", 64)
        MOD = sb("MOD", 48, 2)
        COND = sb("COND", KC, 2)
        tile_sum = sb("tile_sum", T2)
        lru_c = sb("lru_c", KC)
        bank = [ctx.enter_context(nc.psum_tensor(f"bank{b}", [P, 512], F32)) for b in range(8)]

        Y1 = [YG[:, n * KC * S:(n + 1) * KC * S].rearrange("p (c t) -> p c t", c=KC) for n in range(4)]
        Y2 = [YG[:, n * KC * T2:(n + 1) * KC * T2].rearrange("p (c t) -> p c t", c=KC) for n in range(3)]
        G = YG[:, 0:FT * T2].rearrange("p (c t) -> p c t", c=FT)
        SQF = SQ[:, :, :].rearrange("p c t -> p (c t)")
        MXF = MX[:, :, :].rearrange("p c t -> p (c t)")

        def const(name, width=P, rows=P, at=0):
            return CN[0:rows, CCOL[name] + at:CCOL[name] + at + width]

        def par(name, c=0, rows=P):
            return PR[0:rows, bass.ds(PCOL[name] + c, 1)]

        def work(at, *shape):
            n = int(np.prod(shape))
            v = WORK[:, at:at + n]
            if len(shape) == 2:
                v = v.rearrange("p (a b) -> p a b", a=shape[0])
            return v

        def wide(ap, n):
            return ap.broadcast_to([ap.shape[0], ap.shape[1], n])

        ident = const("ident")

        probs = work(0, 2, 512)
        probs_t = work(1024, 2, 512)
        qn = work(2048, 512)
        kn = work(2560, 512)
        sq2 = work(3072, 2, 512)
        rstd = work(4096, 2, 512)
        vt = work(5120, 4, P)
        kn2 = work(2560, 2, S)
        forget_f = sb("forget_f", S)
        forget_l = sb("forget_l", 2, S)
        forget_r = sb("forget_r", 2, S)
        rowmax = sb("rowmax", 2, 2)
        rowsum = sb("rowsum", 2, 2)
        rowinv = sb("rowinv", 2, 2)

        block = ctx.enter_context(nc.Block())

        def run(engine, bodies, prologue=None, ahead=()):
            for number, (kind, layer, turns, _) in enumerate(plan):
                if number and kind not in ahead:
                    engine.wait_ge(tally.sem("phase_done"), WORKERS * number)
                if kind == "stick_first":
                    engine.wait_ge(tally.sem("late_inputs"), 32)
                if prologue is not None:
                    prologue(kind)
                body = bodies.get(kind.removesuffix("_first").removesuffix("_last"))
                if body is not None:
                    if turns == 1:
                        body(Step(tally, plan, number, 0))
                    else:
                        with engine.Fori(0, turns) as turn:
                            body(Step(tally, plan, number, turn))
                engine.drain().then_inc(tally.sem("phase_done"), 1)


        def soft_max(dve, s, k, logits, segments):
            dve.wait_ge(*s.done("logits", k))
            for j, (o, w) in enumerate(segments):
                mm = dve.tensor_reduce(rowmax[:, k % 2, j:j + 1], logits[:, o:o + w], AX, ALU.max, negate=True)
            mm.then_inc(*s.tick("rowmax"))

        def soft_exp(act, s, k, logits, segments):
            act.wait_ge(*s.done("rowmax", k))
            act.wait_ge(*s.before(f"transposed{k % 2}", k // 2))
            for j, (o, w) in enumerate(segments):
                e = act.activation(probs[:, k % 2, o:o + w], logits[:, o:o + w], ACT.Exp,
                                   bias=rowmax[:, k % 2, j:j + 1], accum_out=rowsum[:, k % 2, j:j + 1])
            e.then_inc(*s.tick("probs"))

        def soft_norm(dve, s, k, segments):
            n = len(segments)
            dve.wait_ge(*s.done("probs", k))
            dve.reciprocal(rowinv[:, k % 2, 0:n], rowsum[:, k % 2, 0:n]).then_inc(*s.tick("dve"))
            dve.wait_ge(*s.so_far("dve"))
            for j, (o, w) in enumerate(segments):
                m = dve.tensor_scalar(probs[:, k % 2, o:o + w], probs[:, k % 2, o:o + w],
                                      rowinv[:, k % 2, j:j + 1], None, ALU.mult)
            m.then_inc(*s.tick("normed"))

        def soft_transpose(pe, s, k, out_bank, moves, taken=None):
            pe.wait_ge(*s.done("normed", k))
            pe.wait_ge(*s.before("probs_t", k if taken is None else taken))
            for o, to in moves:
                m = pe.transpose(out_bank[:, to:to + P], probs[:, k % 2, o:o + P], ident)
            m.then_inc(*s.tick(f"transposed{k % 2}"))

        def soft_take(act, s, k, out_bank, width):
            act.wait_ge(*s.done(f"transposed{k % 2}", k // 2))
            act.wait_ge(*s.before(f"pv{k % 2}", k // 2))
            act.activation(probs_t[:, k % 2, 0:width], out_bank[:, 0:width], ACT.Copy)\
               .then_inc(*s.tick("probs_t"))

        FOX_SEGS = [(0, P), (P, 2 * P)]
        FOX_MOVES = [(0, 0), (P, P), (2 * P, 2 * P)]
        MEM_SEGS = [(0, S), (S, S)]
        MEM_MOVES = [(0, 0), (S, P), (P, 2 * P), (S + P, 3 * P)]
        LAT_SEGS = [(0, T2)]
        LAT_MOVES = [(j * P, j * P) for j in range(4)]

        def attend_units(layer):
            out = []
            for g in range(4):
                if first_column(layer) == 0:
                    out.append((g, "ctx", 0))
                out += [(g, "x", 0), (g, "x", 1)]
            return out

        def attend_projections(s):
            return ([2, 3] if s.attends else []) + (["k", 0, 1, "v"] if s.projects else [])

        def attend_bank(s, f):
            return bank[f % 2] if s.attends else bank[(0, 1, 4, 5)[f]]

        def attend_order(s):
            heads = attend_projections(s)
            if not s.attends:
                out = []
                for f in range(len(heads) + 2):
                    if f < len(heads):
                        out.append(("project", f, 0, 1))
                    if f >= 2 and heads[f - 2] != "v":
                        out.append(("rotate", f - 2, 0, 1))
                    if 1 <= f <= len(heads) and heads[f - 1] != "v":
                        out.append(("variance", f - 1, 0, 1))
                return out
            units = attend_units(s.layer)
            per_head = len(units) // 4
            span = 2 * len(units) - 2 if s.projects else 4 * per_head
            starts = [f * span // len(heads) for f in range(len(heads) + 1)]
            gaps = [[] for _ in range(2 * len(units))]
            for f, head in enumerate(heads):
                parts = starts[f + 1] - starts[f]
                for p in range(parts):
                    gaps[starts[f] + p].append(("project", f, p, parts))
                if head != "v":
                    gaps[starts[f + 1]].append(("variance", f, 0, 1))
                    gaps[starts[f + 1] + 1].append(("rotate", f, 0, 1))
            if not s.projects:
                parts = len(gaps) - (span + 2)
                for p in range(parts):
                    gaps[span + 2 + p].append(("gates", 0, p, parts))
            out = [("logits", 0, 0, 1)]
            for k in range(len(units)):
                if k + 1 < len(units):
                    out.append(("logits", k + 1, 0, 1))
                out.append(("norm", k, 0, 1))
                out += gaps[2 * k]
                out.append(("transpose", k, 0, 1))
                out += gaps[2 * k + 1]
                out.append(("values", k, 0, 1))
            return out

        gq, gk = work(0, T2), work(512, T2)
        gv = work(1024, 4, S)
        cum = work(2048, 2, T2)
        dist = work(3072, 2, T2)
        eq, ek = work(4096, T2), work(4608, T2)
        gr = work(5120, 2, T2)
        mq, mk = SQF[:, 0:T2], SQF[:, 512:1024]
        scores = SQF[:, 1024:1536].rearrange("p (c t) -> p c t", c=4)
        qdecay = SQF[:, 1536:2560].rearrange("p (d t) -> p d t", d=2)
        kw = SQF[:, 2560:3584].rearrange("p (d t) -> p d t", d=2)
        glr = SQF[:, 3584:4096]
        kwt = MXF[:, 0:1024].rearrange("p (d c t) -> p d c t", d=2, c=4)
        states = MXF[:, 1024:3072].rearrange("p (d c e) -> p d c e", d=2, c=4)
        decay = MXF[:, 3072:3080].rearrange("p (d c) -> p d c", d=2)
        gtmp = MXF[:, 3584:4096]
        gtmp2 = MXF[:, 0:512]
        orderf, orderb = [0, 1, 2, 3], [1, 0, 3, 2]

        def halves(ap, m):
            return ap.rearrange("p (n h m) -> p n h m", h=2, m=m)

        padded = work(0, 2, S + 2 * PAD)
        conv_sg = work(1024, T2)
        sg2 = work(1536, 2, T2)
        sg_conv = work(1024, KC, T2)
        ada_rows = YG[0:2, 6144:12288]

        mem_v = SQF[:, 0:512].rearrange("p (t e) -> p t e", t=2)
        att_n = SQF[:, 0:512]
        att_t = SQF[:, 512:768]
        att_ks = [SQF[:, 1024:1536], work(2048, T2)]
        att_vs = [vt, work(2560, 4, P)]
        att_q = SQF[:, 1536:3584].rearrange("p (g t) -> p g t", g=4)
        sg = WORK[:, 0:4 * T2].rearrange("p (n t) -> p n t", n=4)
        lru_x = SQF[:, 0:KC * S]
        lru_r = SQF[:, KC * S:2 * KC * S]
        lru_i = MXF[:, 0:KC * S]
        lru_g = MXF[:, KC * S:2 * KC * S]

        up_s = work(0, 2, T2)
        up_c = work(1024, 2, T2)
        small_f = work(0, 2, S)

        @block.sync
        def _(sp):
            sp.dma_start(X[:, :, XS], x_in).then_inc(tally.sem("inputs"), 16)
            sp.dma_start(MX[:, :, CTX], mem_in).then_inc(tally.sem("inputs"), 16)
            sp.dma_start(CN[:, 0:EARLY_CONSTS], consts[:, 0:EARLY_CONSTS]).then_inc(tally.sem("inputs"), 16)
            sp.dma_start(PR[:, :], params).then_inc(tally.sem("inputs"), 16)
            first, last_use = 0, [0] * SLOTS
            for number, (kind, layer, turns, widths) in enumerate(plan):
                n = len(widths)
                if not n:
                    continue
                s = Step(tally, plan, number, 0)
                for u, w in enumerate(widths):
                    slot = u % SLOTS
                    if last_use[slot]:
                        sp.wait_ge(tally.sem("unit"), last_use[slot])
                    sp.dma_start(W[slot][:, 0:w // P, :], stream[first + u, :, 0:w]
                                 .rearrange("p (c m) -> p c m", m=P)).then_inc(*s.tick(f"loaded{slot}"))
                    last_use[slot] = first + u + 1
                if kind == "fox":
                    sp.dma_start(X[:, :, CTX], ctx_in).then_inc(tally.sem("late_inputs"), 16)
                    sp.dma_start(CN[:, EARLY_CONSTS:N_CONSTS], consts[:, EARLY_CONSTS:N_CONSTS])\
                      .then_inc(tally.sem("late_inputs"), 16)
                if turns > 1:
                    with sp.Fori(1, turns) as turn:
                        for u, w in enumerate(widths):
                            sp.wait_ge(tally.sem("unit"), turn * n + (first - n + u + 1))
                            sp.dma_start(W[u][:, 0:w // P, :], stream[turn * n + (first + u), :, 0:w]
                                         .rearrange("p (c m) -> p c m", m=P)).then_inc(tally.sem(f"loaded{u}"), 16)
                    for u in range(n):
                        last_use[u] = first + (turns - 1) * n + u + 1
                first += turns * n
            sp.wait_ge(tally.sem("phase_done"), WORKERS * len(plan))
            sp.dma_start(out, X[:, :, XS]).then_inc(tally.sem("stored"), 16)
            sp.wait_ge(tally.sem("stored"), 16)

        @block.tensor
        def _(pe):
            def project(s, u, out_ap, cols, src=H, k=KC, first=True, last=True, tick=True):
                pe.wait_ge(*s.done(f"loaded{u}"))
                for c in range(k):
                    m = pe.matmul(out_ap, W[u][:, c, :], src[:, c, cols], start=first and c == 0,
                                  stop=last and c == k - 1)
                if tick:
                    m.then_inc(*s.tick("unit"))
                return m

            def project_tokens(s, u, outs, col0, tick=True):
                pe.wait_ge(*s.done(f"loaded{u}"))
                for t, o in enumerate(outs):
                    for c in range(KC):
                        m = pe.matmul(o, H[:, c, col0 + t * P:col0 + (t + 1) * P], W[u][:, c, :],
                                      start=c == 0, stop=c == KC - 1)
                if tick:
                    m.then_inc(*s.tick("unit"))
                return m

            def mean_square(s, out_ap, cols, name):
                for c in range(KC):
                    pe.wait_ge(*s.done("squared", c))
                    m = pe.matmul(out_ap, const("mean1024"), SQ[:, c, cols], start=c == 0, stop=c == KC - 1)
                m.then_inc(*s.tick(name))

            def prepare(s):
                pe.wait_ge(tally.sem("inputs"), 64)
                mean_square(s, bank[0][:, :], slice(0, T2), "variance")

            def forget(s):
                wf = PR[:, PCOL["wf"]:PCOL["wf"] + KC * 48].rearrange("p (c m) -> p c m", c=KC)
                for c in range(KC):
                    m = pe.matmul(bank[7][0:48, 0:S], wf[:, c, :], H[:, c, XS], start=c == 0, stop=c == KC - 1)
                m.then_inc(*s.tick("forget_logits"))

            def pv_pair(s, k, values, weights):
                pe.wait_ge(*s.before(f"taken_out{k}"))
                o = bank[7][64 * k:64 * k + 64, 0:S]
                pe.matmul(o, values[:, 0, 64 * k:64 * k + 64], weights[:, 0:S], start=True, stop=False)
                pe.matmul(o[:, P:S], values[:, 1, 64 * k:64 * k + 64], weights[:, S:3 * P],
                          start=False, stop=True).then_inc(*s.tick(f"pv{k % 2}"))

            def project_pair(s, u):
                if not s.projects:
                    return
                pe.wait_ge(*s.before(("q_taken", "k_taken", "v_taken")[u]))
                if u < 2:
                    project(s, u, bank[u][:, 0:S], XS)
                else:
                    project_tokens(s, 2, [bank[2][:, t * P:(t + 1) * P] for t in range(2)], S)

            def fox(s):
                if s.attends:
                    pe.wait_ge(*s.before("k_taken"))
                    pe.wait_ge(*s.before("probs"))
                    pe.wait_ge(*s.before("probs_t"))
                    for k in range(2):
                        b = bank[4 + k]
                        for (o, w), q in zip(FOX_SEGS, range(2)):
                            qs = slice(q * P, (q + 1) * P)
                            pe.matmul(b[:, o:o + w], qn[:, qs], kn2[:, k, 0:w], start=True, stop=False)
                            pe.matmul(b[:, o:o + w], forget_l[0:48, k, qs], forget_r[0:48, k, 0:w],
                                      start=False, stop=False)
                            m = pe.matmul(b[:, o + w - P:o + w], ident, const("causal_neg"), start=False, stop=True)
                        m.then_inc(*s.tick("logits"))
                project_pair(s, 0)
                project_pair(s, 1)
                if s.attends:
                    soft_transpose(pe, s, 0, bank[6], FOX_MOVES, 0)
                    soft_transpose(pe, s, 1, bank[5], FOX_MOVES, 0)
                if s.projects:
                    pe.wait_ge(*s.before("rstd"))
                    for j in range(2):
                        pe.wait_ge(*s.done("qk_squared", j))
                        m = pe.matmul(bank[3][:, j * S:(j + 1) * S], const("mean64"), sq2[:, j, 0:S],
                                      start=True, stop=True)
                    m.then_inc(*s.tick("variance"))
                project_pair(s, 2)
                if s.attends:
                    pe.wait_ge(*s.before("v_taken"))
                    for k in range(2):
                        pe.wait_ge(*s.done("probs_t", k))
                        pv_pair(s, k, vt, probs_t[:, k, :])

            def lru_in(s):
                pe.wait_ge(*s.before("conv_done"))
                project(s, 0, bank[0][:, 0:S], XS)
                pe.wait_ge(*s.before("gate_taken"))
                project(s, 1, bank[1][:, 0:S], XS)
                pe.wait_ge(*s.done("loaded2"))
                pe.wait_ge(*s.done("conv_done"))
                pe.wait_ge(*s.before("ri_taken"))
                xc = SQF[:, bass.ds(s.turn * S, S)]
                pe.matmul(bank[2][:, 0:S], W[2][:, 0, :], xc, start=True, stop=True)
                pe.matmul(bank[3][:, 0:S], W[2][:, 1, :], xc, start=True, stop=True).then_inc(*s.tick("unit"))

            def stick(s):
                if s.attends:
                    pe.wait_ge(*s.before("q_taken"))
                    pe.wait_ge(*s.before("k_taken"))
                    pe.wait_ge(*s.before("log_beta"))
                    for k in range(2):
                        pe.matmul(bank[4 + k][:, 0:S], kn2[:, k, 0:P], qn[:, 0:S], start=True, stop=True)
                        pe.matmul(bank[4 + k][:, S:3 * P], kn2[:, k, P:S], qn[:, P:S], start=True, stop=True)\
                          .then_inc(*s.tick("logits"))
                for k in range(2):
                    project_pair(s, k)
                    if s.attends:
                        b = bank[3 if k == 0 else 6]
                        sp_k = sq2[:, k, :]
                        pe.wait_ge(*s.before(f"minus_suffix{k}"))
                        pe.wait_ge(*s.done("softplus", k))
                        pe.matmul(b[:, 0:3 * P], const("suffix"), sp_k[:, 0:3 * P], start=True, stop=False)
                        pe.matmul(b[:, P:S], const("ones"), sp_k[:, S:3 * P], start=False, stop=False)
                        pe.matmul(b[:, 0:3 * P], ident, const("strict_big", 3 * P), start=False, stop=True)\
                          .then_inc(*s.tick("suffix"))
                project_pair(s, 2)
                if s.attends:
                    pe.wait_ge(*s.before("v_taken"))
                    for k in range(2):
                        pe.wait_ge(*s.done("weights", k))
                        pv_pair(s, k, vt, probs[:, k, :])

            def memory(s):
                if s.attends:
                    pe.wait_ge(*s.before("q_taken"))
                    pe.wait_ge(*s.before("probs"))
                    for q in range(2):
                        for u in range(2):
                            m = pe.matmul(bank[4][:, q * S:(q + 1) * S], qn[:, u * S + q * P:u * S + (q + 1) * P],
                                          kn[:, u * S:(u + 1) * S], start=u == 0, stop=u == 1)
                    m.then_inc(*s.tick("logits"))
                if s.projects:
                    pe.wait_ge(*s.before("k_taken"))
                    for u in range(2):
                        project(s, u, bank[0][:, u * S:(u + 1) * S], CTX)
                if s.attends:
                    soft_transpose(pe, s, 0, bank[6], MEM_MOVES)
                if s.projects:
                    pe.wait_ge(*s.before("q_taken"))
                    for u in range(2):
                        project(s, 2 + u, bank[1][:, u * S:(u + 1) * S], XS)
                if s.attends:
                    pe.wait_ge(*s.done("probs_t"))
                    pe.wait_ge(*s.before("v_taken"))
                    pe.wait_ge(*s.before("taken_out0"))
                    for e in range(2):
                        for j in range(2):
                            m = pe.matmul(bank[7][:, e * S:(e + 1) * S], mem_v[:, j, e * P:(e + 1) * P],
                                          probs_t[:, 0, j * S:(j + 1) * S], start=j == 0, stop=j == 1)
                    m.then_inc(*s.tick("pv0"))
                if s.projects:
                    pe.wait_ge(*s.before("rstd"))
                    for j in range(2):
                        pe.wait_ge(*s.done("qk_squared", j))
                        for u in range(2):
                            m = pe.matmul(bank[3][:, j * S:(j + 1) * S], const("mean256"),
                                          sq2[:, j, u * S:(u + 1) * S], start=u == 0, stop=u == 1)
                    m.then_inc(*s.tick("variance"))
                    pe.wait_ge(*s.before("v_taken"))
                    for u in range(2):
                        project_tokens(s, 4 + u, [bank[2][:, t * S + u * P:t * S + (u + 1) * P] for t in range(2)], 0)

            def merge(s, branches, cols, count):
                for n in range(count):
                    pe.wait_ge(*s.before(f"gate{n}"))
                    project(s, 2 * n, bank[2 * n][:, 0:T2 - cols.start], cols)
                    pe.wait_ge(*s.before(f"mixed{n}"))
                    project(s, 2 * n + 1, bank[2 * n + 1][:, 0:T2 - cols.start], branches[n][1], src=branches[n][0])

            def merge1(s):
                merge(s, [(y, slice(0, S)) for y in Y1], XS, 4)

            def merge2(s):
                cols = slice(first_column(s.layer), T2)
                for j in range(2):
                    pe.wait_ge(*s.before(f"mixed{j}"))
                    project(s, j, bank[j][:, 0:T2 - cols.start], cols, src=Y2[2])

            def out_tiles(s):
                cols = slice(S if s.plan[s.number][0] == "out1" else first_column(s.layer), T2)
                for u in range(4):
                    pe.wait_ge(*s.before(f"added{u}"))
                    project(s, u, bank[u][:, 0:T2 - cols.start], cols, src=MX)

            def up(s):
                cols = slice(S if s.plan[s.number][0] == "up1" else first_column(s.layer), T2)
                for j in range(2):
                    pe.wait_ge(*s.before(f"hidden{j}"))
                    for u in range(2):
                        if j == 0 and u == 0:
                            pe.wait_ge(*s.done("loaded0"))
                            for c in range(KC):
                                if s.plan[s.number][0] == "up2":
                                    normalised(s, c, cols.start)
                                else:
                                    pe.wait_ge(*s.earlier("ffn_normed", KC - 1 - c))
                                m = pe.matmul(bank[0][:, 0:T2 - cols.start], W[0][:, c, :], H[:, c, cols],
                                              start=c == 0, stop=c == KC - 1)
                            m.then_inc(*s.tick("unit"))
                        else:
                            project(s, 2 * j + u, bank[2 * j + u][:, 0:T2 - cols.start], cols)

            def down(s):
                c0 = S if s.plan[s.number][0] == "down1" else first_column(s.layer)
                cols = slice(0, S) if s.plan[s.number][0] == "down1" else slice(c0, T2)
                for j in range(2):
                    pe.wait_ge(*s.before(f"added{j}"))
                    for q in range(3):
                        u = 3 * j + q
                        project(s, u, bank[j][:, 0:T2 - c0], cols, src=G[:, 8 * q:min(8 * q + 8, FT), :],
                                k=min(8, FT - 8 * q), first=q == 0, last=q == 2)

            def norm_ffn1(s):
                mean_square(s, bank[0][:, 0:S], XS, "variance")

            def ada_rows_ahead(s):
                for r in range(12):
                    if r >= 8:
                        pe.wait_ge(*s.done("row", r - 8))
                    for q in range(4):
                        u = 4 * r + q
                        pe.wait_ge(*s.done(f"loaded{u % SLOTS}", u // SLOTS))
                        w = W[u % SLOTS].rearrange("p c m -> p (c m)").rearrange("p (c m) -> p c m", c=2)
                        for c in range(2):
                            m = pe.matmul(bank[r % 8][0:2, :], COND[:, 2 * q + c, :], w[:, c, :],
                                          start=q == 0 and c == 0, stop=q == 3 and c == 1)
                        m.then_inc(*s.tick("unit"))

            def ada(s):
                pe.wait_ge(*s.earlier("affine", KC - 1))
                for j in range(2):
                    pe.wait_ge(*s.before(f"row{j}"))
                    for q in range(4):
                        u = 4 * j + q
                        pe.wait_ge(*s.done(f"loaded{u}"))
                        w = W[u].rearrange("p c m -> p (c m)").rearrange("p (c m) -> p c m", c=2)
                        for c in range(2):
                            m = pe.matmul(bank[j][0:2, :], COND[:, 2 * q + c, :], w[:, c, :],
                                          start=q == 0 and c == 0, stop=q == 3 and c == 1)
                        m.then_inc(*s.tick("unit"))

            def modulation(s):
                for j in range(48):
                    m = pe.transpose(bank[0][:, 2 * j:2 * j + 2], ada_rows[:, j * P:(j + 1) * P], ident[0:2, 0:2])
                m.then_inc(*s.tick("mod_columns"))

            def normalised(s, c, c0):
                pe.wait_ge(*s.earlier("affine", (KC - 1 - c) * (2 if c0 == 0 else 1)))

            def layernorm(s):
                c0 = norm_column(s.plan[s.number][0], s.layer)
                kind = s.plan[s.number][0]
                if kind in ("conv_norm", "post_mixer", "post_ffn"):
                    m = pe.matmul(bank[0][:, 0:T2 - c0], const("mean1024"), tile_sum[:, c0:T2], start=True, stop=True)
                else:
                    for c in range(KC):
                        if kind == "ln_ffn":
                            normalised(s, c, c0)
                        m = pe.matmul(bank[0][:, 0:T2 - c0], const("mean1024"), X[:, c, c0:T2],
                                      start=c == 0, stop=c == KC - 1)
                m.then_inc(*s.tick("mean"))
                first_gates = 3 if c0 == 0 else 5
                if s.plan[s.number][0] == "conv_norm":
                    for c in range(first_gates):
                        project(s, c, bank[2 + c][:, 0:T2 - c0], slice(c0, T2))
                mean_square(s, bank[1][:, 0:T2 - c0], slice(c0, T2), "variance")
                if s.plan[s.number][0] == "conv_norm":
                    for c in range(first_gates, KC):
                        if c >= 6:
                            pe.wait_ge(*s.done("gate_conv", c - 6))
                        project(s, c, bank[2 + c % 6][:, 0:T2 - c0], slice(c0, T2))

            def attend(s):
                c0 = first_column(s.layer)
                heads, units = attend_projections(s), attend_units(s.layer)
                normed = [f for f, head in enumerate(heads) if head != "v"]
                for stage, i, part, parts in attend_order(s):
                    if stage == "project":
                        out_bank, total = attend_bank(s, i), 4 * KC if heads[i] == "v" else KC
                        if part == 0:
                            pe.wait_ge(*s.done(f"loaded{i}"))
                            if s.attends and i >= 2:
                                pe.wait_ge(*s.done("head_taken", normed.index(i - 2)))
                        for j in range(part * total // parts, (part + 1) * total // parts):
                            t, c = j // KC, j % KC
                            if not s.attends and i == 0:
                                normalised(s, c, 0)
                            if heads[i] == "v":
                                m = pe.matmul(out_bank[:, t * P:(t + 1) * P], H[:, c, t * P:(t + 1) * P],
                                              W[i][:, c, :], start=c == 0, stop=c == KC - 1)
                            else:
                                cols = slice(0 if heads[i] == "k" else c0, T2)
                                m = pe.matmul(out_bank[:, 0:T2 - cols.start], W[i][:, c, :], H[:, c, cols],
                                              start=c == 0, stop=c == KC - 1)
                        if part == parts - 1:
                            m.then_inc(*s.tick("unit"))
                    elif stage == "variance":
                        n = T2 if heads[i] == "k" else T2 - c0
                        pe.wait_ge(*s.done("head_squared", normed.index(i)))
                        pe.wait_ge(*s.before("head_rstd", normed.index(i)))
                        pe.matmul(bank[2][:, 0:n], const("mean128"), sq2[:, 0, 0:n], start=True, stop=True)\
                          .then_inc(*s.tick("variance"))
                    elif stage == "rotate":
                        n = T2 if heads[i] == "k" else T2 - c0
                        pe.wait_ge(*s.done("head_taken", normed.index(i)))
                        pe.wait_ge(*s.before("rotated", normed.index(i)))
                        pe.matmul(bank[3][:, 0:S], const("swap"), att_n[:, n - S:n], start=True, stop=True)\
                          .then_inc(*s.tick("swapped"))
                    elif stage == "gates":
                        wg = PR[:, PCOL[f"wglr{s.layer}"]:PCOL[f"wglr{s.layer}"] + KC * 48]\
                            .rearrange("p (c m) -> p c m", c=KC)
                        if part == 0:
                            pe.wait_ge(*s.done("head_taken", 0))
                        for c in range(part * KC // parts, (part + 1) * KC // parts):
                            m = pe.matmul(bank[0][0:48, :], wg[:, c, :], H[:, c, :], start=c == 0, stop=c == KC - 1)
                        if part == parts - 1:
                            m.then_inc(*s.tick("glr"))
                    elif stage == "logits":
                        g, kind, q = units[i]
                        b, keys = bank[4 + i % 2], att_ks[s.now % 2]
                        if i >= 2:
                            pe.wait_ge(*s.done("probs", i - 2))
                        if g >= 2:
                            pe.wait_ge(*s.done("rotated", g - 2))
                        if kind == "x":
                            m = pe.matmul(b[:, :], att_q[:, g, S + q * P:S + (q + 1) * P], keys, start=True, stop=True)
                        else:
                            for j in range(2):
                                m = pe.matmul(b[:, j * S:(j + 1) * S], att_q[:, g, j * P:(j + 1) * P], keys[:, CTX],
                                              start=True, stop=True)
                        m.then_inc(*s.tick("logits"))
                    elif stage == "transpose":
                        soft_transpose(pe, s, i, bank[6], LAT_MOVES if units[i][1] == "x" else MEM_MOVES)
                    elif stage == "values":
                        values = att_vs[s.now % 2]
                        pe.wait_ge(*s.done("probs_t", i))
                        pe.wait_ge(*s.before("taken_out", i))
                        if units[i][1] == "x":
                            for j in range(4):
                                m = pe.matmul(bank[7][:, 0:P], values[:, j, :], probs_t[:, i % 2, j * P:(j + 1) * P],
                                              start=j == 0, stop=j == 3)
                        else:
                            for j in range(2):
                                m = pe.matmul(bank[7][:, 0:S], values[:, j, :], probs_t[:, i % 2, j * S:(j + 1) * S],
                                              start=j == 0, stop=j == 1)
                        m.then_inc(*s.tick(f"pv{i % 2}"))

            def gla(s):
                c0 = first_column(s.layer)
                n = T2 - c0
                active = range(c0 // P, 4)
                pe.wait_ge(*s.done("loaded0"))
                pe.wait_ge(*s.before("state1"))
                for d in range(2):
                    m = pe.matmul(bank[4 + d][:, :], W[0][0:48, d, :], glr[0:48, :], start=True, stop=True)
                m.then_inc(*s.tick("unit"))
                pe.wait_ge(*s.before("scored"))
                project(s, 1, bank[1][:, :], slice(0, T2))
                pe.wait_ge(*s.before("gla_rstd"))
                project(s, 2, bank[0][:, 0:n], slice(c0, T2))

                def value_half(t, half):
                    if t == 0 and half == 0:
                        pe.wait_ge(*s.before("v_taken"))
                        pe.wait_ge(*s.done("loaded3"))
                        pe.wait_ge(*s.done("loaded4"))
                    o = bank[2 + t // 2][:, (t % 2) * S:(t % 2 + 1) * S].rearrange("p (u e) -> p u e", u=2)
                    for c in range(4 * half, 4 * half + 4):
                        m = pe.matmul(o, H[:, c, t * P:(t + 1) * P], slots[:, 3:5, c, :], start=c == 0,
                                      stop=c == KC - 1)
                    if t == 3 and half:
                        m.then_inc(*s.tick("unit"))

                def gate_half(u, half):
                    if u == 0 and half == 0:
                        pe.wait_ge(*s.before("gla_end"))
                    if half == 0:
                        pe.wait_ge(*s.done(f"loaded{5 + u}"))
                    for c in range(4 * half, 4 * half + 4):
                        m = pe.matmul(bank[6 + u][:, 0:n], W[5 + u][:, c, :], H[:, c, c0:T2], start=c == 0,
                                      stop=c == KC - 1)
                    if half:
                        m.then_inc(*s.tick("unit"))

                def transpose_keys():
                    pe.wait_ge(*s.done("decayed"))
                    for d, order in enumerate((orderf, orderb)):
                        for c in order[:3]:
                            m = pe.transpose(bank[4 + d][:, c * P:(c + 1) * P], kw[:, d, c * P:(c + 1) * P], ident)
                            if d == 0 and c == order[0]:
                                m.then_inc(*s.tick("unit"))
                    m.then_inc(*s.tick("kw_transposed"))

                def update(j):
                    if j == 0:
                        pe.wait_ge(*s.done("kw_taken"))
                        pe.wait_ge(*s.done("v_taken"))
                    for d, order in enumerate((orderf, orderb)):
                        if j:
                            pe.wait_ge(*s.done(f"state{d}", j - 1))
                        pe.matmul(bank[4 + d][:, 0:S], kwt[:, d, order[j], :], gv[:, order[j], :],
                                  start=True, stop=True).then_inc(*s.tick(f"update{d}"))

                between = [lambda: value_half(0, 0), lambda: [value_half(0, 1), value_half(1, 0)],
                           lambda: [value_half(1, 1), value_half(2, 0)],
                           lambda: [value_half(2, 1), value_half(3, 0)],
                           lambda: [value_half(3, 1), transpose_keys()],
                           lambda: gate_half(0, 0), lambda: [gate_half(0, 1), update(0)],
                           lambda: [gate_half(1, 0), update(1)]]
                pe.wait_ge(*s.done("q_taken"))
                pe.wait_ge(*s.done("k_taken"))
                for lv in range(len(LEVELS) + 1):
                    b = bank[lv % 2]
                    if lv >= 2:
                        pe.wait_ge(*s.done("scored", lv - 2))
                    if lv:
                        pe.wait_ge(*s.done("level", lv - 1))
                    for c in active:
                        cs = slice(c * P, (c + 1) * P)
                        m = pe.matmul(b[:, cs], (mk if lv else gk)[:, cs], (mq if lv else gq)[:, cs],
                                      start=True, stop=True)
                    m.then_inc(*s.tick("level_scores"))
                    between[lv]()
                gate_half(1, 1)
                update(2)
                pe.wait_ge(*s.done("state0", 2))
                pe.wait_ge(*s.done("state1", 2))
                pe.wait_ge(*s.done("scored", len(LEVELS)))
                for e in range(2):
                    pe.wait_ge(*s.done("r_taken", e))
                    es = slice(e * P, (e + 1) * P)
                    for c in active:
                        o = bank[6 + e][:, c * P - c0:(c + 1) * P - c0]
                        cs = slice(c * P, (c + 1) * P)
                        m = pe.matmul(o, gv[:, c, es], scores[:, c, :], start=True, stop=False)
                        if c != orderf[0]:
                            m = pe.matmul(o, states[:, 0, c, es], qdecay[:, 0, cs], start=False, stop=c == orderb[0])
                        if c != orderb[0]:
                            m = pe.matmul(o, states[:, 1, c, es], qdecay[:, 1, cs], start=False, stop=True)
                m.then_inc(*s.tick("gla_out"))
                for e in range(2):
                    pe.wait_ge(*s.done("gla_squared", e))
                    m = pe.matmul(bank[0][:, 0:n], const("mean256"), dist[:, e, 0:n], start=e == 0, stop=e == 1)
                m.then_inc(*s.tick("variance"))

            def conv(s):
                cols = slice(first_column(s.layer), T2)
                n = T2 - cols.start
                pe.wait_ge(*s.before("glu"))
                for u in range(2):
                    project(s, u, bank[u][:, 0:n], cols)
                for b in range(2):
                    pe.wait_ge(*s.before(f"gate{b}"))
                    project(s, 2 + 2 * b, bank[2 + 2 * b][:, 0:n], cols)
                    pe.wait_ge(*s.before(f"mixed{b}"))
                    project(s, 3 + 2 * b, bank[3 + 2 * b][:, 0:n], cols, src=Y2[b])

            run(pe, {"prepare": prepare, "forget": forget, "fox": fox, "lru_in": lru_in,
                     "lru_mix": ada_rows_ahead, "stick": stick,
                     "memory": memory, "merge1": merge1, "out1": out_tiles, "norm_ffn1": norm_ffn1, "up1": up,
                     "down1": down, "ada": ada, "modulation": modulation, "ln_mixer": layernorm, "attend": attend,
                     "gla": gla, "conv": conv, "conv_norm": layernorm, "merge2": merge2,
                     "out2": out_tiles,
                     "post_mixer": layernorm, "ln_ffn": layernorm, "up2": up, "down2": down, "post_ffn": layernorm},
                ahead=("fox_first", "attend_first", "up1", "ln_ffn", "up2", "ada"))

        @block.scalar
        def _(act):
            def tables(which):
                act.add_instruction(mybir.InstLoadActFuncSet(
                    act_func_set_id=which, name=nc.get_next_instruction_name(),
                    engine=mybir.EngineType.Activation, ins=[], outs=[]))

            def fence(s):
                act.wait_ge(*s.so_far("act"))

            def rsqrt(s, out_ap, mean_ap, tmp, factor=1.0, name="rstd", eps=EPS):
                act.activation(tmp, mean_ap, ACT.Ln, bias=eps).then_inc(*s.tick("act"))
                fence(s)
                act.activation(out_ap, tmp, ACT.Exp, scale=-0.5, bias=float(np.log(factor)))\
                   .then_inc(*s.tick(name))

            def prepare(s):
                act.wait_ge(*s.done("variance"))
                rsqrt(s, work(1024, T2), bank[0][:, :], work(1536, T2))

            def forget(s):
                act.wait_ge(*s.done("forget_logits"))
                y, e = small_f[0:48, 0, :], small_f[0:48, 1, :]
                act.activation(y, bank[7][0:48, 0:S], ACT.Identity, bias=par("bf", 0, 48)).then_inc(*s.tick("act"))
                fence(s)
                act.activation(e, y, ACT.Abs).then_inc(*s.tick("act"))
                fence(s)
                act.activation(e, e, ACT.Exp, scale=-1.0).then_inc(*s.tick("act"))
                fence(s)
                act.activation(e, e, ACT.Ln, bias=1.0).then_inc(*s.tick("forget_ln"))
                lam = PR[:, PCOL["lru_lam"]:PCOL["lru_lam"] + KC]
                act.activation(small[:, 0:KC], lam, ACT.Abs).then_inc(*s.tick("act"))
                fence(s)
                act.activation(small[:, 0:KC], small[:, 0:KC], ACT.Exp, scale=-1.0).then_inc(*s.tick("lam_exp"))

            def square_pair(s, j, unit_event, width):
                act.wait_ge(*s.done("unit", unit_event))
                if j == 0:
                    act.wait_ge(*s.before("variance"))
                act.activation(sq2[:, j, 0:width], bank[j][:, 0:width], ACT.Square).then_inc(*s.tick("qk_squared"))

            def rstd_pair(s, factors, readers):
                act.wait_ge(*s.done("variance"))
                act.wait_ge(*s.before(readers))
                act.activation(rstd[:, 1, :], bank[3][:, :], ACT.Ln, bias=EPS).then_inc(*s.tick("act"))
                fence(s)
                for j, factor in enumerate(factors):
                    e = act.activation(rstd[:, 0, j * S:(j + 1) * S], rstd[:, 1, j * S:(j + 1) * S], ACT.Exp,
                                       scale=-0.5, bias=float(np.log(factor)))
                e.then_inc(*s.tick("rstd"))

            def take_values(s):
                act.wait_ge(*s.done("unit", 2))
                if s.attends:
                    act.wait_ge(*s.done("pv0"))
                    act.wait_ge(*s.done("pv1"))
                act.activation(vt[:, 0:2, :], bank[2][:, 0:S].rearrange("p (t d) -> p t d", t=2), ACT.Copy)\
                   .then_inc(*s.tick("v_taken"))

            def fox(s):
                if s.attends:
                    soft_exp(act, s, 0, bank[4], FOX_SEGS)
                    soft_exp(act, s, 1, bank[5], FOX_SEGS)
                if s.projects:
                    for j in range(2):
                        square_pair(s, j, j, S)
                if s.attends:
                    soft_take(act, s, 0, bank[6], 3 * P)
                    soft_take(act, s, 1, bank[5], 3 * P)
                if s.projects:
                    rstd_pair(s, (64 ** -0.5, 1.0), "k_taken")
                    take_values(s)

            def lru_in(s):
                i = s.turn
                act.wait_ge(*s.done("unit", 1))
                act.activation(lru_g[:, bass.ds(i * S, S)], bank[1][:, 0:S], ACT.Copy).then_inc(*s.tick("gate_taken"))
                act.wait_ge(*s.done("unit", 2))
                act.activation(lru_r[:, bass.ds(i * S, S)], bank[2][:, 0:S], ACT.Sigmoid, bias=par("lru_ba", i))
                act.activation(lru_i[:, bass.ds(i * S, S)], bank[3][:, 0:S], ACT.Sigmoid, bias=par("lru_bx", i))\
                   .then_inc(*s.tick("ri_taken"))

            def lru_mix(s):
                t1, t2 = work(0, KC * S), work(KC * S, KC * S)
                act.wait_ge(*s.done("log_a"))
                act.activation(t1, lru_r, ACT.Tanh).then_inc(*s.tick("tanh_a"))
                act.wait_ge(*s.done("gelu_in"))
                act.activation(t2, t2, ACT.Tanh, scale=float(np.sqrt(2 / np.pi))).then_inc(*s.tick("gelu_tanh"))
                tables(ACT_SET_LN_EXP)
                act.wait_ge(*s.done("one_minus_a2"))
                act.activation(t1, t1, ACT.Ln).then_inc(*s.tick("act"))
                fence(s)
                act.activation(t1, t1, ACT.Exp, scale=0.5).then_inc(*s.tick("root"))
                act.activation(lru_r, lru_r, ACT.Exp).then_inc(*s.tick("a"))
                for r in range(12):
                    act.wait_ge(*s.done("unit", 4 * r + 3))
                    act.activation(ada_rows[:, r * 512:(r + 1) * 512], bank[r % 8][0:2, :], ACT.Copy)\
                       .then_inc(*s.tick("row"))

            def stick(s):
                if s.attends:
                    for k in range(2):
                        z, e = rstd[:, k, 0:3 * P], sq2[:, k, 0:3 * P]
                        act.wait_ge(*s.done("logits", k))
                        act.wait_ge(*s.before(f"minus_suffix{k}"))
                        act.activation(z, bank[4 + k][:, 0:3 * P], ACT.Copy).then_inc(*s.tick("act"))
                        act.wait_ge(*s.before("suffix", k))
                        act.activation(e, bank[4 + k][:, 0:3 * P], ACT.Abs).then_inc(*s.tick("log_beta"))
                        act.wait_ge(*s.so_far("log_beta"))
                        act.activation(e, e, ACT.Exp, scale=-1.0).then_inc(*s.tick("act"))
                        fence(s)
                        act.activation(e, e, ACT.Ln, bias=1.0).then_inc(*s.tick("log1p"))
                if s.projects:
                    act.wait_ge(*s.done("unit", 0))
                    if s.attends:
                        act.wait_ge(*s.done("logits", 1))
                    act.activation(qn[:, 0:S], bank[0][:, 0:S], ACT.Copy, scale=64 ** -0.5)\
                       .then_inc(*s.tick("q_taken"))
                if s.attends:
                    for k in range(2):
                        act.wait_ge(*s.done(f"minus_suffix{k}"))
                        act.activation(probs[:, k, 0:3 * P], probs[:, k, 0:3 * P], ACT.Exp)\
                           .then_inc(*s.tick("weights"))
                if s.projects:
                    take_values(s)

            def memory(s):
                if s.attends:
                    soft_exp(act, s, 0, bank[4], MEM_SEGS)
                if s.projects:
                    square_pair(s, 0, 1, T2)
                if s.attends:
                    soft_take(act, s, 0, bank[6], T2)
                if s.projects:
                    square_pair(s, 1, 3, T2)
                    rstd_pair(s, (1.0, 256 ** -0.5), "q_taken")
                    act.wait_ge(*s.done("unit", 5))
                    if s.attends:
                        act.wait_ge(*s.done("pv0"))
                    act.activation(mem_v, bank[2][:, :].rearrange("p (t e) -> p t e", t=2), ACT.Copy)\
                       .then_inc(*s.tick("v_taken"))

            def merge(s, count, width, bias):
                for n in range(count):
                    act.wait_ge(*s.done("unit", 2 * n))
                    act.wait_ge(*s.before(f"mixed{n}"))
                    act.activation(sg[:, n, 0:width], bank[2 * n][:, 0:width], ACT.Sigmoid,
                                   bias=bias(n)).then_inc(*s.tick(f"gate{n}"))

            def merge1(s):
                merge(s, 4, S, lambda n: par("b_gate", s.turn + n * KC))

            def norm_ffn1(s):
                for c in range(KC):
                    act.activation(SQ[:, c, XS], X[:, c, XS], ACT.Square).then_inc(*s.tick("squared"))
                act.wait_ge(*s.done("variance"))
                rsqrt(s, work(0, S), bank[0][:, 0:S], work(512, S))

            def up1(s):
                for j in range(2):
                    act.wait_ge(*s.done(f"gate_conv{j}"))
                    act.activation(up_s[:, j, 0:S], up_c[:, j, 0:S], ACT.Sigmoid).then_inc(*s.tick(f"gate_sig{j}"))

            def up2(s):
                n = T2 - first_column(s.layer)
                for j in range(2):
                    act.wait_ge(*s.done("unit", 2 * j))
                    act.wait_ge(*s.before(f"hidden{j}"))
                    act.activation(up_s[:, j, 0:n], bank[2 * j][:, 0:n], ACT.Sigmoid).then_inc(*s.tick(f"gate_sig{j}"))

            def cond(s):
                c = PR[:, PCOL["cond"]:PCOL["cond"] + 2 * KC]
                act.activation(COND[:, :, :].rearrange("p c m -> p (c m)"), c, ACT.Sigmoid).then_inc(*s.tick("cond_sig"))

            def ada(s):
                for j in range(2):
                    act.wait_ge(*s.done("unit", 4 * j + 3))
                    act.activation(ada_rows[:, bass.ds((s.turn * 2 + j) * 512, 512)], bank[j][0:2, :], ACT.Copy)\
                       .then_inc(*s.tick(f"row{j}"))

            def layernorm(s, dest, scale, shift):
                c0 = norm_column(s.plan[s.number][0], s.layer)
                n = T2 - c0
                conv = s.plan[s.number][0] == "conv_norm"
                cen = Y2[2] if conv else H
                for c in range(KC):
                    act.wait_ge(*s.done("centred", c))
                    act.activation(SQ[:, c, c0:T2], cen[:, c, c0:T2], ACT.Square).then_inc(*s.tick("squared"))
                act.wait_ge(*s.done("variance"))
                rsqrt(s, work(0, n), bank[1][:, 0:n], work(512, n))
                if conv:
                    tables(ACT_SET_SIGMOID)
                for c in range(KC):
                    act.wait_ge(*s.done("scaled", c))
                    for part in ([0, 1] if c0 == 0 else [1]):
                        cs = slice(part * S, (part + 1) * S)
                        act.activation(dest[:, c, cs], cen[:, c, cs], ACT.Identity, scale=scale(c, part),
                                       bias=shift(c, part)).then_inc(*s.tick("affine"))
                    if conv:
                        act.wait_ge(*s.so_far("affine"))
                        act.activation(SQ[:, c, c0:T2], cen[:, c, c0:T2], ACT.Sigmoid).then_inc(*s.tick("conv_sig"))
                        act.wait_ge(*s.done("unit", c))
                        act.activation(sg_conv[:, c, 0:n], bank[2 + c % 6][:, 0:n], ACT.Sigmoid)\
                           .then_inc(*s.tick("gate_conv"))

            def ln_mixer(s):
                layernorm(s, H, lambda c, part: MOD[:, 8 + c, 1 - part:2 - part],
                          lambda c, part: MOD[:, c, 1 - part:2 - part])

            def ln_ffn(s):
                layernorm(s, H, lambda c, part: MOD[:, 32 + c, 1 - part:2 - part],
                          lambda c, part: MOD[:, 24 + c, 1 - part:2 - part])

            def post_mixer(s):
                layernorm(s, X, lambda c, part: par(f"ln1_g{s.layer}", c), lambda c, part: par(f"ln1_b{s.layer}", c))

            def post_ffn(s):
                layernorm(s, X, lambda c, part: par(f"ln2_g{s.layer}", c), lambda c, part: par(f"ln2_b{s.layer}", c))

            def conv_norm(s):
                layernorm(s, Y2[2], lambda c, part: par(f"conv_g{s.layer}", c),
                          lambda c, part: par(f"conv_be{s.layer}", c))

            def attend(s):
                heads, units = attend_projections(s), attend_units(s.layer)
                normed = [f for f, head in enumerate(heads) if head != "v"]
                for stage, i, part, parts in attend_order(s):
                    if stage == "project" and part == parts - 1:
                        act.wait_ge(*s.done("unit", i))
                        if heads[i] == "v":
                            act.activation(att_vs[s.next % 2], attend_bank(s, i)[:, :].rearrange("p (t e) -> p t e", t=4),
                                           ACT.Copy).then_inc(*s.tick("v_taken"))
                        else:
                            n = T2 if heads[i] == "k" else T2 - first_column(s.layer)
                            act.wait_ge(*s.before("variance", normed.index(i)))
                            act.activation(sq2[:, 0, 0:n], attend_bank(s, i)[:, 0:n], ACT.Square)\
                               .then_inc(*s.tick("head_squared"))
                    elif stage == "variance":
                        n = T2 if heads[i] == "k" else T2 - first_column(s.layer)
                        act.wait_ge(*s.done("variance", normed.index(i)))
                        act.wait_ge(*s.before("head_taken", normed.index(i)))
                        rsqrt(s, rstd[:, 0, 0:n], bank[2][:, 0:n], rstd[:, 1, 0:n],
                              1.0 if heads[i] == "k" else P ** -0.5, "head_rstd")
                    elif stage == "gates" and part == parts - 1:
                        act.wait_ge(*s.done("glr"))
                        act.activation(glr[0:48, :], bank[0][0:48, :], ACT.Copy)
                    elif stage == "logits":
                        soft_exp(act, s, i, bank[4 + i % 2], LAT_SEGS if units[i][1] == "x" else MEM_SEGS)
                    elif stage == "transpose":
                        soft_take(act, s, i, bank[6], T2)

            def gla(s):
                i = s.turn
                c0 = first_column(s.layer)
                n = T2 - c0
                act.wait_ge(*s.done("unit", 0))
                act.wait_ge(*s.before("gla_end"))
                for d in range(2):
                    y = dist[:, d, :]
                    act.activation(y, bank[4 + d][:, :], ACT.Identity, bias=par(f"gla_ba{s.layer}", i + 4 * d))\
                       .then_inc(*s.tick("act"))
                for func, scale, bias in ((ACT.Abs, 1.0, 0.0), (ACT.Exp, -1.0, 0.0), (ACT.Ln, 1.0, 1.0)):
                    fence(s)
                    for d in range(2):
                        e = (gtmp, gtmp2)[d]
                        act.activation(e, dist[:, d, :] if func == ACT.Abs else e, func, scale=scale, bias=bias)\
                           .then_inc(*s.tick("gate_ln" if func == ACT.Ln else "act"))
                act.wait_ge(*s.done("unit", 2))
                act.activation(gq[:, c0:T2], bank[0][:, 0:n], ACT.Copy, scale=P ** -0.5).then_inc(*s.tick("q_taken"))

                def level(lv):
                    m = LEVELS[lv]
                    act.wait_ge(*s.done("dist", lv))
                    f, b = (halves(dist[:, d, c0:T2], m) for d in range(2))
                    oq, ok = halves(eq[:, c0:T2], m), halves(ek[:, c0:T2], m)
                    if lv:
                        act.wait_ge(*s.done("level", lv - 1))
                    act.activation(oq[:, :, 0, :], b[:, :, 0, :], ACT.Exp, scale=1 / GLA_TAU)
                    act.activation(oq[:, :, 1, :], f[:, :, 1, :], ACT.Exp, scale=1 / GLA_TAU)
                    act.activation(ok[:, :, 0, :], f[:, :, 0, :], ACT.Exp, scale=-1 / GLA_TAU)
                    act.activation(ok[:, :, 1, :], b[:, :, 1, :], ACT.Exp, scale=-1 / GLA_TAU)\
                       .then_inc(*s.tick("level_exp"))

                level(0)
                act.wait_ge(*s.done("end_dist"))
                act.activation(kw[:, :, :], kw[:, :, :], ACT.Exp, scale=1 / GLA_TAU).then_inc(*s.tick("kw_exp"))
                level(1)
                for d in range(2):
                    act.activation(qdecay[:, d, c0:T2], cum[:, d, c0:T2], ACT.Exp, scale=1 / GLA_TAU)\
                       .then_inc(*s.tick("qdecay_exp"))
                for d, at in enumerate((P - 1, 0)):
                    e = act.activation(decay[:, d, :], cum[:, d, :].rearrange("p (c t) -> p c t", c=4)[:, :, at],
                                       ACT.Exp, scale=1 / GLA_TAU)
                e.then_inc(*s.tick("decay_exp"))
                for lv in (2, 3, 4):
                    level(lv)
                act.wait_ge(*s.done("unit", 3))
                for t in range(2):
                    v = act.activation(gv[:, 2 * t:2 * t + 2, :], bank[2 + t][:, :].rearrange("p (t e) -> p t e", t=2),
                                       ACT.Copy)
                v.then_inc(*s.tick("v_taken"))
                act.wait_ge(*s.done("kw_transposed"))
                for d, order in enumerate((orderf, orderb)):
                    for c in order[:3]:
                        e = act.activation(kwt[:, d, c, :], bank[4 + d][:, c * P:(c + 1) * P], ACT.Copy)
                e.then_inc(*s.tick("kw_taken"))
                level(5)
                level(6)
                for u in range(2):
                    act.wait_ge(*s.done("unit", 5 + u))
                    act.activation(gr[:, u, 0:n], bank[6 + u][:, 0:n], ACT.Exp, scale=-1.0).then_inc(*s.tick("r_exp"))
                act.wait_ge(*s.done("gla_out"))
                for e in range(2):
                    act.activation(dist[:, e, 0:n], bank[6 + e][:, 0:n], ACT.Square).then_inc(*s.tick("gla_squared"))
                act.wait_ge(*s.done("variance"))
                rsqrt(s, eq[:, 0:n], bank[0][:, 0:n], ek[:, 0:n], 1.0, "gla_rstd")

            def conv(s):
                n = T2 - first_column(s.layer)
                act.wait_ge(*s.done("unit", 1))
                act.wait_ge(*s.before("glu"))
                act.activation(conv_sg[:, 0:n], bank[1][:, 0:n], ACT.Sigmoid).then_inc(*s.tick("glu_sig"))
                for b in range(2):
                    act.wait_ge(*s.done("unit", 2 + 2 * b))
                    act.wait_ge(*s.before(f"mixed{b}"))
                    act.activation(sg2[:, b, 0:n], bank[2 + 2 * b][:, 0:n], ACT.Sigmoid).then_inc(*s.tick(f"gate{b}"))

            bodies = {"prepare": prepare, "forget": forget, "fox": fox, "lru_in": lru_in, "lru_mix": lru_mix,
                      "stick": stick, "memory": memory, "merge1": merge1, "norm_ffn1": norm_ffn1, "up1": up1,
                      "cond": cond, "ada": ada, "ln_mixer": ln_mixer, "attend": attend, "gla": gla,
                      "conv": conv, "conv_norm": conv_norm, "post_mixer": post_mixer, "ln_ffn": ln_ffn,
                      "up2": up2, "post_ffn": post_ffn}
            sets = {"prepare": ACT_SET_LN_EXP, "cond": ACT_SET_SIGMOID, "merge1": ACT_SET_SIGMOID,
                    "norm_ffn1": ACT_SET_LN_EXP, "up1": ACT_SET_SIGMOID, "ln_mixer": ACT_SET_LN_EXP,
                    "conv": ACT_SET_SIGMOID, "conv_norm": ACT_SET_LN_EXP, "post_mixer": ACT_SET_LN_EXP,
                    "up2": ACT_SET_SIGMOID, "post_ffn": ACT_SET_LN_EXP}
            run(act, bodies, lambda kind: tables(sets[kind]) if kind in sets else None)

        @block.vector
        def _(dve):
            def link(s, instruction):
                instruction.then_inc(*s.tick("dve"))
                dve.wait_ge(*s.so_far("dve"))

            def rms_apply(s, dest, src, gain, r):
                for c in range(KC):
                    dve.scalar_tensor_tensor(dest[:, c, :], src[:, c, :], par(gain, c), r, ALU.mult, ALU.mult)

            def prepare(s):
                dve.memset(tile_sum[:, :], 0.0)
                dve.wait_ge(tally.sem("inputs"), 64)
                for c in range(KC):
                    dve.tensor_tensor(SQ[:, c, CTX], MX[:, c, CTX], MX[:, c, CTX], ALU.mult)
                    dve.tensor_tensor(SQ[:, c, XS], X[:, c, XS], X[:, c, XS], ALU.mult).then_inc(*s.tick("squared"))
                dve.wait_ge(*s.done("rstd"))
                rms_apply(s, H[:, :, XS], X[:, :, XS], "attn_g", work(1024, T2)[:, XS])

            def forget(s):
                rms_apply(s, H[:, :, CTX], MX[:, :, CTX], "mem_g", work(1024, T2)[:, CTX])
                y, e = small_f[0:48, 0, :], small_f[0:48, 1, :]
                dve.wait_ge(*s.done("forget_ln"))
                link(s, dve.scalar_tensor_tensor(e, y, 0.0, e, ALU.min, ALU.subtract))
                link(s, dve.memset(y, 1.0))
                dve.tensor_tensor_scan(forget_f[0:48, :], y, e, 0.0, ALU.mult, ALU.add)
                dve.wait_ge(*s.done("lam_exp"))
                e, t, w, q = (small[:, j * KC:(j + 1) * KC] for j in range(4))
                link(s, dve.tensor_scalar(t, e, 2.0, None, ALU.add))
                link(s, dve.reciprocal(t, t))
                link(s, dve.tensor_tensor(t, t, e, ALU.mult))
                link(s, dve.tensor_tensor(w, t, t, ALU.mult))
                link(s, dve.tensor_scalar(q, w, 2.0 / 19, 2.0 / 17, ALU.mult, ALU.add))
                for n in range(15, 0, -2):
                    link(s, dve.tensor_tensor(q, q, w, ALU.mult))
                    link(s, dve.tensor_scalar(q, q, 2.0 / n, None, ALU.add))
                link(s, dve.tensor_tensor(q, q, t, ALU.mult))
                lam = PR[:, PCOL["lru_lam"]:PCOL["lru_lam"] + KC]
                link(s, dve.tensor_scalar(t, lam, -1.0, 0.0, ALU.mult, ALU.max))
                link(s, dve.tensor_tensor(q, q, t, ALU.add))
                dve.tensor_scalar(lru_c[:, :], q, -8.0, None, ALU.mult)

            def take_pair(s, k, y):
                dve.wait_ge(*s.done(f"pv{k}"))
                r = slice(64 * k, 64 * k + 64)
                dve.tensor_copy(y[r, s.now, :], bank[7][r, 0:S]).then_inc(*s.tick(f"taken_out{k}"))

            def fox(s):
                if s.attends:
                    soft_max(dve, s, 0, bank[4], FOX_SEGS)
                    soft_max(dve, s, 1, bank[5], FOX_SEGS)
                    soft_norm(dve, s, 0, FOX_SEGS)
                    soft_norm(dve, s, 1, FOX_SEGS)
                if s.projects:
                    if s.attends:
                        dve.wait_ge(*s.done("logits", 1))
                    for k in range(2):
                        h = s.next * 2 + k
                        for dest, pick, add in ((forget_l, "head_l", "add_l"), (forget_r, "head_r", "add_r")):
                            dve.tensor_scalar(dest[0:48, k, :], forget_f[0:48, :], CN[0:48, bass.ds(h + CCOL[pick], 1)],
                                              const(add, 1, 48), ALU.mult, ALU.add)
                    dve.wait_ge(*s.done("rstd"))
                    dve.scalar_tensor_tensor(qn[:, 0:S], bank[0][:, 0:S], par("fox_qg"), rstd[:, 0, 0:S],
                                             ALU.mult, ALU.mult).then_inc(*s.tick("q_taken"))
                    for k in range(2):
                        o = dve.scalar_tensor_tensor(kn2[:, k, :], bank[1][:, 0:S], par("fox_kg", k), rstd[:, 0, S:T2],
                                                     ALU.mult, ALU.mult)
                    o.then_inc(*s.tick("k_taken"))
                if s.attends:
                    take_pair(s, 0, Y1[0])
                    take_pair(s, 1, Y1[0])

            def lru_in(s):
                i = s.turn
                xc = lru_x[:, bass.ds(i * S, S)]
                dve.wait_ge(*s.done("unit", 0))
                link(s, dve.tensor_scalar(xc, bank[0][:, 0:S], par("lru_w", i + 3 * KC), par("lru_b", i),
                                          ALU.mult, ALU.add))
                for tap in (2, 1, 0):
                    sh = 3 - tap
                    part = lru_x[:, bass.ds(i * S + sh, S - sh)]
                    o = dve.scalar_tensor_tensor(part, bank[0][:, 0:S - sh], par("lru_w", i + tap * KC), part,
                                                 ALU.mult, ALU.add)
                    if tap:
                        link(s, o)
                o.then_inc(*s.tick("conv_done"))

            def lru_mix(s):
                t1, t2 = work(0, KC * S), work(KC * S, KC * S)
                v = lambda ap: ap.rearrange("p (c t) -> p c t", c=KC)
                dve.tensor_tensor(v(lru_r), v(lru_r), wide(lru_c[:, :].rearrange("p (c o) -> p c o", o=1), S), ALU.mult)\
                   .then_inc(*s.tick("log_a"))
                link(s, dve.tensor_tensor(t2, lru_g, lru_g, ALU.mult))
                link(s, dve.tensor_scalar(t2, t2, 0.044715, 1.0, ALU.mult, ALU.add))
                dve.tensor_tensor(t2, t2, lru_g, ALU.mult).then_inc(*s.tick("gelu_in"))
                link(s, dve.tensor_tensor(lru_i, lru_i, lru_x, ALU.mult))
                dve.wait_ge(*s.done("tanh_a"))
                t3 = work(2 * KC * S, KC * S)
                link(s, dve.tensor_scalar(t3, t1, -1.0, 1.0, ALU.mult, ALU.add))
                link(s, dve.reciprocal(t3, t3))
                link(s, dve.scalar_tensor_tensor(t1, t1, -2.0, t3, ALU.mult, ALU.mult))
                dve.tensor_scalar(t1, t1, 1e-18, None, ALU.max).then_inc(*s.tick("one_minus_a2"))
                dve.wait_ge(*s.done("gelu_tanh"))
                link(s, dve.scalar_tensor_tensor(lru_g, t2, 1.0, lru_g, ALU.add, ALU.mult))
                dve.wait_ge(*s.done("root"))
                dve.wait_ge(*s.done("a"))
                link(s, dve.tensor_tensor(lru_i, lru_i, t1, ALU.mult))
                y = YG[:, KC * S:2 * KC * S]
                for c in range(KC):
                    cs = slice(c * S, (c + 1) * S)
                    o = dve.tensor_tensor_scan(y[:, cs], lru_r[:, cs], lru_i[:, cs], 0.0, ALU.mult, ALU.add)
                link(s, o)
                dve.scalar_tensor_tensor(y, y, 0.5, lru_g, ALU.mult, ALU.mult)

            def stick(s):
                if s.attends:
                    for k in range(2):
                        z, e = rstd[:, k, 0:3 * P], sq2[:, k, 0:3 * P]
                        dve.wait_ge(*s.done("log1p", k))
                        link(s, dve.scalar_tensor_tensor(e, z, 0.0, e, ALU.max, ALU.add))
                        dve.tensor_tensor(e, e, const("strict", 3 * P), ALU.mult).then_inc(*s.tick("softplus"))
                for k in range(2):
                    if s.attends:
                        b = bank[3 if k == 0 else 6]
                        dve.wait_ge(*s.done("suffix", k))
                        dve.wait_ge(*s.before(f"pv{k}"))
                        dve.tensor_tensor(probs[:, k, 0:3 * P], rstd[:, k, 0:3 * P], b[:, 0:3 * P], ALU.subtract)\
                           .then_inc(*s.tick(f"minus_suffix{k}"))
                    if s.projects and k == 0:
                        dve.wait_ge(*s.done("unit", 1))
                        if s.attends:
                            dve.wait_ge(*s.done("logits", 1))
                        for h in range(2):
                            o = dve.tensor_scalar(kn2[:, h, :], bank[1][:, 0:S], const("head_rows", 1, P, h), None,
                                                  ALU.mult)
                        o.then_inc(*s.tick("k_taken"))
                if s.attends:
                    take_pair(s, 0, Y1[2])
                    take_pair(s, 1, Y1[2])

            def memory(s):
                if s.attends:
                    soft_max(dve, s, 0, bank[4], MEM_SEGS)
                    soft_norm(dve, s, 0, MEM_SEGS)
                    dve.wait_ge(*s.done("pv0"))
                    dve.tensor_copy(Y1[3][:, bass.ds(s.now * 2, 2), :],
                                    bank[7][:, :].rearrange("p (e t) -> p e t", e=2)).then_inc(*s.tick("taken_out0"))
                if s.projects:
                    dve.wait_ge(*s.done("rstd"))
                    for u in range(2):
                        o = dve.scalar_tensor_tensor(kn[:, u * S:(u + 1) * S], bank[0][:, u * S:(u + 1) * S],
                                                     par("mem_kg", u), rstd[:, 0, 0:S], ALU.mult, ALU.mult)
                    o.then_inc(*s.tick("k_taken"))
                    for u in range(2):
                        o = dve.scalar_tensor_tensor(qn[:, u * S:(u + 1) * S], bank[1][:, u * S:(u + 1) * S],
                                                     par("mem_qg", u), rstd[:, 0, S:T2], ALU.mult, ALU.mult)
                    o.then_inc(*s.tick("q_taken"))

            def merge(s, count, cols):
                w = T2 - cols.start
                for n in range(count):
                    dve.wait_ge(*s.done("unit", 2 * n + 1))
                    dve.wait_ge(*s.done(f"gate{n}"))
                    dest = MX[:, s.turn, cols]
                    if n == 0:
                        dve.tensor_tensor(dest, sg[:, n, 0:w], bank[2 * n + 1][:, 0:w], ALU.mult)\
                           .then_inc(*s.tick(f"mixed{n}"))
                    else:
                        link(s, dve.tensor_tensor(sg[:, n, 0:w], sg[:, n, 0:w], bank[2 * n + 1][:, 0:w], ALU.mult))
                        dve.tensor_tensor(dest, dest, sg[:, n, 0:w], ALU.add).then_inc(*s.tick(f"mixed{n}"))
                    dve.wait_ge(*s.done(f"mixed{n}"))

            def merge1(s):
                merge(s, 4, XS)

            def merge2(s):
                c0 = first_column(s.layer)
                for j in range(2):
                    dve.wait_ge(*s.done("unit", j))
                    tile = s.turn * 2 + j
                    g = sg_conv[:, tile, 0:T2 - c0]
                    link(s, dve.tensor_tensor(g, g, bank[j][:, 0:T2 - c0], ALU.mult))
                    dve.tensor_tensor(MX[:, tile, c0:T2], MX[:, tile, c0:T2], g, ALU.add)\
                       .then_inc(*s.tick(f"mixed{j}"))

            def out1(s):
                for u in range(4):
                    dve.wait_ge(*s.done("unit", u))
                    t = X[:, s.turn * 4 + u, XS]
                    dve.tensor_tensor(t, t, bank[u][:, 0:S], ALU.add).then_inc(*s.tick(f"added{u}"))

            def down1(s):
                for j in range(2):
                    dve.wait_ge(*s.done("unit", 3 * j + 2))
                    t = X[:, s.turn * 2 + j, XS]
                    dve.tensor_tensor(t, t, bank[j][:, 0:S], ALU.add).then_inc(*s.tick(f"added{j}"))

            def gated_add(s, u, tile, b, gate):
                c0 = first_column(s.layer)
                for part in ([0, 1] if c0 == 0 else [1]):
                    o = dve.tensor_scalar(up_s[:, 0, part * S:(part + 1) * S], b[:, part * S - c0:(part + 1) * S - c0],
                                          MOD[:, bass.ds(tile + gate, 1), 1 - part:2 - part].rearrange("p a b -> p (a b)"),
                                          None, ALU.mult)
                link(s, o)
                t = X[:, tile, c0:T2]
                dve.scalar_tensor_tensor(t, t, ALPHA, up_s[:, 0, c0:T2], ALU.mult, ALU.add)\
                   .then_inc(*s.tick(f"added{u}"))
                dve.wait_ge(*s.done(f"added{u}"))
                link(s, dve.tensor_tensor(tile_sum[:, c0:T2], tile_sum[:, c0:T2], t, ALU.add))

            def out2(s):
                for u in range(4):
                    dve.wait_ge(*s.done("unit", u))
                    gated_add(s, u, s.turn * 4 + u, bank[u], 16)

            def down2(s):
                for j in range(2):
                    dve.wait_ge(*s.done("unit", 3 * j + 2))
                    gated_add(s, j, s.turn * 2 + j, bank[j], 40)

            def norm_ffn1(s):
                dve.wait_ge(*s.done("rstd"))
                for c in range(KC):
                    dve.scalar_tensor_tensor(H[:, c, XS], X[:, c, XS], par("ffn_g", c), work(0, S), ALU.mult, ALU.mult)\
                       .then_inc(*s.tick("ffn_normed"))

            def up1(s):
                for j in range(2):
                    f = s.turn * 2 + j
                    g = bank[2 * j]
                    c = up_c[:, j, :]
                    dve.wait_ge(*s.done("unit", 2 * j))
                    link(s, dve.tensor_scalar(c[:, 0:S], g[:, 0:S], par("ffn_w", f + 2 * FT), par("ffn_b", f),
                                              ALU.mult, ALU.add))
                    link(s, dve.scalar_tensor_tensor(c[:, 1:S], g[:, 0:S - 1], par("ffn_w", f + FT), c[:, 1:S],
                                                     ALU.mult, ALU.add))
                    dve.scalar_tensor_tensor(c[:, 2:S], g[:, 0:S - 2], par("ffn_w", f), c[:, 2:S],
                                             ALU.mult, ALU.add).then_inc(*s.tick(f"gate_conv{j}"))
                    dve.wait_ge(*s.done(f"gate_sig{j}"))
                    link(s, dve.tensor_tensor(c[:, 0:S], c[:, 0:S], up_s[:, j, 0:S], ALU.mult))
                    dve.wait_ge(*s.done("unit", 2 * j + 1))
                    dve.tensor_tensor(G[:, f, 0:S], c[:, 0:S], bank[2 * j + 1][:, 0:S], ALU.mult)\
                       .then_inc(*s.tick(f"hidden{j}"))

            def up2(s):
                c0 = first_column(s.layer)
                n = T2 - c0
                for j in range(2):
                    f = s.turn * 2 + j
                    dve.wait_ge(*s.done(f"gate_sig{j}"))
                    link(s, dve.tensor_tensor(up_c[:, j, 0:n], up_s[:, j, 0:n], bank[2 * j][:, 0:n], ALU.mult))
                    dve.wait_ge(*s.done("unit", 2 * j + 1))
                    dve.tensor_tensor(G[:, f, c0:T2], up_c[:, j, 0:n], bank[2 * j + 1][:, 0:n], ALU.mult)\
                       .then_inc(*s.tick(f"hidden{j}"))

            def cond(s):
                c = PR[:, PCOL["cond"]:PCOL["cond"] + 2 * KC]
                o = COND[:, :, :].rearrange("p c m -> p (c m)")
                dve.wait_ge(*s.done("cond_sig"))
                dve.tensor_tensor(o, o, c, ALU.mult)

            def modulation(s):
                b = PR[:, PCOL[f"b_ada{s.layer}"]:PCOL[f"b_ada{s.layer}"] + 48].rearrange("p (c o) -> p c o", o=1)
                dve.wait_ge(*s.done("mod_columns"))
                link(s, dve.tensor_tensor(MOD[:, :, :], bank[0][:, 0:96].rearrange("p (c o) -> p c o", o=2),
                                          wide(b, 2), ALU.add))
                for at in (8, 32):
                    dve.tensor_scalar(MOD[:, at:at + 8, :], MOD[:, at:at + 8, :], 1.0, None, ALU.add)

            def layernorm(s):
                c0 = norm_column(s.plan[s.number][0], s.layer)
                n = T2 - c0
                kind = s.plan[s.number][0]
                src, cen = (Y2[2], Y2[2]) if kind == "conv_norm" else (X, H)
                dve.wait_ge(*s.done("mean"))
                for c in range(KC):
                    dve.tensor_tensor(cen[:, c, c0:T2], src[:, c, c0:T2], bank[0][:, 0:n], ALU.subtract)\
                       .then_inc(*s.tick("centred"))
                if kind in ("conv_norm", "post_mixer", "post_ffn"):
                    dve.memset(tile_sum[:, :], 0.0)
                dve.wait_ge(*s.done("rstd"))
                for c in range(KC):
                    dve.wait_ge(*s.done("squared", c))
                    dve.tensor_tensor(cen[:, c, c0:T2], cen[:, c, c0:T2], work(0, n), ALU.mult)\
                       .then_inc(*s.tick("scaled"))
                if kind == "conv_norm":
                    for c in range(KC):
                        dve.wait_ge(*s.done("conv_sig", c))
                        dve.tensor_tensor(cen[:, c, c0:T2], cen[:, c, c0:T2], SQ[:, c, c0:T2], ALU.mult)

            def attend(s):
                c0 = first_column(s.layer)
                cos, sin = const("cos", S), const("sin", S)
                heads, units = attend_projections(s), attend_units(s.layer)
                normed = [f for f, head in enumerate(heads) if head != "v"]
                for stage, i, part, parts in attend_order(s):
                    if stage in ("variance", "rotate"):
                        n = T2 if heads[i] == "k" else T2 - c0
                        dest = att_ks[s.next % 2] if heads[i] == "k" else att_q[:, heads[i], c0:T2]
                    if stage == "variance":
                        gain = par(f"kg{s.layer}" if heads[i] == "k" else f"qg{s.layer}")
                        if s.attends and heads[i] in (0, 1):
                            dve.wait_ge(*s.done("logits", (heads[i] + 1) * len(units) // 4 - 1))
                        dve.wait_ge(*s.done("head_rstd", normed.index(i)))
                        dve.scalar_tensor_tensor(att_n[:, 0:n], attend_bank(s, i)[:, 0:n], gain, rstd[:, 0, 0:n],
                                                 ALU.mult, ALU.mult).then_inc(*s.tick("head_taken"))
                        dve.wait_ge(*s.so_far("head_taken"))
                        if n == T2:
                            dve.tensor_copy(dest[:, 0:S], att_n[:, 0:S])
                        link(s, dve.tensor_tensor(dest[:, n - S:n], att_n[:, n - S:n], cos, ALU.mult))
                    elif stage == "rotate":
                        dve.wait_ge(*s.done("swapped", normed.index(i)))
                        link(s, dve.tensor_tensor(att_t, sin, bank[3][:, 0:S], ALU.mult))
                        dve.tensor_tensor(dest[:, n - S:n], dest[:, n - S:n], att_t, ALU.add)\
                           .then_inc(*s.tick("rotated"))
                        dve.wait_ge(*s.so_far("rotated"))
                    elif stage == "logits":
                        soft_max(dve, s, i, bank[4 + i % 2], LAT_SEGS if units[i][1] == "x" else MEM_SEGS)
                    elif stage == "norm":
                        soft_norm(dve, s, i, LAT_SEGS if units[i][1] == "x" else MEM_SEGS)
                    elif stage == "values":
                        g, kind, q = units[i]
                        w = P if kind == "x" else S
                        at = S + q * P if kind == "x" else 0
                        dve.wait_ge(*s.done(f"pv{i % 2}", i // 2))
                        dve.tensor_copy(Y2[0][:, s.now * 4 + g, at:at + w], bank[7][:, 0:w])\
                           .then_inc(*s.tick("taken_out"))

            def gla(s):
                c0 = first_column(s.layer)
                n = T2 - c0
                first = c0 // P
                for d in range(2):
                    y, e = dist[:, d, :], (gtmp, gtmp2)[d]
                    dve.wait_ge(*s.done("gate_ln", d))
                    dve.scalar_tensor_tensor(e, y, 0.0, e, ALU.min, ALU.subtract).then_inc(*s.tick("dve"))
                dve.wait_ge(*s.so_far("dve"))
                dve.tensor_tensor_scan(cum[:, 0, :], const("run_f", T2), gtmp, 0.0, ALU.mult, ALU.add)
                dve.tensor_tensor_scan(cum[:, 1, ::-1], const("run_b", T2)[:, ::-1], gtmp2[:, ::-1], 0.0,
                                       ALU.mult, ALU.add).then_inc(*s.tick("cum"))
                dve.wait_ge(*s.so_far("cum"))

                def distances(lv):
                    m = LEVELS[lv]
                    if lv:
                        dve.wait_ge(*s.done("level_exp", lv - 1))
                    for d, at in enumerate((m - 1, m)):
                        v = cum[:, d, c0:T2].rearrange("p (n w) -> p n w", w=2 * m)
                        o = dve.tensor_tensor(dist[:, d, c0:T2].rearrange("p (n w) -> p n w", w=2 * m), v,
                                              wide(v[:, :, at:at + 1], 2 * m), ALU.subtract)
                    o.then_inc(*s.tick("dist"))

                distances(0)
                dve.wait_ge(*s.done("unit", 1))
                dve.tensor_copy(gk, bank[1][:, :]).then_inc(*s.tick("k_taken"))
                for d, at in enumerate((P - 1, 0)):
                    v = cum[:, d, :].rearrange("p (c t) -> p c t", c=4)
                    o = dve.tensor_tensor(kw[:, d, :].rearrange("p (c t) -> p c t", c=4),
                                          wide(v[:, :, at:at + 1], P), v, ALU.subtract)
                o.then_inc(*s.tick("end_dist"))
                sc = scores[:, first:4, :]

                def scored(lv):
                    b = bank[lv % 2][:, c0:T2].rearrange("p (c t) -> p c t", t=P)
                    dve.wait_ge(*s.done("level_scores", lv))
                    if lv == 0:
                        o = dve.tensor_tensor(sc, const("twice_ident").rearrange("p (o t) -> p o t", o=1)
                                              .broadcast_to([P, 4 - first, P]), b, ALU.mult)
                    else:
                        mask = const("levels", P, P, (lv - 1) * P).rearrange("p (o t) -> p o t", o=1)\
                            .broadcast_to([P, 4 - first, P]).bitcast(U32)
                        dve.wait_ge(*s.so_far("scored"))
                        dve.memset(small[:, 63:64], 0.0)
                        o = dve.copy_predicated(sc, mask, b)
                    o.then_inc(*s.tick("scored"))

                def state(j):
                    for d, order in enumerate((orderf, orderb)):
                        c, nxt = order[j], order[j + 1]
                        dve.wait_ge(*s.done(f"update{d}", j))
                        if j == 0:
                            dve.tensor_copy(states[:, d, nxt, :], bank[4 + d][:, 0:S]).then_inc(*s.tick(f"state{d}"))
                        else:
                            dve.wait_ge(*s.so_far(f"state{d}"))
                            dve.scalar_tensor_tensor(states[:, d, nxt, :], states[:, d, c, :], decay[:, d, c:c + 1],
                                                     bank[4 + d][:, 0:S], ALU.mult, ALU.add)\
                               .then_inc(*s.tick(f"state{d}"))

                dve.wait_ge(*s.done("q_taken"))
                dve.wait_ge(*s.so_far("k_taken"))
                for lv in range(len(LEVELS)):
                    dve.wait_ge(*s.done("level_exp", lv))
                    if lv:
                        dve.wait_ge(*s.done("level_scores", lv))
                    dve.tensor_tensor(mq[:, c0:T2], gq[:, c0:T2], eq[:, c0:T2], ALU.mult)
                    dve.tensor_tensor(mk[:, c0:T2], gk[:, c0:T2], ek[:, c0:T2], ALU.mult).then_inc(*s.tick("level"))
                    if lv + 1 < len(LEVELS):
                        distances(lv + 1)
                    scored(lv)
                    if lv == 1:
                        dve.wait_ge(*s.done("kw_exp"))
                        for d in range(2):
                            o = dve.tensor_tensor(kw[:, d, :], kw[:, d, :], gk, ALU.mult)
                        o.then_inc(*s.tick("decayed"))
                    if lv == 2:
                        for d in range(2):
                            dve.wait_ge(*s.done("qdecay_exp", d))
                            dve.tensor_tensor(qdecay[:, d, c0:T2], qdecay[:, d, c0:T2], gq[:, c0:T2], ALU.mult)
                        dve.wait_ge(*s.done("decay_exp"))
                scored(len(LEVELS))

                def silu(u):
                    g = gr[:, u, 0:n]
                    dve.wait_ge(*s.done("r_exp", u))
                    link(s, dve.tensor_scalar(g, g, 1.0, None, ALU.add))
                    link(s, dve.reciprocal(g, g))
                    dve.tensor_tensor(g, g, bank[6 + u][:, 0:n], ALU.mult).then_inc(*s.tick("r_taken"))

                state(0)
                silu(0)
                state(1)
                state(2)
                silu(1)
                dve.wait_ge(*s.done("gla_rstd"))
                for e in range(2):
                    o = dve.scalar_tensor_tensor(dist[:, e, 0:n], bank[6 + e][:, 0:n], par(f"gla_g{s.layer}", e),
                                                 eq[:, 0:n], ALU.mult, ALU.mult)
                link(s, o)
                o = dve.tensor_tensor(Y2[1][:, bass.ds(s.turn * 2, 2), c0:T2], dist[:, :, 0:n], gr[:, :, 0:n], ALU.mult)
                o.then_inc(*s.tick("gla_end"))

            def conv(s):
                c0 = first_column(s.layer)
                n = T2 - c0
                parts = slice(c0 // S, 2)
                dve.wait_ge(*s.done("glu_sig"))
                for at in (0, PAD + S):
                    link(s, dve.memset(padded[:, :, at:at + PAD], 0.0))
                dve.tensor_tensor(padded[:, parts, PAD:PAD + S], conv_sg[:, 0:n].rearrange("p (a t) -> p a t", t=S),
                                  bank[0][:, 0:n].rearrange("p (a t) -> p a t", t=S), ALU.mult)\
                   .then_inc(*s.tick("glu"))
                dve.wait_ge(*s.done("glu"))
                sums = [Y2[2][:, s.turn, c0:T2].rearrange("p (a t) -> p a t", t=S), work(2560, 2, S)[:, parts, :]]
                for tap in range(CONV):
                    src, w = padded[:, parts, tap:tap + S], par(f"conv_w{s.layer}", s.turn + tap * KC)
                    if tap >= 2:
                        dve.wait_ge(s.so_far("dve")[0], s.so_far("dve")[1] - 1)
                    if tap == 0:
                        o = dve.tensor_scalar(sums[0], src, w, par(f"conv_b{s.layer}", s.turn), ALU.mult, ALU.add)
                    elif tap == 1:
                        o = dve.tensor_scalar(sums[1], src, w, None, ALU.mult)
                    else:
                        o = dve.scalar_tensor_tensor(sums[tap % 2], src, w, sums[tap % 2], ALU.mult, ALU.add)
                    o.then_inc(*s.tick("dve"))
                dve.wait_ge(*s.so_far("dve"))
                link(s, dve.tensor_tensor(sums[0], sums[0], sums[1], ALU.add))
                total = tile_sum[:, c0:T2].rearrange("p (a t) -> p a t", t=S)
                link(s, dve.tensor_tensor(total, total, sums[0], ALU.add))
                for b in range(2):
                    dve.wait_ge(*s.done("unit", 3 + 2 * b))
                    dve.wait_ge(*s.done(f"gate{b}"))
                    dest, gates = MX[:, s.turn, c0:T2], sg2[:, b, 0:n]
                    if b == 0:
                        dve.tensor_tensor(dest, gates, bank[3][:, 0:n], ALU.mult).then_inc(*s.tick("mixed0"))
                        dve.wait_ge(*s.done("mixed0"))
                    else:
                        link(s, dve.tensor_tensor(gates, gates, bank[5][:, 0:n], ALU.mult))
                        dve.tensor_tensor(dest, dest, gates, ALU.add).then_inc(*s.tick("mixed1"))

            run(dve, {"prepare": prepare, "forget": forget, "fox": fox, "lru_in": lru_in, "lru_mix": lru_mix,
                      "stick": stick, "memory": memory, "merge1": merge1, "out1": out1, "norm_ffn1": norm_ffn1,
                      "up1": up1, "down1": down1, "cond": cond, "modulation": modulation, "ln_mixer": layernorm,
                      "attend": attend, "gla": gla, "conv": conv, "conv_norm": layernorm, "merge2": merge2,
                      "out2": out2, "post_mixer": layernorm, "ln_ffn": layernorm, "up2": up2, "down2": down2,
                      "post_ffn": layernorm})

        @block.gpsimd
        def _(pool):
            for name in sorted(tally.primed):
                pool.nop().then_inc(tally.sem(name), 1)
            run(pool, {})

    return tally.seen



def columns(v):
    return np.asarray(v).reshape(-1, P).T


def unit(w, col, width=P):
    rows = w.shape[0]
    out = np.zeros((P, KC, P), np.float32)
    out[:, 0:rows // P, :] = w[:, col:col + P].reshape(rows // P, P, P).transpose(1, 0, 2)
    return out.reshape(P, KC * P)


def weight_stream(a):
    w_in, kv = a["w_in"][0], a["w_mem_kv"][0]
    fq, fk, fv, ff = 0, D, 2 * D, 3 * D
    lx = ff + 16
    lg, sq_, sk, sv = lx + D, lx + 2 * D, lx + 3 * D, lx + 4 * D
    mq, gates = lx + 5 * D, lx + 6 * D
    out = []

    def ada_units(l):
        return list(a["w_ada_2"][l].reshape(4, 2, P, 12, 512).transpose(3, 0, 2, 1, 4).reshape(48, P, 1024))

    for i in range(8):
        out += [unit(w_in, fq + i * P), unit(w_in, fk + i * P), unit(w_in, fv + i * P)]
    for i in range(8):
        diag = np.zeros((P, KC * P), np.float32)
        for j, name in enumerate(("lru_w_a", "lru_w_x")):
            for b in range(2):
                diag[64 * b:64 * b + 64, j * P + 64 * b:j * P + 64 * b + 64] = a[name][0, 2 * i + b]
        out += [unit(w_in, lx + i * P), unit(w_in, lg + i * P), diag]
    out += ada_units(0)
    for i in range(8):
        out += [unit(w_in, sq_ + i * P), unit(w_in, sk + i * P), unit(w_in, sv + i * P)]
    for h in range(4):
        out += [unit(w, c + h * 2 * P + u * P) for w, c in ((kv, 0), (w_in, mq), (kv, D)) for u in range(2)]
    for i in range(8):
        for n in range(4):
            out += [unit(w_in, gates + n * D + i * P), unit(a["w_branch"][0, n], i * P)]
    out += [unit(a["w_out"][0], i * P) for i in range(8)]
    for f in range(FT):
        out += [unit(a["w_up"][0], f * P), unit(a["w_up"][0], D_FF + f * P)]
    for i in range(8):
        out += [unit(a["w_down"][0][q * D:(q + 1) * D], i * P) for q in range(3)]
    for l in range(LAYERS):
        if l:
            out += ada_units(l)
        w = a["w_in_2"][l]
        k, v, kg, vg, glr = 0, 256, 512, 1024, 2048
        q, qg, r = 2080, 2080 + 1024, 2080 + 1536
        glu, gate = r + 1024, r + 1024 + 2048
        for j in range(2):
            out += [unit(w, k + j * P)] + [unit(w, q + (4 * j + g) * P) for g in range(2)]
            out += [unit(w, v + j * P)] + [unit(w, q + (4 * j + g) * P) for g in range(2, 4)]
        for h in range(4):
            a2 = np.zeros((P, KC * P), np.float32)
            for d in range(2):
                a2[32 * d:32 * d + 16, d * P:(d + 1) * P] = a["gla_w_a2_2"][l, d][:, h * P:(h + 1) * P]
            out += [a2, unit(w, kg + h * P), unit(w, qg + h * P), unit(w, vg + 2 * h * P),
                    unit(w, vg + (2 * h + 1) * P), unit(w, r + 2 * h * P), unit(w, r + (2 * h + 1) * P)]
        for i in range(8):
            out += [unit(w, glu + i * P), unit(w, glu + D + i * P)]
            for n, name in enumerate(("w_att_o_2", "w_gla_o_2")):
                out += [unit(w, gate + n * D + i * P), unit(a[name][l], i * P)]
        out += [unit(w, gate + 2 * D + i * P) for i in range(8)]
        out += [unit(a["w_conv_o_2"][l], i * P) for i in range(8)]
        out += [unit(a["w_out_2"][l], i * P) for i in range(8)]
        for f in range(FT):
            out += [unit(a["w_ff_gate_2"][l], f * P), unit(a["w_ff_up_2"][l], f * P)]
        for i in range(8):
            out += [unit(a["w_ff_down_2"][l][q_ * D:(q_ + 1) * D], i * P) for q_ in range(3)]
    return np.stack(out)


def parameters(a):
    p = np.zeros((P, N_PARAMS), np.float32)

    def put(name, block):
        p[0:block.shape[0], PCOL[name]:PCOL[name] + block.shape[1]] = block

    put("attn_g", columns(a["attn_norm_g"]))
    put("mem_g", columns(a["mem_norm_g"]))
    wf = np.zeros((P, KC, 48), np.float32)
    wf[:, :, 0:16] = a["w_in"][0][:, 3 * D:3 * D + 16].reshape(KC, P, 16).transpose(1, 0, 2)
    wf[:, :, 32:48] = wf[:, :, 0:16]
    put("wf", wf.reshape(P, -1))
    bf = np.zeros((48, 1), np.float32)
    bf[0:16, 0] = bf[32:48, 0] = a["b_forget"][0]
    put("bf", bf)
    put("fox_qg", np.tile(a["fox_q_norm_g"][0], 2)[:, None])
    for k in range(2):
        p[64 * k:64 * k + 64, PCOL["fox_kg"] + k] = a["fox_k_norm_g"][0]
    put("lru_w", columns(a["lru_conv_w"][0]))
    for name, key in (("lru_b", "lru_conv_b"), ("lru_ba", "lru_b_a"), ("lru_bx", "lru_b_x"), ("lru_lam", "lru_lambda"),
                      ("mem_qg", "mem_q_norm_g"), ("mem_kg", "mem_k_norm_g"), ("b_gate", "b_gate"),
                      ("ffn_g", "ffn_norm_g"), ("ffn_w", "ffn_conv_w"), ("ffn_b", "ffn_conv_b")):
        put(name, columns(a[key][0]))
    put("cond", np.stack([columns(a["c_2"][0]), columns(a["c_ctx_2"])], axis=2).reshape(P, -1))
    for l in range(LAYERS):
        for name, key in (("b_ada", "b_ada_2"), ("qg", "q_norm_2"), ("kg", "k_norm_2"), ("gla_ba", "gla_b_a_2"),
                          ("gla_g", "gla_norm_2"), ("conv_w", "conv_w_dw_2"), ("conv_b", "conv_b_dw_2"),
                          ("conv_g", "conv_ln_g_2"), ("conv_be", "conv_ln_b_2"), ("ln1_g", "ln1_g_2"),
                          ("ln1_b", "ln1_b_2"), ("ln2_g", "ln2_g_2"), ("ln2_b", "ln2_b_2")):
            put(f"{name}{l}", columns(a[key][l]))
        glr = np.zeros((P, KC, 48), np.float32)
        for d in range(2):
            glr[:, :, 32 * d:32 * d + 16] = a["w_in_2"][l][:, 2048 + 16 * d:2064 + 16 * d]\
                .reshape(KC, P, 16).transpose(1, 0, 2)
        put(f"wglr{l}", glr.reshape(P, -1))
    return p


def constants():
    c = np.zeros((P, N_CONSTS), np.float32)

    def put(name, block, at=0):
        block = np.asarray(block, np.float32)
        c[0:block.shape[0], CCOL[name] + at:CCOL[name] + at + block.shape[1]] = block

    k, q = np.arange(P)[:, None], np.arange(P)[None, :]
    eye = np.eye(P)
    put("ident", eye)
    put("mean1024", np.full((P, P), 1 / 1024))
    put("mean64", (k // 64 == q // 64) / 64)
    put("mean128", np.full((P, P), 1 / 128))
    put("mean256", np.full((P, P), 1 / 256))
    put("ones", np.ones((P, P)))
    put("suffix", k >= q)
    swap = np.zeros((P, P))
    swap[np.arange(1, P, 2), np.arange(0, P, 2)] = -1
    swap[np.arange(0, P, 2), np.arange(1, P, 2)] = 1
    put("swap", swap)
    put("causal_neg", np.where(q > k, NEG, 0.0))
    strict = k < q
    put("strict", np.concatenate([strict, np.ones((P, P)), strict], 1))
    big = np.where(strict, 0.0, -NEG)
    put("strict_big", np.concatenate([big, np.zeros((P, P)), big], 1))
    for n, m in enumerate(LEVELS):
        put("levels", (k // (2 * m) == q // (2 * m)) & (k // m != q // m), n * P)
    put("twice_ident", 2 * eye)
    t = np.arange(S)
    half = P // 2
    inv = np.float32(10000.0) ** (-np.arange(0, half, 2, dtype=np.float32) / np.float32(half))
    ang = np.concatenate([(t // 64).astype(np.float32)[:, None] * inv, (t % 64).astype(np.float32)[:, None] * inv], 1)
    put("cos", np.repeat(np.cos(ang), 2, axis=1).T)
    put("sin", np.repeat(np.sin(ang), 2, axis=1).T)
    cols = np.arange(T2)
    put("run_f", np.tile((cols % P != 0), (P, 1)))
    put("run_b", np.tile((cols % P != P - 1), (P, 1)))
    h = np.arange(16)[None, :]
    rows = np.arange(48)[:, None]
    put("head_l", rows == 32 + h)
    put("head_r", np.where(rows == h, -1.0, 0.0))
    put("add_l", rows < 16)
    put("add_r", rows >= 32)
    put("head_rows", k // 64 == np.arange(2)[None, :])
    return c


def feature_major(v):
    return np.ascontiguousarray(np.asarray(v).T.reshape(KC, P, -1).transpose(1, 0, 2))


def kernel(**inputs):
    import concourse.bacc as bacc
    from concourse.bass_utils import run_bass_kernel_spmd

    a = {k: np.asarray(v) for k, v in inputs.items()}
    arrays = {"params": parameters(a), "consts": constants(), "stream": weight_stream(a),
              "x_in": feature_major(a["x"][0]), "mem_in": feature_major(a["mem"][0]),
              "ctx_in": feature_major(a["ctx_2"][0])}

    def build(counted):
        nc = bacc.Bacc("TRN2", target_bir_lowering=False, num_devices=1)
        ins = {k: nc.dram_tensor(k, v.shape, F32, kind="ExternalInput").ap() for k, v in arrays.items()}
        out = nc.dram_tensor("out", (P, KC, S), F32, kind="ExternalOutput").ap()
        return nc, program(nc, out=out, counted=counted, **ins)

    _, counted = build({})
    _, counted = build(counted)
    nc, _ = build(counted)
    result = run_bass_kernel_spmd(nc, [arrays], core_ids=[0])
    got = result.results[0]["out"]
    return np.ascontiguousarray(got.transpose(1, 0, 2).reshape(D, S).T)[None]
```
